# Optimizing a Trainium2 kernel written in Bass

```python
import jax, jax.numpy as jnp
from jax import lax
import numpy as np
import math

D_MODEL = 1024
BATCH = 1
SEQ = 1024
DEPTH = 1

D_MIX = D_MODEL
D_POOL = D_MIX // 2
POOL_WINDOWS = (2, 4, 8, 16)
N_POOL_GROUPS = len(POOL_WINDOWS)
POOL_GROUP = D_POOL // N_POOL_GROUPS
HEAD_DIM = 64
D_ATTN = D_MIX - D_POOL
N_HEADS = D_ATTN // HEAD_DIM
N_KV_HEADS = 2
GQA_GROUP = N_HEADS // N_KV_HEADS
D_KV = N_KV_HEADS * HEAD_DIM
WINDOW = 128
BLOCK = 128
IN_WIDTHS = (D_POOL, D_POOL, D_ATTN, D_KV, D_KV, D_ATTN)
D_IN = sum(IN_WIDTHS)
EPS = 1e-6
NEG_INF = -1e30


def rmsnorm(x, gain):
    x32 = x.astype(jnp.float32)
    y = x32 * lax.rsqrt(jnp.mean(x32 * x32, axis=-1, keepdims=True) + EPS) * gain.astype(jnp.float32)
    return y.astype(x.dtype)

def alibi_slopes():
    return jnp.exp2(-8.0 * jnp.arange(1, N_HEADS + 1, dtype=jnp.float32) / N_HEADS)

def pool_mixer(u, w_grp, scale):
    B, S, _ = u.shape
    u32 = u.astype(jnp.float32).reshape(B, S, N_POOL_GROUPS, POOL_GROUP)
    csum = jnp.cumsum(u32, axis=1)
    csum = jnp.concatenate([jnp.zeros_like(csum[:, :1]), csum], axis=1)
    pos = jnp.arange(1, S + 1, dtype=jnp.float32)
    means = []
    for g, w in enumerate(POOL_WINDOWS):
        c = csum[:, :, g]
        lo = jnp.concatenate([jnp.zeros_like(c[:, :w - 1]), c[:, :S + 1 - w]], axis=1)
        count = jnp.minimum(pos, float(w))[None, :, None]
        means.append((c[:, 1:] - lo) / count)
    pooled = jnp.stack(means, axis=2) - u32
    mixed = jnp.einsum('bsgc,gcd->bsgd', pooled.astype(u.dtype), w_grp)
    return mixed.reshape(B, S, D_POOL) * scale

def swa_sink_attention(q, k, v, sinks):
    B, S, _ = q.shape
    NB = S // BLOCK
    q = q.reshape(B, NB, BLOCK, N_KV_HEADS, GQA_GROUP, HEAD_DIM)
    k = k.reshape(B, NB, BLOCK, N_KV_HEADS, HEAD_DIM)
    v = v.reshape(B, NB, BLOCK, N_KV_HEADS, HEAD_DIM)

    def with_prev(t):
        prev = jnp.concatenate([jnp.zeros_like(t[:, :1]), t[:, :-1]], axis=1)
        return jnp.concatenate([prev, t], axis=2)

    kb, vb = with_prev(k), with_prev(v)
    scores = jnp.einsum('bnqhgd,bnkhd->bnhgqk', q, kb).astype(jnp.float32) * (HEAD_DIM ** -0.5)
    qi = jnp.arange(BLOCK)[:, None]
    kj = jnp.arange(2 * BLOCK)[None, :]
    dist = qi + BLOCK - kj
    in_win = (dist >= 0) & (dist < WINDOW)
    key_exists = (jnp.arange(NB)[:, None, None] > 0) | (kj >= BLOCK)[None]
    valid = in_win[None] & key_exists
    slopes = alibi_slopes().reshape(N_KV_HEADS, GQA_GROUP)
    bias = -slopes[:, :, None, None] * dist.astype(jnp.float32)
    scores = jnp.where(valid[None, :, None, None], scores + bias, NEG_INF)
    sink = jnp.broadcast_to(sinks.astype(jnp.float32).reshape(N_KV_HEADS, GQA_GROUP, 1, 1),
                            scores.shape[:-1] + (1,))
    probs = jax.nn.softmax(jnp.concatenate([scores, sink], axis=-1), axis=-1)[..., :-1]
    out = jnp.einsum('bnhgqk,bnkhd->bnqhgd', probs.astype(v.dtype), vb)
    return out.reshape(B, S, D_ATTN)

def first_inputs(seed: int = 0) -> dict:
    key = jax.random.key(seed)
    ks = jax.random.split(key, 9)
    x = jax.random.normal(ks[0], (BATCH, SEQ, D_MODEL), jnp.float32)
    w_in = jax.random.normal(ks[1], (DEPTH, D_MODEL, D_IN), jnp.float32) * D_MODEL ** -0.5
    pool_w = jax.random.normal(ks[2], (DEPTH, N_POOL_GROUPS, POOL_GROUP, POOL_GROUP), jnp.float32) * POOL_GROUP ** -0.5
    pool_scale = 1.0 + 0.1 * jax.random.normal(ks[3], (DEPTH, D_POOL), jnp.float32)
    attn_sinks = 0.5 * jax.random.normal(ks[4], (DEPTH, N_HEADS), jnp.float32)
    w_out = jax.random.normal(ks[5], (DEPTH, D_MIX, D_MODEL), jnp.float32) * D_MIX ** -0.5
    norm_pre = 1.0 + 0.1 * jax.random.normal(ks[6], (DEPTH, D_MODEL), jnp.float32)
    norm_post = 1.0 + 0.1 * jax.random.normal(ks[7], (DEPTH, D_MODEL), jnp.float32)
    return {"x": x, "w_in": w_in, "pool_w": pool_w, "pool_scale": pool_scale,
            "attn_sinks": attn_sinks, "w_out": w_out, "norm_pre": norm_pre, "norm_post": norm_post}

def first_block(x, w_in, pool_w, pool_scale, attn_sinks, w_out, norm_pre, norm_post):
    splits = [int(s) for s in np.cumsum(IN_WIDTHS)[:-1]]
    for layer in range(DEPTH):
        h = rmsnorm(x, norm_pre[layer])
        proj = h @ w_in[layer]
        pool_u, pool_gate, q, k, v, attn_gate = jnp.split(proj, splits, axis=-1)
        pool_out = pool_mixer(pool_u, pool_w[layer], pool_scale[layer]) * jax.nn.silu(pool_gate)
        attn_out = swa_sink_attention(q, k, v, attn_sinks[layer]) * jax.nn.silu(attn_gate)
        y = jnp.concatenate([pool_out, attn_out], axis=-1) @ w_out[layer]
        x = x + rmsnorm(y, norm_post[layer])
    return x


ROPE_THETA = 10000.0
RMS_EPS = 1e-6
NEG_INF_2 = -1e30

MLA_HEADS = 8
MLA_Q_RANK = 256
MLA_KV_RANK = 128
MLA_NOPE_DIM = 64
MLA_ROPE_DIM = 32
MLA_V_DIM = 64
MLA_QK_DIM = MLA_NOPE_DIM + MLA_ROPE_DIM
MLA_WIDTH = MLA_HEADS * MLA_V_DIM
Q_BLOCK = 128

DIL_CONFIGS = ((128, 1), (512, 4), (2048, 16))
DIL_GROUPS = len(DIL_CONFIGS)
DIL_HEADS_PER_GROUP = 8
DIL_HEAD_DIM = 64
DIL_HEADS = DIL_GROUPS * DIL_HEADS_PER_GROUP
DIL_QKV_WIDTH = DIL_HEADS * DIL_HEAD_DIM
DIL_WIDTH = DIL_HEADS_PER_GROUP * DIL_HEAD_DIM

IN_SPLITS = (MLA_Q_RANK, MLA_KV_RANK, MLA_ROPE_DIM, MLA_WIDTH,
             DIL_QKV_WIDTH, DIL_QKV_WIDTH, DIL_QKV_WIDTH, DIL_WIDTH,
             D_MODEL, D_MODEL)
IN_WIDTH = sum(IN_SPLITS)


def rmsnorm_2(x, g):
    xf = x.astype(jnp.float32)
    xf = xf * lax.rsqrt(jnp.mean(xf * xf, axis=-1, keepdims=True) + RMS_EPS)
    return xf.astype(x.dtype) * g

def rope(t, positions):
    dim = t.shape[-1]
    inv_freq = ROPE_THETA ** (-jnp.arange(0, dim, 2, dtype=jnp.float32) / dim)
    ang = positions.astype(jnp.float32)[..., None] * inv_freq
    ang = jnp.concatenate([ang, ang], axis=-1)[:, :, None, :]
    cos, sin = jnp.cos(ang).astype(t.dtype), jnp.sin(ang).astype(t.dtype)
    t1, t2 = t[..., : dim // 2], t[..., dim // 2:]
    rot = jnp.concatenate([-t2, t1], axis=-1)
    return t * cos + rot * sin

def mla_attention(c_q, c_kv, k_rope, positions, q_norm_g, kv_norm_g, w_uq, w_ukv):
    B, S, _ = c_q.shape
    q = (rmsnorm_2(c_q, q_norm_g) @ w_uq).reshape(B, S, MLA_HEADS, MLA_QK_DIM)
    q = jnp.concatenate([q[..., :MLA_NOPE_DIM], rope(q[..., MLA_NOPE_DIM:], positions)], axis=-1)
    q = q * (MLA_QK_DIM ** -0.5)
    kv = (rmsnorm_2(c_kv, kv_norm_g) @ w_ukv).reshape(B, S, MLA_HEADS, MLA_NOPE_DIM + MLA_V_DIM)
    k_nope, v = kv[..., :MLA_NOPE_DIM], kv[..., MLA_NOPE_DIM:]
    k_pe = rope(k_rope[:, :, None, :], positions)
    k = jnp.concatenate([k_nope, jnp.broadcast_to(k_pe, (B, S, MLA_HEADS, MLA_ROPE_DIM))], axis=-1)
    n_blk = S // Q_BLOCK
    qb = q.reshape(B, n_blk, Q_BLOCK, MLA_HEADS, MLA_QK_DIM).transpose(1, 0, 2, 3, 4)

    def one_block(q_blk):
        s = jnp.einsum('bqhd,bkhd->bhqk', q_blk, k).astype(jnp.float32)
        p = jax.nn.softmax(s, axis=-1).astype(v.dtype)
        return jnp.einsum('bhqk,bkhd->bqhd', p, v)

    out = lax.map(one_block, qb)
    return out.transpose(1, 0, 2, 3, 4).reshape(B, S, MLA_WIDTH)

def dilated_group(q, k, v, dilation, side):
    B, S, H, D = q.shape
    L = S // dilation
    nb = -(-L // side)
    Lp = nb * side

    def to_sub(t):
        t = t.reshape(B, L, dilation, H, D).transpose(0, 2, 3, 1, 4)
        return jnp.pad(t, ((0, 0), (0, 0), (0, 0), (0, Lp - L), (0, 0)))

    def neighbourhood(t):
        tp = jnp.pad(t, ((0, 0), (0, 0), (0, 0), (side, side), (0, 0)))
        tb = tp.reshape(B, dilation, H, nb + 2, side, D)
        return jnp.concatenate([tb[:, :, :, :-2], tb[:, :, :, 1:-1], tb[:, :, :, 2:]], axis=4)

    qb = to_sub(q).reshape(B, dilation, H, nb, side, D)
    kb = neighbourhood(to_sub(k))
    vb = neighbourhood(to_sub(v))
    a = jnp.arange(side)[:, None]
    c = jnp.arange(3 * side)[None, :]
    key_pos = (jnp.arange(nb)[:, None, None] - 1) * side + c[None]
    valid = (c >= a)[None] & (c <= a + 2 * side)[None] & (key_pos >= 0) & (key_pos < L)
    s = jnp.einsum('brhnqd,brhnkd->brhnqk', qb, kb).astype(jnp.float32) * (D ** -0.5)
    s = jnp.where(valid, s, NEG_INF_2)
    m = jnp.max(s, axis=-1, keepdims=True)
    p = jnp.exp(s - m)
    den = jnp.sum(p, axis=-1)
    o = jnp.einsum('brhnqk,brhnkd->brhnqd', p.astype(v.dtype), vb).astype(jnp.float32) / den[..., None]
    lse = m[..., 0] + jnp.log(den)
    o = o.reshape(B, dilation, H, Lp, D)[:, :, :, :L].transpose(0, 3, 1, 2, 4).reshape(B, S, H, D)
    lse = lse.reshape(B, dilation, H, Lp)[:, :, :, :L].transpose(0, 3, 1, 2).reshape(B, S, H)
    return o, lse

def dilated_mixture(q, k, v, positions):
    B, S, _ = q.shape
    q = rope(q.reshape(B, S, DIL_HEADS, DIL_HEAD_DIM), positions)
    k = rope(k.reshape(B, S, DIL_HEADS, DIL_HEAD_DIM), positions)
    v = v.reshape(B, S, DIL_HEADS, DIL_HEAD_DIM)
    outs, lses = [], []
    for g, (window, dilation) in enumerate(DIL_CONFIGS):
        sl = slice(g * DIL_HEADS_PER_GROUP, (g + 1) * DIL_HEADS_PER_GROUP)
        o, lse = dilated_group(q[:, :, sl], k[:, :, sl], v[:, :, sl], dilation, window // (2 * dilation))
        outs.append(o)
        lses.append(lse)
    outs = jnp.stack(outs, axis=0)
    alpha = jax.nn.softmax(jnp.stack(lses, axis=0), axis=0)
    out = jnp.sum(alpha[..., None] * outs, axis=0)
    return out.reshape(B, S, DIL_WIDTH).astype(q.dtype)

def hybrid_layer(x, positions, attn_norm_g, w_in, b_gate, mla_q_norm_g, mla_kv_norm_g,
                 w_uq, w_ukv, w_o_mla, w_o_dil, w_out):
    h = rmsnorm_2(x, attn_norm_g)
    proj = h @ w_in
    split_points = [int(p) for p in np.cumsum(IN_SPLITS)[:-1]]
    (c_q, c_kv, k_rope, z_mla, q_dil, k_dil, v_dil, z_dil,
     g_mla, g_dil) = jnp.split(proj, split_points, axis=-1)
    a_out = mla_attention(c_q, c_kv, k_rope, positions, mla_q_norm_g, mla_kv_norm_g, w_uq, w_ukv)
    y_mla = (a_out * jax.nn.silu(z_mla)) @ w_o_mla
    d_out = dilated_mixture(q_dil, k_dil, v_dil, positions)
    y_dil = (d_out * jax.nn.silu(z_dil)) @ w_o_dil
    gate_mla = jax.nn.sigmoid(g_mla + b_gate[:D_MODEL])
    gate_dil = jax.nn.sigmoid(g_dil + b_gate[D_MODEL:])
    merged = gate_mla * y_mla + gate_dil * y_dil
    return x + merged @ w_out

def second_inputs(seed: int = 0) -> dict:
    key = jax.random.key(seed)
    ks = jax.random.split(key, 14)
    f32 = jnp.float32

    def normal(k, shape, fan_in):
        return jax.random.normal(k, shape, f32) * fan_in ** -0.5

    def gain(k, shape):
        return 1.0 + 0.02 * jax.random.normal(k, shape, f32)

    x = jax.random.normal(ks[0], (BATCH, SEQ, D_MODEL), f32)
    positions = jnp.broadcast_to(jnp.arange(SEQ, dtype=jnp.int32)[None, :], (BATCH, SEQ))
    return {
        "x": x,
        "positions": positions,
        "attn_norm_g": gain(ks[1], (DEPTH, D_MODEL)),
        "w_in": normal(ks[2], (DEPTH, D_MODEL, IN_WIDTH), D_MODEL),
        "b_gate": 0.02 * jax.random.normal(ks[3], (DEPTH, 2 * D_MODEL), f32),
        "mla_q_norm_g": gain(ks[4], (DEPTH, MLA_Q_RANK)),
        "mla_kv_norm_g": gain(ks[5], (DEPTH, MLA_KV_RANK)),
        "w_uq": normal(ks[6], (DEPTH, MLA_Q_RANK, MLA_HEADS * MLA_QK_DIM), MLA_Q_RANK),
        "w_ukv": normal(ks[7], (DEPTH, MLA_KV_RANK, MLA_HEADS * (MLA_NOPE_DIM + MLA_V_DIM)), MLA_KV_RANK),
        "w_o_mla": normal(ks[8], (DEPTH, MLA_WIDTH, D_MODEL), MLA_WIDTH),
        "w_o_dil": normal(ks[9], (DEPTH, DIL_WIDTH, D_MODEL), DIL_WIDTH),
        "w_out": normal(ks[10], (DEPTH, D_MODEL, D_MODEL), D_MODEL),
        "final_norm_g": gain(ks[11], (D_MODEL,)),
    }

def second_block(x, positions, attn_norm_g, w_in, b_gate, mla_q_norm_g, mla_kv_norm_g,
              w_uq, w_ukv, w_o_mla, w_o_dil, w_out, final_norm_g):
    h = x
    for layer in range(DEPTH):
        h = hybrid_layer(h, positions, attn_norm_g[layer], w_in[layer], b_gate[layer],
                         mla_q_norm_g[layer], mla_kv_norm_g[layer], w_uq[layer], w_ukv[layer],
                         w_o_mla[layer], w_o_dil[layer], w_out[layer])
    return rmsnorm_2(h, final_norm_g)


def setup_inputs(seed=0):
    out = dict(first_inputs(seed))
    for name, value in second_inputs(seed + 1).items():
        if name != "x":
            out[name + "_2"] = value
    return out


def reference(
    x, w_in, pool_w, pool_scale, attn_sinks, w_out, norm_pre, norm_post, positions_2,
    attn_norm_g_2, w_in_2, b_gate_2, mla_q_norm_g_2, mla_kv_norm_g_2, w_uq_2, w_ukv_2,
    w_o_mla_2, w_o_dil_2, w_out_2, final_norm_g_2,
):
    x = first_block(
        x, w_in, pool_w, pool_scale, attn_sinks, w_out, norm_pre, norm_post,
    )
    return second_block(
        x, positions_2, attn_norm_g_2, w_in_2, b_gate_2, mla_q_norm_g_2, mla_kv_norm_g_2,
        w_uq_2, w_ukv_2, w_o_mla_2, w_o_dil_2, w_out_2, final_norm_g_2,
    )


_drawn_inputs = setup_inputs


def setup_inputs(seed=0):
    import zlib

    import numpy as np

    out = dict(_drawn_inputs(seed))
    spreads = {}
    factors = {'attn_sinks': 6.001,
     'attn_norm_g_2': 8.0,
     'b_gate_2': 8.0,
     'mla_q_norm_g_2': 8.0,
     'mla_kv_norm_g_2': 8.0,
     'w_uq_2': 2.814,
     'final_norm_g_2': 2.667}
    for name, (base, spread) in spreads.items():
        noise = np.random.default_rng([zlib.crc32(name.encode()), seed]).standard_normal(out[name].shape)
        drawn = base * np.exp(spread * noise) if base else spread * noise
        out[name] = __import__('jax').numpy.asarray(drawn.astype(out[name].dtype))
    for name, factor in factors.items():
        out[name] = (out[name] * factor).astype(out[name].dtype)
    return out
```

```python
from contextlib import ExitStack

import concourse.bass as bass
import numpy as np
from concourse import mybir

F32 = mybir.dt.float32
F32R = mybir.dt.float32r
I32 = mybir.dt.int32
ALU = mybir.AluOpType
ACT = mybir.ActivationFunctionType
AX_X = mybir.AxisListType.X

P = 128
S = 1024
D = 1024
KT = D // P
TT = S // P
COLS = 512
HALF = S // COLS
EPS = 1e-6
NEG = -1e30
H1 = 8
HD = 64
POOL_W = (2, 4, 8, 16)
PAD = 16
G = 4
HH = H1 // G
MASK_W = 3 * P
FREQS = 32
MLA_R = 32
MLA_QK = 96
C_Q, C_KV = 256, 128
C_W = C_Q + C_KV + MLA_R
DIL_QKV = 1536
DILATIONS = (1, 4, 16)
STAT = 2 * H1
CHUNK_K = 2
STAGE = 2
TWO_PI = 6.283185307179586
TWO_PI_PARTS = (6.28125, 0.0019350051879882812, 3.019915981956752e-07)
PI_IN = 3.1415925
ROUND = 12582912.0


def constants():
    q = np.arange(P)[:, None]
    c = np.arange(2 * P)[None, :]
    dist = (q + P - c).astype(np.float32)
    slopes = np.exp2(-8.0 * np.arange(1, H1 + 1, dtype=np.float32) / H1).astype(np.float32)
    valid = (dist >= 0) & (dist < P)
    swa = np.where(valid[:, None, :], -slopes[None, :, None] * dist[:, None, :], np.float32(NEG))
    j = np.arange(MASK_W)[None, :]
    band = np.where(np.abs(j - P - q) <= HD, 0.0, NEG)
    k = np.arange(P)[None, :]
    pairs = np.where(q % 2 == k % 2, 0.0, NEG)
    n = np.arange(PAD)
    inv = np.stack([1.0 / np.minimum(n + 1, w) for w in POOL_W])
    f32 = 10000.0 ** (-np.arange(0, HD, 2, dtype=np.float32) / np.float32(HD))
    f16 = 10000.0 ** (-np.arange(0, MLA_R, 2, dtype=np.float32) / np.float32(MLA_R))
    return {
        "c_swa": np.ascontiguousarray(swa.reshape(P, -1), np.float32),
        "c_mask": np.ascontiguousarray(np.concatenate([band, pairs], 1), np.float32),
        "c_inv": np.ascontiguousarray(inv, np.float32),
        "c_freq": np.ascontiguousarray(np.concatenate([f32, f16])[None, :], np.float32),
        "c_ident": np.eye(P, dtype=np.float32),
    }


def hybrid_blocks_kernel(nc, x, w_in, pool_w, pool_scale, attn_sinks, w_out, norm_pre, norm_post,
                         positions, attn_norm_g, w_in_2, b_gate, q_norm_g, kv_norm_g, w_uq, w_ukv,
                         w_o_mla, w_o_dil, w_out_2, final_norm_g,
                         c_swa, c_mask, c_inv, c_freq, c_ident, out, upto=99):
    ctx = ExitStack()
    sems = {}
    shared = {
        "product_done": (("u_done", 8), ("pg_done", 8), ("qkv_done", 12), ("ag_done", 8), ("y_done", TT),
                         ("c_done", TT), ("g_done", 48), ("qm_done", 2 * TT), ("y2_done", 2 * KT), ("o_done", TT)),
        "product_copied": (("u_evac", 8), ("pg_evac", 8), ("qkv_evac", 12), ("ag_evac", 8), ("c_evac", TT), ("g_evac", 48)),
        "product_used": (("pg_mul", 8), ("ag_mul", 8), ("y_read", TT), ("qm_read", 2 * TT), ("y2_read", 2 * KT), ("o_read", TT)),
        "input_transposed": (("x_T", 16), ("x1_T", 16), ("cT", 8)),
        "input_high": (("x_hi", 16), ("x1_hi", 16), ("cT_hi", 8)),
        "input_split": (("x_evac", 16), ("x1_evac", 16), ("cT_lo", 8)),
        "rows_scaled": (("x_scaled", TT), ("x1_scaled", TT), ("c_scaled", 2 * TT)),
        "squared": (("x_sq", TT), ("y_sq", TT), ("x1_sq", TT), ("c_sqd", 2 * TT), ("o_sq", TT)),
        "rooted": (("x_root", 1), ("y_root", TT), ("x1_root", 1), ("c_root", 2), ("o_root", TT)),
        "inverted": (("x_rstd", 1), ("y_rstd", TT), ("x1_rstd", 1), ("o_rstd", TT)),
        "scored": (("swa_scored", 16), ("d_scored", 48)),
        "masked": (("swa_masked", 16), ("d_masked", 48)),
        "row_max": (("swa_max", 16), ("d_max", 48)),
        "exponentials": (("swa_exp", 64), ("d_exp", 192)),
        "probs_transposed": (("swa_T", 16), ("d_T", 48)),
        "probs_copied": (("swa_pT", 16), ("d_pT", 48)),
        "values_summed": (("swa_valued", 16), ("d_valued", 48)),
        "values_copied": (("swa_out", 16), ("d_out", 48)),
        "high_part": (("mixT_hi", KT), ("vm_hi", TT), ("mixers_hi", 16)),
        "low_part": (("mixT_split", KT), ("vm_lo", TT), ("mixers_lo", 16)),
        "pool_in_out": (("pool_c", 80), ("pool_spill", 64), ("pool_back", 64)),
    }
    for t in range(TT):
        shared[f"rows_in{t}"] = ((f"x_in{t}", 16), (f"x1_in{t}", 16))
    for b in range(2):
        shared[f"x_tile_in{b}"] = ((f"x_back{b}", 64), (f"x1_back{b}", 64))
        shared[f"tile_out{b}"] = ((f"x1_out{b}", 64), (f"g_spill{b}", 96), (f"d_store{b}", 192), (f"qm_spill{b}", 64))
    alias = {}
    for own, users in shared.items():
        base = 0
        for name, count in users:
            alias[name] = own, base
            base += count

    def sem(name):
        name = alias.get(name, (name, 0))[0]
        if name not in sems:
            sems[name] = ctx.enter_context(nc.semaphore(name))
        return sems[name]

    def after(name, count):
        return sem(name), alias.get(name, (name, 0))[1] + count

    w1 = w_in[0].rearrange("(k p) n -> p k n", p=P)
    w2 = w_in_2[0].rearrange("(k p) n -> p k n", p=P)
    wo1 = w_out[0].rearrange("(k p) n -> p k n", p=P)
    wo2 = w_out_2[0].rearrange("(k p) n -> p k n", p=P)

    def panel(w, c0, n=COLS):
        return [(k, n, w[:, k:k + CHUNK_K, c0:c0 + n]) for k in range(0, KT, CHUNK_K)]

    off2 = np.cumsum([0, C_Q, C_KV, MLA_R, 512, DIL_QKV, DIL_QKV, DIL_QKV, 512, D, D]).tolist()
    o_c, _, _, o_zm, o_q, o_k, o_v, o_zd, o_gm, o_gd, _ = off2
    panels = []
    index = {}

    def add(name, chunks):
        index[name] = len(panels)
        panels.append(chunks)

    add("u", panel(w1, 0))
    add("pgate", panel(w1, 512))
    add("q", panel(w1, 1024))
    add("kv", panel(w1, 1536, 256))
    add("agate", panel(w1, 1792))
    add("o0", panel(wo1, 0))
    add("o1", panel(wo1, 512))
    add("c", panel(w2, o_c, C_W))
    add("zm", panel(w2, o_zm))
    add("zd", panel(w2, o_zd))
    for i in range(2):
        add(f"gm{i}", panel(w2, o_gm + COLS * i))
    for i in range(2):
        add(f"gd{i}", panel(w2, o_gd + COLS * i))
    for g in range(3):
        add(f"k{g}", panel(w2, o_k + COLS * g))
        add(f"v{g}", panel(w2, o_v + COLS * g))
        add(f"q{g}", panel(w2, o_q + COLS * g))
    uq = w_uq[0].rearrange("(k p) n -> p k n", p=P)
    ukv = w_ukv[0].rearrange("p (k n) -> p k n", k=2)
    add("mla", [(0, 384, uq[:, :, 0:384]), (2, 384, uq[:, :, 384:768]), (4, 512, ukv)])
    for name, w in (("om", w_o_mla), ("od", w_o_dil)):
        wk = w[0].rearrange("(k p) n -> p k n", p=P)
        add(name, [(4 * n + k, COLS, wk[:, k:k + 2, COLS * n:COLS * n + COLS])
                   for n in range(2) for k in (0, 2)])
    add("p0", panel(wo2, 0))
    add("p1", panel(wo2, 512))
    if upto <= 1:
        panels = panels[:7]
    elif upto <= 2:
        panels = panels[:index["mla"]]
    chunk_end = np.cumsum([len(p) for p in panels]).tolist()

    x1_d = nc.dram_tensor("x1_scr", [S, D], F32, kind="Internal").ap()
    pool_d = nc.dram_tensor("pool_scr", [512, S], F32, kind="Internal").ap()
    zm_d = nc.dram_tensor("zm_scr", [512, S], F32, kind="Internal").ap()
    zd_d = nc.dram_tensor("zd_scr", [512, S], F32, kind="Internal").ap()
    g_d = nc.dram_tensor("gate_scr", [2 * D, S], F32, kind="Internal").ap()
    rope_d = nc.dram_tensor("rope_scr", [P, 2 * TT * MLA_R // 2], F32, kind="Internal").ap()
    c_d = nc.dram_tensor("c_scr", [S, C_W], F32, kind="Internal").ap()
    qm_d = nc.dram_tensor("qmla_scr", [S, H1 * MLA_QK], F32, kind="Internal").ap()
    am_d = nc.dram_tensor("amla_scr", [512, S], F32, kind="Internal").ap()
    dd_d = nc.dram_tensor("dilout_scr", [512, S], F32, kind="Internal").ap()
    dil_d = [nc.dram_tensor(f"dil{g}_scr", [S, 512 + STAT], F32, kind="Internal").ap()
             for g in range(3)]

    def sb(name, shape, dt=F32, scope=ctx):
        return scope.enter_context(nc.sbuf_tensor(name, shape, dt))

    ps = ctx.enter_context(nc.psum_tensor("ps", [P, 8, COLS], F32))
    ident = sb("ident", [P, P])
    stage = sb("w_stage", [P, STAGE, CHUNK_K, COLS])
    wh = sb("w_hi", [P, 2, KT, COLS], F32R)
    wl = sb("w_lo", [P, 2, KT, COLS], F32R)
    small = sb("small", [P, 88])
    EPS_C = small[:, 87:88]
    ssq, rstd = small[:, 0:8], small[:, 8:16]
    gain_pre, pscale = small[:, 16:24], small[:, 24:28]
    gain_2 = small[:, 28:36]
    gain_q, gain_kv = small[:, 36:38], small[:, 38:39]
    bgate = small[:, 40:56]
    sinks_n = small[:, 56:64]
    sinks_p = small[:, 64:72]

    keep = ExitStack()
    aT = sb("attn_outT", [P, 4, S], F32, keep)
    a1 = ExitStack()
    hTh = sb("h1T_hi", [P, KT, S], F32R, a1)
    hTl = sb("h1T_lo", [P, KT, S], F32R, a1)
    s0 = ExitStack()
    xt = sb("x_tiles", [P, TT, D], F32, s0)
    junk = sb("x_sq", [P, D], F32, s0)
    s0.close()
    s1 = ExitStack()
    uT = sb("uT", [P, 2, PAD + S], F32, s1)
    sA = sb("wsumA", [P, PAD + S], F32, s1)
    sB = sb("wsumB", [P, PAD + S], F32, s1)
    pooled = sb("pooled", [P, 2, S], F32, s1)
    edge = sb("pool_edge", [P, 4, PAD], F32, s1)
    edge_t = sb("pool_edge_t", [P, PAD], F32, s1)
    pool_wt = sb("pool_wt", [P, 4, P], F32, s1)
    pmT = sb("pool_outT", [P, 4, S], F32, s1)
    sg1 = sb("silu_pool", [P, 2, COLS], F32, s1)
    s1.close()
    s2 = ExitStack()
    qT = sb("q1T", [P, 4, S], F32, s2)
    kT = sb("k1T", [P, S], F32, s2)
    vT = sb("v1T", [P, S], F32, s2)
    v1 = sb("v1", [P, TT, P], F32, s2)
    swa_b = sb("swa_bias", [P, H1, 2 * P], F32, s2)
    pr = sb("probs", [P, 2, G, 2 * P], F32, s2)
    pT = sb("probsT", [P, 2 * G, P], F32, s2)
    ao = sb("attn_tok", [P, H1, HD], F32, s2)
    st = sb("attn_stats", [P, 4, H1], F32, s2)
    s2.close()
    s3 = ExitStack()
    pmR = sb("pool_outT_back", [P, 4, S], F32, s3)
    sgA = sb("silu_attn", [P, 2, COLS], F32, s3)
    s3.close()
    a1.close()
    a2 = ExitStack()
    mTh = sb("mixT_hi", [P, KT, S], F32R, a2)
    mTl = sb("mixT_lo", [P, KT, S], F32R, a2)
    sb("pool_outT_place", [P, 4, S], F32, a2)
    xr = sb("x_back", [P, 2, D], F32, a2)
    yn = sb("y_normed", [P, D], F32, a2)
    ysq = sb("y_sq", [P, D], F32, a2)
    x1 = sb("x1_tile", [P, 2, D], F32, a2)
    gpost = sb("gain_post", [P, D], F32, a2)
    a2.close()
    keep.close()

    b1 = ExitStack()
    h2h = sb("h2T_hi", [P, KT, S], F32R, b1)
    h2l = sb("h2T_lo", [P, KT, S], F32R, b1)
    cos_d = sb("cos_dil", [P, 3, TT, FREQS], F32, b1)
    sin_d = sb("sin_dil", [P, 3, TT, FREQS], F32, b1)
    cos_m = sb("cos_mla", [P, TT, MLA_R // 2], F32, b1)
    sin_m = sb("sin_mla", [P, TT, MLA_R // 2], F32, b1)
    s5 = ExitStack()
    xt2 = sb("x1_tiles", [P, TT, D], F32, s5)
    junk2 = sb("x1_sq", [P, D], F32, s5)
    posi = sb("positions", [P, 3, TT], I32, s5)
    posf = sb("positions_f", [P, 3, TT], F32, s5)
    freq = sb("freqs", [P, FREQS + MLA_R // 2], F32, s5)
    ang = sb("angles", [P, 28, FREQS], F32, s5)
    turn = sb("turns", [P, 28, FREQS], F32, s5)
    red = sb("reduced", [P, 28, FREQS], F32, s5)
    s5.close()
    s6 = ExitStack()
    c_sb = sb("c_tok", [P, TT, C_W], F32, s6)
    c_sq = sb("c_sq", [P, C_Q], F32, s6)
    c_ss = sb("c_ss", [P, 2, TT], F32, s6)
    c_t = sb("c_rope_t", [P, 4, TT, MLA_R // 2], F32, s6)
    s6.close()
    s7 = ExitStack()
    gt = sb("gate_tiles", [P, 4, S], F32, s7)
    s7.close()
    s8 = ExitStack()
    kTd = sb("kT_dil", [P, 4, S], F32, s8)
    vd = sb("v_dil", [P, TT + 1, COLS], F32, s8)
    rc = sb("rope_cos_part", [P, COLS], F32, s8)
    rs = sb("rope_sin_part", [P, COLS], F32, s8)
    rr = sb("rope_out", [P, COLS], F32, s8)
    qTd = sb("qT_dil", [P, 2, 4, P], F32, s8)
    prd = sb("probs_dil", [P, 2, G, 2 * P], F32, s8)
    pTd = sb("probsT_dil", [P, 2 * G, P], F32, s8)
    osb = sb("dil_out", [P, 2, COLS + STAT], F32, s8)
    masks = sb("masks", [P, MASK_W + P], F32, s8)
    s8.close()
    b1.close()
    s9 = ExitStack()
    nums = sb("dil_nums", [P, 2, 3, COLS], F32, s9)
    stats = sb("dil_stats", [P, 3, TT, STAT], F32, s9)
    coef = sb("dil_coef", [P, 3, TT, H1], F32, s9)
    joint = sb("dil_joint", [P, TT, H1], F32, s9)
    dsum = sb("dil_sum", [P, TT, H1], F32, s9)
    wsum = sb("dil_weighted", [P, 3, COLS], F32, s9)
    zdT = sb("z_dilT", [P, 4, S], F32, s9)
    dgT = sb("dil_gatedT", [P, 4, S], F32, s9)
    s9.close()
    b2 = ExitStack()
    cqh, cql = (sb(f"cqT_{x}", [P, 2, S], F32R, b2) for x in ("hi", "lo"))
    ckh, ckl = (sb(f"ckvT_{x}", [P, S], F32R, b2) for x in ("hi", "lo"))
    Kh, Kl = (sb(f"kT_mla_{x}", [MLA_QK, 2, S], F32R, b2) for x in ("hi", "lo"))
    Vh, Vl = (sb(f"v_mla_{x}", [P, TT, COLS], F32R, b2) for x in ("hi", "lo"))
    s10 = ExitStack()
    c_bk = sb("c_back", [P, TT, C_W], F32, s10)
    q_sb = sb("q_tok", [P, 2, H1, MLA_QK], F32, s10)
    q_t = sb("q_rope_t", [P, 4, H1, MLA_R // 2], F32, s10)
    cos_q = sb("cos_mla_q", [P, TT, MLA_R // 2], F32, s10)
    sin_q = sb("sin_mla_q", [P, TT, MLA_R // 2], F32, s10)
    s10.close()
    Qh, Ql = (sb(f"qT_mla_{x}", [MLA_QK, 2, S], F32R, b2) for x in ("hi", "lo"))
    PTh, PTl = (sb(f"pT_mla_{x}", [P, 2, TT, 2 * P], F32R, b2) for x in ("hi", "lo"))
    pm = sb("p_mla", [P, 2, S], F32, b2)
    am = sb("a_mla", [P, 2, 2 * P], F32, b2)
    zm = sb("z_mlaT", [P, 2, 2 * P], F32, b2)
    qm = sb("q_tok_back", [P, TT, MLA_QK], F32, b2)
    b2.close()
    b3 = ExitStack()
    Mh, Ml = (sb(f"mergedT_{x}", [P, KT, S], F32R, b3) for x in ("hi", "lo"))
    s11 = ExitStack()
    oh, ol = (sb(f"mixersT_{x}", [P, 8, COLS], F32R, s11) for x in ("hi", "lo"))
    raw = sb("mixersT", [P, 8, COLS], F32, s11)
    gg = sb("gates", [P, 2, 2, COLS], F32, s11)
    yg = sb("y_gated", [P, 2, COLS], F32, s11)
    s11.close()
    s12 = ExitStack()
    xr2 = sb("x1_back", [P, 2, D], F32, s12)
    oo = sb("block_out", [P, D], F32, s12)
    osq = sb("block_out_sq", [P, D], F32, s12)
    fin = sb("final", [P, 2, D], F32, s12)
    gfin = sb("gain_final", [P, D], F32, s12)
    s12.close()
    b3.close()

    GATES = ("zm", "zd", "gm0", "gm1", "gd0", "gd1")
    C_KINDS = ((0, P), (P, P), (C_Q, P), (C_W - MLA_QK, MLA_QK))
    C_UNITS = [(n, kind) for n in range(HALF) for kind in range(4)]

    def tile_start(g, t):
        return ((P * t, 1), (t // 2 + 4 * P * (t % 2), 4), (t, 8))[g]

    def spread(start, step):
        return lambda h, k: h[:, k, start:start + step * (P - 1) + 1:step]

    def group_toks(g, t):
        return spread(*tile_start(g, t))

    def value_tiles(g):
        if g:
            return [(t, group_toks(g, t)) for t in range(TT)]
        starts = [0] + [P * t - HD for t in range(1, TT)] + [S - P]
        return [(t, spread(s_, 1)) for t, s_ in enumerate(starts)]

    def window(g, t):
        if g == 2:
            return P * t, P, MASK_W, [(0, P, t, 0, P)]
        if g == 1:
            first = t - t % 2
            return P * first, 2 * P, P * (1 - t % 2), [(0, P, first, 0, P), (P, P, first + 1, 0, P)]
        if t == 0:
            return 0, 3 * HD, P, [(0, HD, 0, 0, HD), (HD, P, 1, 0, P)]
        if t == TT - 1:
            return S - 3 * HD, 3 * HD, HD, [(0, P, t, 0, P), (HD, P, t + 1, HD, HD)]
        return P * t - HD, 2 * P, HD, [(0, P, t, 0, P), (P, P, t + 1, 0, P)]

    n_t = H1 * TT

    def d_step(g, i):
        return HH * TT * g + i

    block = ctx.enter_context(nc.Block())
    ENG = ("pe", "act", "dve")

    def phase_end(e, who):
        e.drain().then_inc(sem(f"through_{who}"), 1)

    def phase_start(e, who, n):
        for other in ENG:
            if other != who:
                e.wait_ge(*after(f"through_{other}", n))

    @block.sync
    def _(sp):
        n = 0
        for chunks in panels:
            for k, cols, src in chunks:
                if n >= STAGE:
                    sp.wait_ge(*after("w_split", n - STAGE + 1))
                sp.dma_start(stage[:, n % STAGE, :, 0:cols], src).then_inc(sem(f"w_landed{n % STAGE}"), 16)
                n += 1

    @block.gpsimd
    def _(pool):
        n = 0
        for p, chunks in enumerate(panels):
            if p >= 2:
                pool.wait_ge(*after("panel_used", p - 1))
            for k, cols, src in chunks:
                raw = stage[:, n % STAGE, :, 0:cols]
                hi = wh[:, p % 2, k:k + CHUNK_K, 0:cols]
                lo = wl[:, p % 2, k:k + CHUNK_K, 0:cols]
                parts = [(raw, hi, lo)]
                if p == index["q"]:
                    parts = [(raw[:, i].rearrange("p (a m c) -> p m a c", a=2, c=HD),
                              *(w[:, i].rearrange("p (m a c) -> p m a c", a=2, c=HD) for w in (hi, lo)))
                             for i in range(CHUNK_K)]
                pool.wait_ge(*after(f"w_landed{n % STAGE}", 16 * (n // STAGE + 1)))
                for raw_, hi_, _ in parts:
                    last = nc.gpsimd.tensor_copy(hi_, raw_)
                last.then_inc(sem("w_high"), 1)
                pool.wait_ge(*after("w_high", n + 1))
                for raw_, hi_, lo_ in parts:
                    last = nc.gpsimd.tensor_tensor(lo_, raw_, hi_.bitcast(F32), ALU.subtract)
                last.then_inc(sem("w_split"), 1)
                n += 1

    @block.tensor
    def _(pe):
        units = {"n": 0}

        def panel_ready(name):
            pe.wait_ge(*after("w_split", chunk_end[index[name]]))

        def unit_bank(phase, ring, u, free):
            if u >= ring:
                pe.wait_ge(*after(free, u - ring + 1))
            return u % ring

        def three_passes(acc, pairs, last_inc=None, n_k=KT):
            m = None
            for i, (ah, al, bh, bl) in enumerate(pairs):
                for j, (a, b) in enumerate(((ah, bh), (ah, bl), (al, bh))):
                    m = pe.matmul(acc, a, b, start=(i == 0 and j == 0),
                                  stop=(i == len(pairs) - 1 and j == 2))
            return m

        def wide_unit(name, acc, hh, hl, n, wcols):
            s = index[name] % 2
            sl = slice(COLS * n, COLS * n + COLS)
            return three_passes(acc, [(wcols(wh, s, k), wcols(wl, s, k), hh[:, k, sl], hl[:, k, sl])
                                      for k in range(KT)])

        def tok_unit(name, acc, hh, hl, toks, cols=COLS, k0=0, n_k=KT):
            s = index[name] % 2
            return three_passes(acc, [(toks(hh, k), toks(hl, k), wh[:, s, k0 + k, 0:cols], wl[:, s, k0 + k, 0:cols])
                                      for k in range(n_k)])

        def plain_cols(m):
            return lambda w, s, k: w[:, s, k, P * m:P * m + P]

        def plain_toks(t):
            return lambda h, k: h[:, k, P * t:P * t + P]

        pe.wait_ge(*after("const", 16 * 8))
        def transposes_in(tiles, tag):
            for n in range(HALF):
                for k in range(KT):
                    u = n * KT + k
                    b = unit_bank(tag, 4, u, f"{tag}_evac")
                    for j in range(4):
                        t = 4 * n + j
                        if k == 0:
                            pe.wait_ge(*after(f"{tag}_scaled", t + 1))
                        m = pe.transpose(ps[:, b, P * j:P * j + P], tiles[:, t, P * k:P * k + P], ident[:])
                    m.then_inc(sem(f"{tag}_T"), 1)
        transposes_in(xt, "x")
        phase_end(pe, "pe")

        phase_start(pe, "pe", 1)
        panel_ready("u")
        for g in range(4):
            for n in range(HALF):
                u = 2 * g + n
                b = unit_bank("u", 4, u, "u_evac")
                wide_unit("u", ps[:, b, :], hTh, hTl, n, plain_cols(g)).then_inc(sem("u_done"), 1)
        pe.drain().then_inc(sem("panel_used"), 1)
        panel_ready("pgate")

        def pool_mix(g):
            pe.wait_ge(*after("pooled", g + 1))
            for n in range(HALF):
                u = 2 * g + n
                if u >= 2:
                    pe.wait_ge(*after("mix_evac", u - 1))
                pe.matmul(ps[:, 4 + u % 2, :], pool_wt[:, g, :], pooled[:, g % 2, COLS * n:COLS * n + COLS],
                          start=True, stop=True).then_inc(sem("mix_done"), 1)

        for m in range(4):
            pool_mix(m)
            for n in range(HALF):
                u = 2 * m + n
                if u == 0:
                    pe.wait_ge(*after("u_evac", 8))
                b = unit_bank("pg", 2, u, "pg_evac")
                wide_unit("pgate", ps[:, b, :], hTh, hTl, n, plain_cols(m)).then_inc(sem("pg_done"), 1)
        pe.drain().then_inc(sem("panel_used"), 1)
        phase_end(pe, "pe")

        phase_start(pe, "pe", 2)
        u = 0
        for name, ms in (("q", range(4)), ("kv", range(2))):
            panel_ready(name)
            for m in ms:
                for n in range(HALF):
                    b = unit_bank("qkv", 4, u, "qkv_evac")
                    wide_unit(name, ps[:, b, :], hTh, hTl, n, plain_cols(m)).then_inc(sem("qkv_done"), 1)
                    u += 1
            pe.drain().then_inc(sem("panel_used"), 1)
        pe.wait_ge(*after("qkv_evac", u))
        for half in range(2):
            for j in range(4):
                t = 4 * half + j
                m = pe.transpose(ps[:, 4 + half, P * j:P * j + P], vT[:, P * t:P * t + P], ident[:])
            m.then_inc(sem("v1_T"), 1)
        pe.wait_ge(*after("v1_evac", 2))

        def keys_of(t):
            return (0, P) if t == 0 else (P * (t - 1), 2 * P)

        def swa_scores(i):
            t, hh = divmod(i, HH)
            k0, nk = keys_of(t)
            if i >= 1:
                pe.wait_ge(*after("swa_masked", i))
            for j in range(G):
                h = G * hh + j
                rows = slice(HD * (h // 4), HD * (h // 4) + HD)
                m = pe.matmul(ps[:, j // 2, (j % 2) * 256:(j % 2) * 256 + nk], qT[rows, h % 4, P * t:P * t + P],
                              kT[rows, k0:k0 + nk], start=True, stop=True)
            m.then_inc(sem("swa_scored"), 1)

        def swa_transposes(i):
            t, hh = divmod(i, HH)
            nb = keys_of(t)[1] // P
            pe.wait_ge(*after("swa_exp", G * (i + 1)))
            if i >= 1:
                pe.wait_ge(*after("swa_pT", i))
            for j in range(G):
                for kb in range(nb):
                    c = 2 * j + kb
                    m = pe.transpose(ps[:, 2 + c // 4, (c % 4) * P:(c % 4) * P + P],
                                     pr[:, i % 2, j, P * kb:P * kb + P], ident[:])
            m.then_inc(sem("swa_T"), 1)

        def swa_values(i):
            t, hh = divmod(i, HH)
            nb = keys_of(t)[1] // P
            pe.wait_ge(*after("swa_pT", i + 1))
            if i >= 2:
                pe.wait_ge(*after("swa_out", i - 1))
            for j in range(G):
                h = G * hh + j
                for kb in range(nb):
                    kt = t - nb + 1 + kb
                    m = pe.matmul(ps[:, 4 + i % 2, HD * j:HD * j + HD], pT[:, 2 * j + kb, :],
                                  v1[:, kt, HD * (h // 4):HD * (h // 4) + HD], start=(kb == 0), stop=(kb == nb - 1))
            m.then_inc(sem("swa_valued"), 1)

        def swa_back(t):
            pe.wait_ge(*after("swa_out", 2 * t + 2))
            if t >= 1:
                pe.wait_ge(*after("swa_aT", t))
            flat = ao[:].rearrange("p h d -> p (h d)")
            for j in range(4):
                m = pe.transpose(ps[:, 6, P * j:P * j + P], flat[:, P * j:P * j + P], ident[:])
            m.then_inc(sem("swa_backT"), 1)

        steps = TT * HH
        for i in range(steps + 2):
            if i < steps:
                swa_scores(i)
            if i >= 2:
                swa_values(i - 2)
                if (i - 2) % HH == HH - 1:
                    swa_back((i - 2) // HH)
            if 1 <= i <= steps:
                swa_transposes(i - 1)
        phase_end(pe, "pe")

        phase_start(pe, "pe", 3)
        panel_ready("agate")
        for m in range(4):
            for n in range(HALF):
                u = 2 * m + n
                b = unit_bank("ag", 4, u, "ag_evac")
                wide_unit("agate", ps[:, b, :], hTh, hTl, n, plain_cols(m)).then_inc(sem("ag_done"), 1)
        pe.drain().then_inc(sem("panel_used"), 1)
        phase_end(pe, "pe")

        phase_start(pe, "pe", 4)
        panel_ready("o1")
        pe.wait_ge(*after("mixT_split", KT))
        for t in range(TT):
            if t >= 2:
                pe.wait_ge(*after("y_read", t - 1))
            for half, name in enumerate(("o0", "o1")):
                m = tok_unit(name, ps[:, 2 * (t % 2) + half, :], mTh, mTl, plain_toks(t))
            m.then_inc(sem("y_done"), 1)
        pe.drain().then_inc(sem("panel_used"), 2)
        phase_end(pe, "pe")

        phase_start(pe, "pe", 5)
        transposes_in(xt2, "x1")
        phase_end(pe, "pe")

        phase_start(pe, "pe", 6)
        panel_ready("c")
        for t in range(TT):
            b = unit_bank("c", 4, t, "c_evac")
            tok_unit("c", ps[:, b, 0:C_W], h2h, h2l, plain_toks(t), C_W).then_inc(sem("c_done"), 1)
        pe.drain().then_inc(sem("panel_used"), 1)
        phase_end(pe, "pe")

        phase_start(pe, "pe", 7)
        u = 0
        for name in GATES:
            panel_ready(name)
            for m in range(4):
                for n in range(HALF):
                    b = unit_bank("g", 4, u, "g_evac")
                    wide_unit(name, ps[:, b, :], h2h, h2l, n, plain_cols(m)).then_inc(sem("g_done"), 1)
                    u += 1
            pe.drain().then_inc(sem("panel_used"), 1)
        phase_end(pe, "pe")

        phase_start(pe, "pe", 8)
        pe.wait_ge(*after("masks_in", 16))
        nu = [0, 0]

        def proj(name, toks, part=None):
            s = index[name] % 2
            if part in (None, 0):
                if nu[0] >= 2:
                    pe.wait_ge(*after("d_read", nu[0] - 1))
            acc = ps[:, nu[0] % 2, :]
            ks = {None: range(KT), 0: range(KT // 2), 1: range(KT // 2, KT)}[part]
            for k in ks:
                for a, b in ((h2h, wh), (h2h, wl), (h2l, wh)):
                    m = pe.matmul(acc, toks(a, k), b[:, s, k, :], start=(k == 0 and b is wh and a is h2h),
                                  stop=(k == KT - 1 and a is h2l))
            if part in (None, 1):
                m.then_inc(sem("d_done"), 1)
                nu[0] += 1

        def rotated_transposes():
            r = nu[1]
            pe.wait_ge(*after("rotated", r + 1))
            if r >= 1:
                pe.wait_ge(*after("rotT_read", r))
            for j in range(4):
                m = pe.transpose(ps[:, 2, P * j:P * j + P], rr[:, P * j:P * j + P], ident[:])
            m.then_inc(sem("rotT"), 1)
            nu[1] += 1

        def d_scores(g, i):
            n = d_step(g, i)
            t, hh = divmod(i, HH)
            k0, nk, _, _ = window(g, t)
            pe.wait_ge(*after("rotT_read", 2 * TT * g + TT + t + 1))
            if n >= 1:
                pe.wait_ge(*after("d_masked", n))
            for j in range(G):
                h = G * hh + j
                rows = slice(HD * (h % 2), HD * (h % 2) + HD)
                m = pe.matmul(ps[:, 3 + j % 2, (j // 2) * 256:(j // 2) * 256 + nk], qTd[rows, t % 2, h // 2, :],
                              kTd[rows, h // 2, k0:k0 + nk], start=True, stop=True)
            m.then_inc(sem("d_scored"), 1)

        def d_transposes(g, i):
            n = d_step(g, i)
            blocks = window(g, i // HH)[3]
            pe.wait_ge(*after("d_exp", G * (n + 1)))
            if n >= 1:
                pe.wait_ge(*after("d_pT", n))
            for j in range(G):
                for kb, (c0, width, _, _, _) in enumerate(blocks):
                    c = 2 * j + kb
                    m = pe.transpose(ps[0:width, 5 + c // 4, (c % 4) * P:(c % 4) * P + P],
                                     prd[:, i % 2, j, c0:c0 + width], ident[:])
            m.then_inc(sem("d_T"), 1)

        def d_values(g, i):
            n = d_step(g, i)
            t, hh = divmod(i, HH)
            blocks = window(g, t)[3]
            pe.wait_ge(*after("d_pT", n + 1))
            if n >= 1:
                pe.wait_ge(*after("d_out", n))
            for j in range(G):
                h = G * hh + j
                for kb, (_, _, vt, r0, nr) in enumerate(blocks):
                    m = pe.matmul(ps[:, 7, HD * j:HD * j + HD], pTd[r0:r0 + nr, 2 * j + kb, :],
                                  vd[r0:r0 + nr, vt, HD * h:HD * h + HD], start=(kb == 0), stop=(kb == len(blocks) - 1))
            m.then_inc(sem("d_valued"), 1)

        for g in range(3):
            panel_ready(f"k{g}")
            for t in range(TT + 1):
                if t < TT:
                    proj(f"k{g}", group_toks(g, t))
                if t >= 1:
                    rotated_transposes()
            pe.drain().then_inc(sem("panel_used"), 1)
            panel_ready(f"v{g}")
            for s0_, toks in value_tiles(g):
                proj(f"v{g}", toks)
            pe.drain().then_inc(sem("panel_used"), 1)
            panel_ready(f"q{g}")
            pe.wait_ge(*after("d_read", nu[0]))
            for t in range(TT + 2):
                a = 2 * (t - 1)
                if 0 <= a < 2 * TT:
                    d_scores(g, a)
                if 0 <= a - 1 < 2 * TT:
                    d_values(g, a - 1)
                if t < TT:
                    proj(f"q{g}", group_toks(g, t), 0)
                if 0 <= a < 2 * TT:
                    d_transposes(g, a)
                    d_scores(g, a + 1)
                if t < TT:
                    proj(f"q{g}", group_toks(g, t), 1)
                if 0 <= a < 2 * TT:
                    d_values(g, a)
                    d_transposes(g, a + 1)
                if t < TT:
                    rotated_transposes()
            pe.drain().then_inc(sem("panel_used"), 1)
        phase_end(pe, "pe")

        phase_start(pe, "pe", 9)
        for t in range(TT):
            pe.wait_ge(*after("joint", t + 1))
            if t >= 2:
                pe.wait_ge(*after("dg_done", t - 1))
            for j in range(4):
                m = pe.transpose(ps[:, t % 2, P * j:P * j + P], wsum[:, 0, P * j:P * j + P], ident[:])
            m.then_inc(sem("jointT"), 1)
        phase_end(pe, "pe")

        phase_start(pe, "pe", 10)
        pe.wait_ge(*after("c_back", 16))
        for u, (n, kind) in enumerate(C_UNITS):
            b = unit_bank("cT", 4, u, "cT_lo")
            c0, width = C_KINDS[kind]
            for j in range(4):
                m = pe.transpose(ps[0:width, b, P * j:P * j + P], c_bk[:, 4 * n + j, c0:c0 + width], ident[:])
            m.then_inc(sem("cT"), 1)
        pe.wait_ge(*after("cT_lo", len(C_UNITS)))
        panel_ready("mla")
        s = index["mla"] % 2
        for t in range(TT):
            for half in range(2):
                u = 2 * t + half
                if u >= 4:
                    pe.wait_ge(*after("qm_read", u - 3))
                three_passes(ps[:, u % 4, 0:384], [
                    (cqh[:, k, P * t:P * t + P], cql[:, k, P * t:P * t + P],
                     wh[:, s, 2 * half + k, 0:384], wl[:, s, 2 * half + k, 0:384]) for k in range(2)]).then_inc(sem("qm_done"), 1)
            if t >= 2:
                pe.wait_ge(*after("vm_lo", t - 1))
            for n in range(2):
                v_cols = [w[:, s, 4 + n, :].rearrange("p (h c) -> p h c", c=P)[:, :, HD:] for w in (wh, wl)]
                m = three_passes(ps[:, 4 + t % 2, 256 * n:256 * n + 256].rearrange("p (h c) -> p h c", c=HD), [
                    (ckh[:, P * t:P * t + P], ckl[:, P * t:P * t + P], *v_cols)])
            m.then_inc(sem("vm_done"), 1)
        phase_end(pe, "pe")

        phase_start(pe, "pe", 11)

        def head_inputs(h, part):
            x = 4 * h + part
            if x >= 1:
                pe.wait_ge(*after("qk_lo", x))
            if part < 2:
                pe.wait_ge(*after("qm_back", 16 * (h + 1)))
                for j in range(4):
                    m = pe.transpose(ps[0:MLA_QK, 7, P * j:P * j + P], qm[:, 4 * part + j, :], ident[:])
            else:
                n = part - 2
                w = [y[:, s, 4 + h // 4, P * (h % 4):P * (h % 4) + P] for y in (wh, wl)]
                m = three_passes(ps[:, 7, :], [(*w, ckh[:, COLS * n:COLS * n + COLS], ckl[:, COLS * n:COLS * n + COLS])])
            m.then_inc(sem("qk_done"), 1)

        def m_scores(i):
            h, qt = divmod(i, TT)
            pe.wait_ge(*after("qk_lo", 4 * h + 4))
            if i >= 2:
                pe.wait_ge(*after("m_exp", i - 1))
            for n in range(HALF):
                m = three_passes(ps[:, 2 * (i % 2) + n, :], [
                    (Qh[:, h % 2, P * qt:P * qt + P], Ql[:, h % 2, P * qt:P * qt + P],
                     Kh[:, h % 2, COLS * n:COLS * n + COLS], Kl[:, h % 2, COLS * n:COLS * n + COLS])])
            m.then_inc(sem("m_scored"), 1)

        def m_transposes(i):
            pe.wait_ge(*after("m_normed", i + 1))
            if i >= 1:
                pe.wait_ge(*after("m_lo", i))
            for kt in range(TT):
                m = pe.transpose(ps[:, 4 + kt // 4, (kt % 4) * P:(kt % 4) * P + P], pm[:, i % 2, P * kt:P * kt + P], ident[:])
            m.then_inc(sem("m_T"), 1)

        def m_values(b):
            h = b // 4
            pe.wait_ge(*after("m_lo", 2 * b + 2))
            if b >= 1:
                pe.wait_ge(*after("m_out", b))
            c = P * (h // 2)
            three_passes(ps[:, 6, 0:256], [(Vh[:, kt, c:c + P], Vl[:, kt, c:c + P], PTh[:, b % 2, kt, :], PTl[:, b % 2, kt, :])
                                           for kt in range(TT)]).then_inc(sem("m_valued"), 1)

        for part in range(4):
            head_inputs(0, part)
        for i in range(H1 * TT + 2):
            if i < H1 * TT:
                m_scores(i)
                h, qt = divmod(i, TT)
                if h + 1 < H1 and qt in (2, 3, 4, 5):
                    head_inputs(h + 1, qt - 2)
            if i >= 3 and i % 2 == 1:
                m_values((i - 3) // 2)
            if 1 <= i <= H1 * TT:
                m_transposes(i - 1)
        pe.drain().then_inc(sem("panel_used"), 1)
        phase_end(pe, "pe")

        phase_start(pe, "pe", 12)
        panel_ready("od")
        for n in range(HALF):
            pe.wait_ge(*after("mixers_lo", 8 * n + 8))
            for m_ in range(KT):
                u = KT * n + m_
                if u >= 2:
                    pe.wait_ge(*after("y2_read", u - 1))
                for o, name in enumerate(("om", "od")):
                    s = index[name] % 2
                    c = P * (m_ % 4)
                    m = three_passes(ps[:, 2 * (u % 2) + o, :], [
                        (wh[:, s, 4 * (m_ // 4) + k, c:c + P], wl[:, s, 4 * (m_ // 4) + k, c:c + P],
                         oh[:, 4 * o + k, :], ol[:, 4 * o + k, :]) for k in range(4)])
                m.then_inc(sem("y2_done"), 1)
        pe.drain().then_inc(sem("panel_used"), 2)
        phase_end(pe, "pe")

        phase_start(pe, "pe", 13)
        panel_ready("p1")
        for t in range(TT):
            if t >= 2:
                pe.wait_ge(*after("o_read", t - 1))
            for half, name in enumerate(("p0", "p1")):
                m = tok_unit(name, ps[:, 2 * (t % 2) + half, :], Mh, Ml, plain_toks(t))
            m.then_inc(sem("o_done"), 1)

    @block.scalar
    def _(act):
        x_tok = x[0].rearrange("(t p) d -> t p d", p=P)
        for t in range(TT):
            act.dma_start(xt[:, t, :], x_tok[t]).then_inc(sem(f"x_in{t}"), 16)
        consts = [
            (ident[:], c_ident),
            (gain_pre, norm_pre[0].rearrange("(k p) -> p k", p=P)),
            (pscale, pool_scale[0].rearrange("(k p) -> p k", p=P)),
            (gain_2, attn_norm_g[0].rearrange("(k p) -> p k", p=P)),
            (gain_q, q_norm_g[0].rearrange("(k p) -> p k", p=P)),
            (gain_kv, kv_norm_g[0].rearrange("(k p) -> p k", p=P)),
            (bgate, b_gate[0].rearrange("(k p) -> p k", p=P)),
            (sinks_p, attn_sinks[0:1, :].to_broadcast([P, H1])),
        ]
        with nc.allow_non_contiguous_dma(reason="vectors of one value a partition"):
            for dst, src in consts:
                act.dma_start(dst, src).then_inc(sem("const"), 16)
        act.wait_ge(*after("zeroed", 1))

        def norm_stats(tiles, width, squares, tag):
            for t in range(TT):
                act.wait_ge(*after(f"{tag}_in{t}", 16))
                act.activation(squares, tiles[:, t, :], ACT.Square, accum_out=ssq[:, t:t + 1]).then_inc(sem(f"{tag}_sq"), 1)
                act.wait_ge(*after(f"{tag}_sq", t + 1))
            act.activation(rstd, ssq, ACT.Sqrt, scale=1.0 / width, bias=EPS_C).then_inc(sem(f"{tag}_root"), 1)

        norm_stats(xt, D, junk[:], "x")
        for n in range(HALF):
            for k in range(KT):
                u = n * KT + k
                act.wait_ge(*after("x_T", u + 1))
                act.activation(hTh[:, k, COLS * n:COLS * n + COLS], ps[:, u % 4, :], ACT.Copy,
                               scale=gain_pre[:, k:k + 1]).then_inc(sem("x_hi"), 1)
        phase_end(act, "act")

        phase_start(act, "act", 1)
        act.dma_start(pool_wt[:], pool_w[0].rearrange("g c d -> c g d")).then_inc(sem("pool_c"), 16)
        for g in range(4):
            act.dma_start(edge[:, g, :], c_inv[g:g + 1, :].to_broadcast([P, PAD])).then_inc(sem("pool_c"), 16)
        act.wait_ge(*after("u_pad", 1))
        for u in range(8):
            g, n = divmod(u, 2)
            act.wait_ge(*after("u_done", u + 1))
            if g >= 2:
                act.wait_ge(*after("pooled", g - 1))
            act.activation(uT[:, g % 2, PAD + COLS * n:PAD + COLS * n + COLS], ps[:, u % 4, :],
                           ACT.Copy).then_inc(sem("u_evac"), 1)
        for u in range(8):
            act.wait_ge(*after("pg_done", u + 1))
            if u >= 2:
                act.wait_ge(*after("pg_mul", u - 1))
            act.activation(sg1[:, u % 2, :], ps[:, u % 2, :], ACT.Silu).then_inc(sem("pg_evac"), 1)
        for g in range(4):
            act.wait_ge(*after("pg_mul", 2 * g + 2))
            act.dma_start(pool_d[P * g:P * g + P, :], pmT[:, g, :]).then_inc(sem("pool_spill"), 16)
        act.wait_ge(*after("pool_spill", 64))
        phase_end(act, "act")

        phase_start(act, "act", 2)
        act.dma_start(swa_b[:].rearrange("p h k -> p (h k)"), c_swa).then_inc(sem("swa_c"), 16)
        for u in range(12):
            act.wait_ge(*after("qkv_done", u + 1))
            m, n = divmod(u, 2)
            sl = slice(COLS * n, COLS * n + COLS)
            dst = qT[:, m, sl] if m < 4 else (kT[:, sl] if m == 4 else vT[:, sl])
            act.activation(dst, ps[:, u % 4, :], ACT.Copy, scale=HD ** -0.5 if m < 4 else 1.0).then_inc(sem("qkv_evac"), 1)
        act.wait_ge(*after("v1_T", 2))
        for half in range(2):
            act.activation(v1[:, 4 * half:4 * half + 4, :], ps[:, 4 + half, :], ACT.Copy).then_inc(sem("v1_evac"), 1)

        steps = TT * HH

        def swa_pT(i):
            nb = 1 if i < HH else 2
            act.wait_ge(*after("swa_T", i + 1))
            if i >= 1:
                act.wait_ge(*after("swa_valued", i))
            src = ps[:, 2:4, :].rearrange("p b (j c) -> p (b j) c", c=P)
            if nb == 1:
                act.activation(pT[:, 0:8:2, :], src[:, 0:8:2, :], ACT.Copy).then_inc(sem("swa_pT"), 1)
            else:
                act.activation(pT[:], src, ACT.Copy).then_inc(sem("swa_pT"), 1)

        for i in range(steps + 1):
            if i < steps:
                t, hh = divmod(i, HH)
                nk = P if t == 0 else 2 * P
                act.wait_ge(*after("swa_max", i + 1))
                for j in range(G):
                    h = G * hh + j
                    act.activation(pr[:, i % 2, j, 0:nk], pr[:, i % 2, j, 0:nk], ACT.Exp,
                                   bias=st[:, 0, h:h + 1], accum_out=st[:, 1, h:h + 1]).then_inc(sem("swa_exp"), 1)
                act.activation(st[:, 2, G * hh:G * hh + G], st[:, 3, G * hh:G * hh + G], ACT.Exp).then_inc(sem("swa_sink"), 1)
            if i >= 1:
                swa_pT(i - 1)
        for t in range(TT):
            pass
        phase_end(act, "act")

        phase_start(act, "act", 3)
        for g in range(4):
            act.dma_start(pmR[:, g, :], pool_d[P * g:P * g + P, :]).then_inc(sem("pool_back"), 16)
        for u in range(8):
            act.wait_ge(*after("ag_done", u + 1))
            if u >= 2:
                act.wait_ge(*after("ag_mul", u - 1))
            act.activation(sgA[:, u % 2, :], ps[:, u % 4, :], ACT.Silu).then_inc(sem("ag_evac"), 1)
        phase_end(act, "act")

        phase_start(act, "act", 4)
        act.wait_ge(*after("pool_back", 64))
        for k in range(KT):
            src = pmR[:, k, :] if k < 4 else aT[:, k - 4, :]
            act.activation(mTh[:, k, :], src, ACT.Copy).then_inc(sem("mixT_hi"), 1)
        act.dma_start(gpost[:], norm_post[0:1, :].to_broadcast([P, D])).then_inc(sem("gpost"), 16)
        x1_tok = x1_d.rearrange("(t p) d -> t p d", p=P)

        def x_back(t):
            if t >= 2:
                act.wait_ge(*after("x1_made", t - 1))
            act.dma_start(xr[:, t % 2, :], x_tok[t]).then_inc(sem(f"x_back{t % 2}"), 16)

        def x1_store(t):
            act.wait_ge(*after("x1_made", t + 1))
            act.dma_start(x1_tok[t], x1[:, t % 2, :]).then_inc(sem(f"x1_out{t % 2}"), 16)

        x_back(0)
        x_back(1)
        for t in range(TT):
            act.wait_ge(*after("y_done", t + 1))
            if t >= 1:
                act.wait_ge(*after("y_sq", t))
            b = 2 * (t % 2)
            act.activation(ysq[:].rearrange("p (b c) -> p b c", b=2), ps[:, b:b + 2, :], ACT.Square,
                           accum_out=ssq[:, t:t + 1]).then_inc(sem("y_sq"), 1)
            act.wait_ge(*after("y_sq", t + 1))
            act.activation(rstd[:, t:t + 1], ssq[:, t:t + 1], ACT.Sqrt, scale=1.0 / D, bias=EPS_C).then_inc(sem("y_root"), 1)
            if t >= 1:
                x1_store(t - 1)
                if t + 1 < TT:
                    x_back(t + 1)
        x1_store(TT - 1)
        for b in range(2):
            act.wait_ge(*after(f"x1_out{b}", 16 * TT // 2))
        phase_end(act, "act")

        phase_start(act, "act", 5)
        with nc.allow_non_contiguous_dma(reason="one position a partition"):
            pos_row = positions[0]
            for g in range(3):
                for t in range(TT):
                    start, step = tile_start(g, t)
                    src = pos_row[start:start + step * (P - 1) + 1:step].rearrange("(p a) -> p a", a=1)
                    act.dma_start(posi[:, g, t:t + 1], src).then_inc(sem("pos_in"), 16)
            act.dma_start(freq[:], c_freq.to_broadcast([P, FREQS + MLA_R // 2])).then_inc(sem("pos_in"), 16)
        for t in range(TT):
            act.dma_start(xt2[:, t, :], x1_tok[t]).then_inc(sem(f"x1_in{t}"), 16)
        norm_stats(xt2, D, junk2[:], "x1")
        for n in range(HALF):
            for k in range(KT):
                u = n * KT + k
                act.wait_ge(*after("x1_T", u + 1))
                act.activation(h2h[:, k, COLS * n:COLS * n + COLS], ps[:, u % 4, :], ACT.Copy,
                               scale=gain_2[:, k:k + 1]).then_inc(sem("x1_hi"), 1)
        for i, (dst, q) in enumerate(((sin_d, 0), (cos_d, 1))):
            act.wait_ge(*after("angles", i + 1))
            act.activation(dst[:].rearrange("p g t f -> p (g t) f"), red[:, 0:24, :], ACT.Sin).then_inc(sem("tables"), 1)
            m_dst = (sin_m, cos_m)[i]
            act.activation(m_dst[:], red[:, 24:28, :].rearrange("p a (b f) -> p (a b) f", b=2), ACT.Sin).then_inc(sem("tables"), 1)
        act.wait_ge(*after("tables", 4))
        w_m = TT * MLA_R // 2
        act.dma_start(rope_d[:, 0:w_m], cos_m[:].rearrange("p t f -> p (t f)")).then_inc(sem("rope_spill"), 16)
        act.dma_start(rope_d[:, w_m:], sin_m[:].rearrange("p t f -> p (t f)")).then_inc(sem("rope_spill"), 16)
        act.wait_ge(*after("rope_spill", 32))
        phase_end(act, "act")

        phase_start(act, "act", 6)
        for t in range(TT):
            act.wait_ge(*after("c_done", t + 1))
            act.activation(c_sb[:, t, :], ps[:, t % 4, 0:C_W], ACT.Copy).then_inc(sem("c_evac"), 1)
            act.wait_ge(*after("c_evac", t + 1))
            for i, (c0, w) in enumerate(((0, C_Q), (C_Q, C_KV))):
                act.activation(c_sq[:, 0:w], c_sb[:, t, c0:c0 + w], ACT.Square, accum_out=c_ss[:, i, t:t + 1]).then_inc(sem("c_sqd"), 1)
                act.wait_ge(*after("c_sqd", 2 * t + i + 1))
        for i, w in enumerate((C_Q, C_KV)):
            act.activation(c_ss[:, i, :], c_ss[:, i, :], ACT.Sqrt, scale=1.0 / w, bias=EPS_C).then_inc(sem("c_root"), 1)
        act.wait_ge(*after("c_roped", 1))
        act.wait_ge(*after("c_scaled", 2 * TT))
        act.dma_start(c_d.rearrange("(t p) c -> p t c", p=P), c_sb[:]).then_inc(sem("c_spill"), 16)
        act.wait_ge(*after("c_spill", 16))
        phase_end(act, "act")

        phase_start(act, "act", 7)
        mt = 0
        for gi, name in enumerate(GATES):
            dst = (zm_d, zd_d, g_d, g_d, g_d, g_d)[gi]
            row0 = 0 if gi < 2 else COLS * (gi - 2)
            for m in range(4):
                if mt >= 4:
                    act.wait_ge(*after(f"g_spill{mt % 4}", 16 * (mt // 4)))
                for n in range(HALF):
                    u = 2 * mt + n
                    act.wait_ge(*after("g_done", u + 1))
                    d = gt[:, mt % 4, COLS * n:COLS * n + COLS]
                    if gi < 2:
                        act.activation(d, ps[:, u % 4, :], ACT.Silu).then_inc(sem("g_evac"), 1)
                    else:
                        c = row0 // P + m
                        act.activation(d, ps[:, u % 4, :], ACT.Sigmoid, bias=bgate[:, c:c + 1]).then_inc(sem("g_evac"), 1)
                act.wait_ge(*after("g_evac", 2 * mt + 2))
                act.dma_start(dst[row0 + P * m:row0 + P * m + P, :], gt[:, mt % 4, :]).then_inc(sem(f"g_spill{mt % 4}"), 16)
                mt += 1
        for b in range(4):
            act.wait_ge(*after(f"g_spill{b}", 16 * mt // 4))
        phase_end(act, "act")

        phase_start(act, "act", 8)
        act.dma_start(masks[:], c_mask).then_inc(sem("masks_in"), 16)
        nrot = 0
        nv = 0

        def rotT_read(g, t, keys):
            act.wait_ge(*after("rotT", nrot + 1))
            src = ps[:, 2, :].rearrange("p (j c) -> p j c", c=P)
            if keys:
                act.activation(kTd[:, :, P * t:P * t + P], src, ACT.Copy).then_inc(sem("rotT_read"), 1)
            else:
                if t >= 2:
                    act.wait_ge(*after("d_scored", d_step(g, 2 * (t - 2) + 2)))
                act.activation(qTd[:, t % 2, :, :], src, ACT.Copy, scale=HD ** -0.5).then_inc(sem("rotT_read"), 1)

        def d_exp(g, i):
            n = d_step(g, i)
            t, hh = divmod(i, HH)
            nk = window(g, t)[1]
            act.wait_ge(*after("d_max", n + 1))
            for j in range(G):
                h = G * hh + j
                o = osb[:, t % 2, :]
                act.activation(prd[:, i % 2, j, 0:nk], prd[:, i % 2, j, 0:nk], ACT.Exp, bias=o[:, COLS + h:COLS + h + 1],
                               accum_out=o[:, COLS + H1 + h:COLS + H1 + h + 1]).then_inc(sem("d_exp"), 1)

        def d_pT(g, i):
            n = d_step(g, i)
            blocks = window(g, i // HH)[3]
            act.wait_ge(*after("d_T", n + 1))
            if n >= 1:
                act.wait_ge(*after("d_valued", n))
            src = ps[:, 5:7, :].rearrange("p b (j c) -> p (b j) c", c=P)
            if len(blocks) == 1:
                act.activation(pTd[:, 0:8:2, :], src[:, 0:8:2, :], ACT.Copy).then_inc(sem("d_pT"), 1)
            elif blocks[0][1] < P:
                w = blocks[0][1]
                act.activation(pTd[0:w, 0:8:2, :], src[0:w, 0:8:2, :], ACT.Copy)
                act.activation(pTd[:, 1:8:2, :], src[:, 1:8:2, :], ACT.Copy).then_inc(sem("d_pT"), 1)
            else:
                act.activation(pTd[:], src, ACT.Copy).then_inc(sem("d_pT"), 1)

        def d_store(g, t):
            act.wait_ge(*after("d_out", d_step(g, 2 * t + 2)))
            start, step = tile_start(g, t)
            act.dma_start(dil_d[g][start:start + step * (P - 1) + 1:step, :], osb[:, t % 2, :]).then_inc(sem(f"d_store{t % 2}"), 16)

        nd = 0
        for g in range(3):
            for t in range(TT):
                rotT_read(g, t, True)
                nrot += 1
            nd += TT
            act.wait_ge(*after("d_read", nd))
            for t in range(len(value_tiles(g))):
                act.wait_ge(*after("d_done", nd + t + 1))
                act.activation(vd[:, t, :], ps[:, (nd + t) % 2, :], ACT.Copy).then_inc(sem("d_read"), 1)
            nd += len(value_tiles(g)) + TT
            for t in range(TT + 2):
                a = 2 * (t - 1)
                if 0 <= a < 2 * TT:
                    d_exp(g, a)
                    d_pT(g, a)
                    d_exp(g, a + 1)
                if 0 <= a < 2 * TT:
                    d_pT(g, a + 1)
                if t < TT:
                    rotT_read(g, t, False)
                    nrot += 1
                if t >= 2:
                    d_store(g, t - 2)
        for b in range(2):
            act.wait_ge(*after(f"d_store{b}", 16 * 3 * TT // 2))
        phase_end(act, "act")

        phase_start(act, "act", 9)
        for g in range(3):
            act.dma_start(stats[:, g, :, :], dil_d[g].rearrange("(t p) c -> p t c", p=P)[:, :, COLS:]).then_inc(sem("stats_in"), 16)
        for j in range(4):
            act.dma_start(zdT[:, j, :], zd_d[P * j:P * j + P, :]).then_inc(sem("zd_in"), 16)

        def nums_in(t):
            if t >= 2:
                act.wait_ge(*after("weighted", 3 * (t - 1)))
            for g in range(3):
                act.dma_start(nums[:, t % 2, g, :], dil_d[g][P * t:P * t + P, 0:COLS]).then_inc(sem(f"nums_in{t % 2}"), 16)

        nums_in(0)
        nums_in(1)
        for g in range(3):
            act.wait_ge(*after("coef_arg", g + 1))
            act.activation(coef[:, g, :, :], coef[:, g, :, :], ACT.Exp).then_inc(sem("coef_exp"), 1)
        for t in range(2, TT):
            nums_in(t)
        act.wait_ge(*after("dg_done", TT))
        for j in range(4):
            act.dma_start(dd_d[P * j:P * j + P, :], dgT[:, j, :]).then_inc(sem("dg_spill"), 16)
        act.wait_ge(*after("dg_spill", 64))
        phase_end(act, "act")

        phase_start(act, "act", 10)
        act.dma_start(c_bk[:], c_d.rearrange("(t p) c -> p t c", p=P)).then_inc(sem("c_back"), 16)
        act.dma_start(cos_q[:].rearrange("p t f -> p (t f)"), rope_d[:, 0:w_m]).then_inc(sem("rope_back"), 16)
        act.dma_start(sin_q[:].rearrange("p t f -> p (t f)"), rope_d[:, w_m:]).then_inc(sem("rope_back"), 16)
        for u, (n, kind) in enumerate(C_UNITS):
            sl = slice(COLS * n, COLS * n + COLS)
            act.wait_ge(*after("cT", u + 1))
            if kind < 2:
                act.activation(cqh[:, kind, sl], ps[:, u % 4, :], ACT.Copy, scale=gain_q[:, kind:kind + 1]).then_inc(sem("cT_hi"), 1)
            elif kind == 2:
                act.activation(ckh[:, sl], ps[:, u % 4, :], ACT.Copy, scale=gain_kv).then_inc(sem("cT_hi"), 1)
            else:
                for b in range(2):
                    last = act.activation(Kh[HD:MLA_QK, b, sl], ps[HD:MLA_QK, u % 4, :], ACT.Copy)
                last.then_inc(sem("cT_hi"), 1)
        for t in range(TT):
            for half in range(2):
                u = 2 * t + half
                act.wait_ge(*after("qm_done", u + 1))
                if half == 0 and t >= 2:
                    act.wait_ge(*after(f"qm_spill{t % 2}", 16 * (t // 2)))
                act.activation(q_sb[:, t % 2, 4 * half:4 * half + 4, :], ps[:, u % 4, 0:384].rearrange("p (h c) -> p h c", c=MLA_QK),
                               ACT.Copy, scale=float(MLA_QK) ** -0.5).then_inc(sem("qm_read"), 1)
            act.wait_ge(*after("vm_done", t + 1))
            act.activation(Vh[:, t, :], ps[:, 4 + t % 2, :], ACT.Copy).then_inc(sem("vm_hi"), 1)
            if t >= 1:
                act.wait_ge(*after("qm_roped", t))
                act.dma_start(qm_d[P * (t - 1):P * t, :], q_sb[:, (t - 1) % 2].rearrange("p h c -> p (h c)")).then_inc(sem(f"qm_spill{(t - 1) % 2}"), 16)
        act.wait_ge(*after("qm_roped", TT))
        act.dma_start(qm_d[P * (TT - 1):, :], q_sb[:, (TT - 1) % 2].rearrange("p h c -> p (h c)")).then_inc(sem(f"qm_spill{(TT - 1) % 2}"), 16)
        for b in range(2):
            act.wait_ge(*after(f"qm_spill{b}", 16 * TT // 2))
        phase_end(act, "act")

        phase_start(act, "act", 11)
        qm_rows = qm_d.rearrange("(t p) c -> p t c", p=P)

        def head_load(h):
            if h >= 1:
                act.wait_ge(*after("qk_done", 4 * (h - 1) + 2))
            act.dma_start(qm[:], qm_rows[:, :, MLA_QK * h:MLA_QK * h + MLA_QK]).then_inc(sem("qm_back"), 16)

        def head_hi(x):
            h, part = divmod(x, 4)
            sl = slice(COLS * (part % 2), COLS * (part % 2) + COLS)
            act.wait_ge(*after("qk_done", x + 1))
            if h >= 2:
                act.wait_ge(*after("m_scored", TT * (h - 1)))
            dst, n = (Qh, MLA_QK) if part < 2 else (Kh, HD)
            act.activation(dst[0:n, h % 2, sl], ps[0:n, 7, :], ACT.Copy).then_inc(sem("qk_hi"), 1)

        def zm_load(b):
            h, qb = divmod(b, 4)
            if b >= 2:
                act.wait_ge(*after("m_out", b - 1))
            rows = slice(HD * (h % 2), HD * (h % 2) + HD)
            act.dma_start(zm[rows, b % 2, :], zm_d[HD * h:HD * h + HD, 256 * qb:256 * qb + 256]).then_inc(sem(f"zm_in{b % 2}"), 16)

        def am_store(b):
            h, qb = divmod(b, 4)
            act.wait_ge(*after("m_out", b + 1))
            rows = slice(HD * (h % 2), HD * (h % 2) + HD)
            act.dma_start(am_d[HD * h:HD * h + HD, 256 * qb:256 * qb + 256], am[rows, b % 2, :]).then_inc(sem(f"am_out{b % 2}"), 16)

        m_sum = ssq
        head_load(0)
        zm_load(0)
        zm_load(1)
        for part in range(4):
            head_hi(part)
        head_load(1)
        for i in range(n_t + 3):
            if i < n_t:
                act.wait_ge(*after("m_max", i + 1))
                if i >= 2:
                    act.wait_ge(*after("m_T", i - 1))
                act.activation(pm[:, i % 2, :].rearrange("p (b c) -> p b c", b=2), ps[:, 2 * (i % 2):2 * (i % 2) + 2, :], ACT.Exp,
                               bias=rstd[:, i % 8:i % 8 + 1], accum_out=m_sum[:, i % 8:i % 8 + 1]).then_inc(sem("m_exp"), 1)
                h, qt = divmod(i, TT)
                if h + 1 < H1 and qt in (2, 3, 4, 5):
                    head_hi(4 * (h + 1) + qt - 2)
                    if qt == 5 and h + 2 < H1:
                        head_load(h + 2)
                act.wait_ge(*after("m_recip", i + 1))
                act.activation(pm[:, i % 2, :], pm[:, i % 2, :], ACT.Copy, scale=m_sum[:, i % 8:i % 8 + 1]).then_inc(sem("m_normed"), 1)
            if 1 <= i <= n_t:
                k = i - 1
                act.wait_ge(*after("m_T", k + 1))
                if k >= 4:
                    act.wait_ge(*after("m_valued", (k - 4) // 2 + 1))
                act.activation(PTh[:, (k // 2) % 2, :, P * (k % 2):P * (k % 2) + P],
                               ps[:, 4:6, :].rearrange("p b (j c) -> p (b j) c", c=P), ACT.Copy).then_inc(sem("m_hi"), 1)
            if i >= 4 and i % 2 == 0:
                b = i // 2 - 2
                am_store(b)
                if b + 2 < 4 * H1:
                    zm_load(b + 2)
        for b in range(2):
            act.wait_ge(*after(f"am_out{b}", 16 * 2 * H1))
        phase_end(act, "act")

        phase_start(act, "act", 12)

        def mixers_in(n):
            if n:
                act.wait_ge(*after("mixers_lo", 8))
            for o, src in enumerate((am_d, dd_d)):
                act.dma_start(raw[:, 4 * o:4 * o + 4, :], src.rearrange("(k p) s -> p k s", p=P)[:, :, COLS * n:COLS * n + COLS]).then_inc(sem("mixers_in"), 16)

        def gates_in(u):
            n, m_ = divmod(u, KT)
            if u >= 2:
                act.wait_ge(*after("y2_read", u - 1))
            for o in range(2):
                r0 = D * o + P * m_
                act.dma_start(gg[:, u % 2, o, :], g_d[r0:r0 + P, COLS * n:COLS * n + COLS]).then_inc(sem(f"gates_in{u % 2}"), 16)

        mixers_in(0)
        gates_in(0)
        gates_in(1)
        for n in range(HALF):
            act.wait_ge(*after("mixers_in", 32 * (n + 1)))
            if n:
                act.wait_ge(*after("y2_done", KT))
            for k in range(8):
                act.activation(oh[:, k, :], raw[:, k, :], ACT.Copy).then_inc(sem("mixers_hi"), 1)
            if n == 0:
                mixers_in(1)
            for m_ in range(KT):
                u = KT * n + m_
                act.wait_ge(*after("merged", u + 1))
                act.activation(Mh[:, m_, COLS * n:COLS * n + COLS], yg[:, 0, :], ACT.Copy).then_inc(sem("merged_hi"), 1)
                if u + 2 < 2 * KT:
                    gates_in(u + 2)
        phase_end(act, "act")

        phase_start(act, "act", 13)
        act.dma_start(gfin[:], final_norm_g.rearrange("(a d) -> a d", a=1).to_broadcast([P, D])).then_inc(sem("gfin"), 16)
        out_tok = out[0].rearrange("(t p) d -> t p d", p=P)

        def x1_back(t):
            if t >= 2:
                act.wait_ge(*after("o_read", t - 1))
            act.dma_start(xr2[:, t % 2, :], x1_tok[t]).then_inc(sem(f"x1_back{t % 2}"), 16)

        def out_store(t):
            act.wait_ge(*after("final", t + 1))
            act.dma_start(out_tok[t], fin[:, t % 2, :]).then_inc(sem(f"out_stored{t % 2}"), 16)

        x1_back(0)
        x1_back(1)
        for t in range(TT):
            act.wait_ge(*after("o_read", t + 1))
            if t >= 1:
                act.wait_ge(*after("o_sq", t))
            act.activation(osq[:], oo[:], ACT.Square, accum_out=ssq[:, t:t + 1]).then_inc(sem("o_sq"), 1)
            act.wait_ge(*after("o_sq", t + 1))
            act.activation(rstd[:, t:t + 1], ssq[:, t:t + 1], ACT.Sqrt, scale=1.0 / D, bias=EPS_C).then_inc(sem("o_root"), 1)
            if t >= 1:
                out_store(t - 1)
            if t + 2 < TT:
                x1_back(t + 2)
        out_store(TT - 1)
        for b in range(2):
            act.wait_ge(*after(f"out_stored{b}", 16 * TT // 2))

    @block.vector
    def _(dve):
        turns_taken = [0]

        def in_turn(ins):
            ins.then_inc(sem("vector_step"), 1)
            turns_taken[0] += 1
            dve.wait_ge(sem("vector_step"), turns_taken[0])

        nc.vector.memset(EPS_C, EPS).then_inc(sem("zeroed"), 1)
        dve.wait_ge(*after("const", 16 * 8))
        nc.vector.tensor_scalar(sinks_n, sinks_p, -1.0, None, ALU.mult).then_inc(sem("sink_c"), 1)

        def inverse_root(tag, n=1):
            dve.wait_ge(*after(f"{tag}_root", n))

        inverse_root("x")
        nc.vector.reciprocal(rstd, rstd).then_inc(sem("x_rstd"), 1)
        dve.wait_ge(*after("x_rstd", 1))
        for t in range(TT):
            nc.vector.tensor_scalar(xt[:, t, :], xt[:, t, :], rstd[:, t:t + 1], None, ALU.mult).then_inc(sem("x_scaled"), 1)
        for n in range(HALF):
            for k in range(KT):
                u = n * KT + k
                sl = slice(COLS * n, COLS * n + COLS)
                dve.wait_ge(*after("x_hi", u + 1))
                nc.vector.scalar_tensor_tensor(hTl[:, k, sl], ps[:, u % 4, :], gain_pre[:, k:k + 1],
                                               hTh[:, k, sl].bitcast(F32), ALU.mult, ALU.subtract).then_inc(sem("x_evac"), 1)
        phase_end(dve, "dve")

        phase_start(dve, "dve", 1)
        for buf in (uT[:, 0, 0:PAD], uT[:, 1, 0:PAD], sA[:, 0:PAD]):
            nc.vector.memset(buf, 0.0)
        nc.vector.memset(sB[:, 0:PAD], 0.0).then_inc(sem("u_pad"), 1)
        dve.wait_ge(*after("u_pad", 1))
        dve.wait_ge(*after("pool_c", 80))
        def pool_mul(u):
            g, n = divmod(u, 2)
            sl = slice(COLS * n, COLS * n + COLS)
            dve.wait_ge(*after("mix_done", u + 1))
            nc.vector.tensor_scalar(pmT[:, g, sl], ps[:, 4 + u % 2, :], pscale[:, g:g + 1], None,
                                    ALU.mult).then_inc(sem("mix_evac"), 1)

        def pool_finish(g):
            pool_mul(2 * g)
            pool_mul(2 * g + 1)
            for n in range(HALF):
                u = 2 * g + n
                sl = slice(COLS * n, COLS * n + COLS)
                dve.wait_ge(*after("pg_evac", u + 1))
                dve.wait_ge(*after("mix_evac", u + 1))
                nc.vector.tensor_tensor(pmT[:, g, sl], pmT[:, g, sl], sg1[:, u % 2, :], ALU.mult).then_inc(sem("pg_mul"), 1)

        for g, w in enumerate(POOL_W):
            dve.wait_ge(*after("u_evac", 2 * g + 2))
            src, d, bufs = uT[:, g % 2, :], 1, [sA, sB]
            while d < w:
                dst = bufs[0][:]
                in_turn(nc.vector.tensor_tensor(dst[:, PAD:], src[:, PAD:], src[:, PAD - d:PAD + S - d], ALU.add))
                src, d = dst, 2 * d
                bufs.reverse()
            if g >= 2:
                dve.wait_ge(*after("mix_done", 2 * (g - 1)))
            in_turn(nc.vector.scalar_tensor_tensor(pooled[:, g % 2, :], src[:, PAD:], 1.0 / w, uT[:, g % 2, PAD:],
                                                ALU.mult, ALU.subtract))
            in_turn(nc.vector.tensor_tensor(edge_t[:], src[:, PAD:2 * PAD], edge[:, g, :], ALU.mult))
            in_turn(nc.vector.tensor_tensor(pooled[:, g % 2, 0:PAD], edge_t[:], uT[:, g % 2, PAD:2 * PAD], ALU.subtract))
            nc.vector.memset(edge_t[:, 0:1], 0.0).then_inc(sem("pooled"), 1)
            if g >= 1:
                pool_finish(g - 1)
        pool_finish(3)
        phase_end(dve, "dve")

        phase_start(dve, "dve", 2)
        dve.wait_ge(*after("swa_c", 16))
        steps = TT * HH
        def softmax_in(i):
            t, hh = divmod(i, HH)
            hs = slice(G * hh, G * hh + G)
            nk = P if t == 0 else 2 * P
            sc = ps[:, 0:2, :].rearrange("p b (j k) -> p (b j) k", j=2)[:, :, 0:nk]
            dst = pr[:, i % 2, :, 0:nk]
            dve.wait_ge(*after("swa_scored", i + 1))
            if i >= 2:
                dve.wait_ge(*after("swa_T", i - 1))
            nc.vector.tensor_tensor(dst, sc, swa_b[:, hs, 2 * P - nk:2 * P], ALU.add).then_inc(sem("swa_masked"), 1)
            dve.wait_ge(*after("swa_masked", i + 1))
            if t >= 1:
                dve.wait_ge(*after("swa_out", 2 * (t - 1) + hh + 1))
            in_turn(nc.vector.tensor_reduce(st[:, 0, hs], dst, AX_X, ALU.max, negate=True))
            in_turn(nc.vector.tensor_tensor(st[:, 0, hs], st[:, 0, hs], sinks_n[:, hs], ALU.min))
            nc.vector.tensor_tensor(st[:, 3, hs], st[:, 0, hs], sinks_p[:, hs], ALU.add).then_inc(sem("swa_max"), 1)

        def normalise(i):
            t, hh = divmod(i, HH)
            hs = slice(G * hh, G * hh + G)
            dve.wait_ge(*after("swa_valued", i + 1))
            dve.wait_ge(*after("swa_sink", i + 1))
            in_turn(nc.vector.tensor_tensor(st[:, 1, hs], st[:, 1, hs], st[:, 2, hs], ALU.add))
            in_turn(nc.vector.reciprocal(st[:, 1, hs], st[:, 1, hs]))
            if t >= 1:
                dve.wait_ge(*after("swa_backT", t))
            nc.vector.tensor_tensor(ao[:, hs, :], ps[:, 4 + i % 2, 0:256].rearrange("p (h d) -> p h d", d=HD),
                                    st[:, 1, hs].unsqueeze(2).to_broadcast([P, G, HD]), ALU.mult).then_inc(sem("swa_out"), 1)

        def back(t):
            dve.wait_ge(*after("swa_backT", t + 1))
            nc.vector.tensor_copy(aT[:, :, P * t:P * t + P], ps[:, 6, :].rearrange("p (j c) -> p j c", c=P)).then_inc(sem("swa_aT"), 1)

        for i in range(steps + 3):
            if i < steps:
                if i >= 2:
                    normalise(i - 2)
                softmax_in(i)
            elif i - 2 < steps:
                normalise(i - 2)
            if i >= 3 and (i - 3) % HH == HH - 1:
                back((i - 3) // HH)
        phase_end(dve, "dve")

        phase_start(dve, "dve", 3)
        for u in range(8):
            m, n = divmod(u, 2)
            sl = slice(COLS * n, COLS * n + COLS)
            dve.wait_ge(*after("ag_evac", u + 1))
            nc.vector.tensor_tensor(aT[:, m, sl], aT[:, m, sl], sgA[:, u % 2, :], ALU.mult).then_inc(sem("ag_mul"), 1)
        phase_end(dve, "dve")

        phase_start(dve, "dve", 4)
        for k in range(KT):
            src = pmR[:, k, :] if k < 4 else aT[:, k - 4, :]
            dve.wait_ge(*after("mixT_hi", k + 1))
            nc.vector.tensor_tensor(mTl[:, k, :], src, mTh[:, k, :].bitcast(F32), ALU.subtract).then_inc(sem("mixT_split"), 1)
        dve.wait_ge(*after("mixT_split", KT))
        dve.wait_ge(*after("gpost", 16))
        for t in range(TT):
            b = 2 * (t % 2)
            dve.wait_ge(*after("y_root", t + 1))
            nc.vector.reciprocal(rstd[:, t:t + 1], rstd[:, t:t + 1]).then_inc(sem("y_rstd"), 1)
            dve.wait_ge(*after("y_rstd", t + 1))
            nc.vector.scalar_tensor_tensor(yn[:].rearrange("p (b c) -> p b c", b=2), ps[:, b:b + 2, :], rstd[:, t:t + 1],
                                           gpost[:].rearrange("p (b c) -> p b c", b=2), ALU.mult, ALU.mult).then_inc(sem("y_read"), 1)
            dve.wait_ge(*after("y_read", t + 1))
            dve.wait_ge(*after(f"x_back{t % 2}", 16 * (t // 2 + 1)))
            if t >= 2:
                dve.wait_ge(*after(f"x1_out{t % 2}", 16 * (t // 2)))
            nc.vector.tensor_tensor(x1[:, t % 2, :], yn[:], xr[:, t % 2, :], ALU.add).then_inc(sem("x1_made"), 1)
        phase_end(dve, "dve")


        phase_start(dve, "dve", 5)
        inverse_root("x1")
        nc.vector.reciprocal(rstd, rstd).then_inc(sem("x1_rstd"), 1)
        dve.wait_ge(*after("x1_rstd", 1))
        for t in range(TT):
            nc.vector.tensor_scalar(xt2[:, t, :], xt2[:, t, :], rstd[:, t:t + 1], None, ALU.mult).then_inc(sem("x1_scaled"), 1)
        for n in range(HALF):
            for k in range(KT):
                u = n * KT + k
                sl = slice(COLS * n, COLS * n + COLS)
                dve.wait_ge(*after("x1_hi", u + 1))
                nc.vector.scalar_tensor_tensor(h2l[:, k, sl], ps[:, u % 4, :], gain_2[:, k:k + 1],
                                               h2h[:, k, sl].bitcast(F32), ALU.mult, ALU.subtract).then_inc(sem("x1_evac"), 1)
        dve.wait_ge(*after("pos_in", 16 * 25))
        in_turn(nc.vector.tensor_copy(posf[:], posi[:]))
        for i in range(3 * TT):
            in_turn(nc.vector.tensor_scalar(ang[:, i, :], freq[:, 0:FREQS], posf[:, i // TT, i % TT:i % TT + 1], None, ALU.mult))
        for t in range(TT):
            in_turn(nc.vector.tensor_scalar(ang[:, 24 + t // 2, 16 * (t % 2):16 * (t % 2) + 16], freq[:, FREQS:],
                                         posf[:, 0, t:t + 1], None, ALU.mult))
        for i, quarter in enumerate((0.0, 0.25)):
            in_turn(nc.vector.tensor_scalar(turn[:], ang[:], 1.0 / TWO_PI, quarter, ALU.mult, ALU.add))
            in_turn(nc.vector.tensor_scalar(turn[:], turn[:], ROUND, None, ALU.add))
            in_turn(nc.vector.tensor_scalar(turn[:], turn[:], ROUND, None, ALU.subtract))
            if i:
                dve.wait_ge(*after("tables", 2))
            src = ang
            for part in TWO_PI_PARTS:
                in_turn(nc.vector.scalar_tensor_tensor(red[:], turn[:], -part, src[:], ALU.mult, ALU.add))
                src = red
            if i:
                in_turn(nc.vector.tensor_scalar(red[:], red[:], TWO_PI / 4, None, ALU.add))
            nc.vector.tensor_scalar(red[:], red[:], PI_IN, -PI_IN, ALU.min, ALU.max).then_inc(sem("angles"), 1)
        phase_end(dve, "dve")

        phase_start(dve, "dve", 6)
        dve.wait_ge(*after("c_evac", TT))
        r0, hw = C_Q + C_KV, MLA_R // 2
        lo_, hi_ = c_sb[:, :, r0:r0 + hw], c_sb[:, :, r0 + hw:r0 + 2 * hw]
        for i, (a, b) in enumerate(((lo_, cos_m), (hi_, sin_m), (hi_, cos_m), (lo_, sin_m))):
            in_turn(nc.vector.tensor_tensor(c_t[:, i], a, b[:], ALU.mult))
        in_turn(nc.vector.tensor_tensor(lo_, c_t[:, 0], c_t[:, 1], ALU.subtract))
        nc.vector.tensor_tensor(hi_, c_t[:, 2], c_t[:, 3], ALU.add).then_inc(sem("c_roped"), 1)
        dve.wait_ge(*after("c_root", 2))
        in_turn(nc.vector.reciprocal(c_ss[:], c_ss[:]))
        for t in range(TT):
            for i, (c0, w) in enumerate(((0, C_Q), (C_Q, C_KV))):
                nc.vector.tensor_scalar(c_sb[:, t, c0:c0 + w], c_sb[:, t, c0:c0 + w], c_ss[:, i, t:t + 1], None,
                                        ALU.mult).then_inc(sem("c_scaled"), 1)
        phase_end(dve, "dve")

        phase_start(dve, "dve", 7)
        phase_end(dve, "dve")

        phase_start(dve, "dve", 8)
        dve.wait_ge(*after("masks_in", 16))
        nr = [0, 0]

        def rotate(g, t):
            u = nr[0]
            dve.wait_ge(*after("d_done", u + 1))
            src = ps[:, u % 2, :].rearrange("p (h f) -> p h f", f=FREQS)
            cos, sin = (x_[:, g, t:t + 1, :].to_broadcast([P, 2 * H1, FREQS]) for x_ in (cos_d, sin_d))
            nc.vector.tensor_tensor(rc[:].rearrange("p (h f) -> p h f", f=FREQS), src, cos, ALU.mult).then_inc(sem("rope_cos"), 1)
            nc.vector.tensor_tensor(rs[:].rearrange("p (h f) -> p h f", f=FREQS), src, sin, ALU.mult).then_inc(sem("d_read"), 1)
            dve.wait_ge(*after("rope_cos", nr[1] + 1))
            dve.wait_ge(*after("d_read", u + 1))
            if nr[1] >= 1:
                dve.wait_ge(*after("rotT", nr[1]))
            c4, s4_, o4 = (x_[:].rearrange("p (h a f) -> p h a f", a=2, f=FREQS) for x_ in (rc, rs, rr))
            nc.vector.tensor_tensor(o4[:, :, 0, :], c4[:, :, 0, :], s4_[:, :, 1, :], ALU.subtract).then_inc(sem("rope_half"), 1)
            nc.vector.tensor_tensor(o4[:, :, 1, :], c4[:, :, 1, :], s4_[:, :, 0, :], ALU.add).then_inc(sem("rotated"), 1)
            dve.wait_ge(*after("rotated", nr[1] + 1))
            nr[0] += 1
            nr[1] += 1

        def d_soft(g, i):
            n = d_step(g, i)
            t, hh = divmod(i, HH)
            _, nk, mc, _ = window(g, t)
            dve.wait_ge(*after("d_scored", n + 1))
            if n >= 2:
                dve.wait_ge(*after("d_T", n - 1))
            dst = prd[:, i % 2, :, 0:nk]
            for b in range(2):
                sc = ps[:, 3 + b, :].rearrange("p (j k) -> p j k", j=2)[:, :, 0:nk]
                mask = masks[:, mc:mc + nk].unsqueeze(1).to_broadcast([P, 2, nk])
                last = nc.vector.tensor_tensor(dst[:, b::2, :], sc, mask, ALU.add)
            last.then_inc(sem("d_masked"), 1)
            dve.wait_ge(*after("d_masked", n + 1))
            if hh == 0 and (g or t >= 2):
                dve.wait_ge(*after(f"d_store{t % 2}", 16 * ((TT * g + t) // 2)))
            c0 = COLS + G * hh
            nc.vector.tensor_reduce(osb[:, t % 2, c0:c0 + G], dst, AX_X, ALU.max, negate=True).then_inc(sem("d_max"), 1)

        def d_out(g, i):
            n = d_step(g, i)
            t, hh = divmod(i, HH)
            dve.wait_ge(*after("d_valued", n + 1))
            nc.vector.tensor_copy(osb[:, t % 2, 256 * hh:256 * hh + 256], ps[:, 7, 0:256]).then_inc(sem("d_out"), 1)

        for g in range(3):
            for t in range(TT):
                rotate(g, t)
            nv_ = len(value_tiles(g))
            nr[0] += nv_
            dve.wait_ge(*after("d_read", nr[0]))
            for t in range(TT + 2):
                a = 2 * (t - 1)
                if 0 <= a < 2 * TT:
                    d_soft(g, a)
                if 0 <= a - 1 < 2 * TT:
                    d_out(g, a - 1)
                if 0 <= a < 2 * TT:
                    d_soft(g, a + 1)
                if t < TT:
                    rotate(g, t)
                if 0 <= a < 2 * TT:
                    d_out(g, a)
        phase_end(dve, "dve")

        phase_start(dve, "dve", 9)
        dve.wait_ge(*after("stats_in", 48))
        nm = [stats[:, g, :, 0:H1] for g in range(3)]
        den = [stats[:, g, :, H1:] for g in range(3)]
        in_turn(nc.vector.tensor_tensor(joint[:], nm[0], nm[1], ALU.min))
        in_turn(nc.vector.tensor_tensor(joint[:], joint[:], nm[2], ALU.min))
        for g in range(3):
            nc.vector.tensor_tensor(coef[:, g], joint[:], nm[g], ALU.subtract).then_inc(sem("coef_arg"), 1)
        dve.wait_ge(*after("coef_exp", 3))
        for g in range(3):
            in_turn(nc.vector.tensor_tensor(den[g], den[g], coef[:, g], ALU.mult))
        in_turn(nc.vector.tensor_tensor(dsum[:], den[0], den[1], ALU.add))
        in_turn(nc.vector.tensor_tensor(dsum[:], dsum[:], den[2], ALU.add))
        in_turn(nc.vector.reciprocal(dsum[:], dsum[:]))
        for g in range(3):
            in_turn(nc.vector.tensor_tensor(coef[:, g], coef[:, g], dsum[:], ALU.mult))
        dve.wait_ge(*after("zd_in", 64))

        def gate(t):
            dve.wait_ge(*after("jointT", t + 1))
            nc.vector.tensor_tensor(dgT[:, :, P * t:P * t + P], ps[:, t % 2, :].rearrange("p (j c) -> p j c", c=P),
                                    zdT[:, :, P * t:P * t + P], ALU.mult).then_inc(sem("dg_done"), 1)

        for t in range(TT):
            dve.wait_ge(*after(f"nums_in{t % 2}", 48 * (t // 2 + 1)))
            if t >= 1:
                dve.wait_ge(*after("jointT", t))
            for g in range(3):
                nc.vector.tensor_tensor(wsum[:, g, :].rearrange("p (h d) -> p h d", d=HD),
                                        nums[:, t % 2, g, :].rearrange("p (h d) -> p h d", d=HD),
                                        coef[:, g, t, :].unsqueeze(2).to_broadcast([P, H1, HD]), ALU.mult).then_inc(sem("weighted"), 1)
            dve.wait_ge(*after("weighted", 3 * t + 3))
            in_turn(nc.vector.tensor_tensor(wsum[:, 0, :], wsum[:, 0, :], wsum[:, 1, :], ALU.add))
            nc.vector.tensor_tensor(wsum[:, 0, :], wsum[:, 0, :], wsum[:, 2, :], ALU.add).then_inc(sem("joint"), 1)
            dve.wait_ge(*after("joint", t + 1))
            gate(t)
        phase_end(dve, "dve")

        phase_start(dve, "dve", 10)
        for u, (n, kind) in enumerate(C_UNITS):
            sl = slice(COLS * n, COLS * n + COLS)
            dve.wait_ge(*after("cT_hi", u + 1))
            if kind < 2:
                last = nc.vector.scalar_tensor_tensor(cql[:, kind, sl], ps[:, u % 4, :], gain_q[:, kind:kind + 1],
                                                      cqh[:, kind, sl].bitcast(F32), ALU.mult, ALU.subtract)
            elif kind == 2:
                last = nc.vector.scalar_tensor_tensor(ckl[:, sl], ps[:, u % 4, :], gain_kv, ckh[:, sl].bitcast(F32),
                                                      ALU.mult, ALU.subtract)
            else:
                for b in range(2):
                    last = nc.vector.tensor_tensor(Kl[HD:MLA_QK, b, sl], ps[HD:MLA_QK, u % 4, :],
                                                   Kh[HD:MLA_QK, b, sl].bitcast(F32), ALU.subtract)
            last.then_inc(sem("cT_lo"), 1)
        dve.wait_ge(*after("rope_back", 32))
        for t in range(TT):
            dve.wait_ge(*after("qm_read", 2 * t + 2))
            q_lo, q_hi = q_sb[:, t % 2, :, HD:HD + hw], q_sb[:, t % 2, :, HD + hw:]
            cos, sin = (x_[:, t:t + 1, :].to_broadcast([P, H1, hw]) for x_ in (cos_q, sin_q))
            for i, (a, b) in enumerate(((q_lo, cos), (q_hi, sin), (q_hi, cos), (q_lo, sin))):
                in_turn(nc.vector.tensor_tensor(q_t[:, i], a, b, ALU.mult))
            in_turn(nc.vector.tensor_tensor(q_lo, q_t[:, 0], q_t[:, 1], ALU.subtract))
            nc.vector.tensor_tensor(q_hi, q_t[:, 2], q_t[:, 3], ALU.add).then_inc(sem("qm_roped"), 1)
            dve.wait_ge(*after("vm_hi", t + 1))
            nc.vector.tensor_tensor(Vl[:, t, :], ps[:, 4 + t % 2, :], Vh[:, t, :].bitcast(F32), ALU.subtract).then_inc(sem("vm_lo"), 1)
        phase_end(dve, "dve")

        phase_start(dve, "dve", 11)

        def head_lo(x_):
            h, part = divmod(x_, 4)
            sl = slice(COLS * (part % 2), COLS * (part % 2) + COLS)
            dve.wait_ge(*after("qk_hi", x_ + 1))
            dst, hi, n = (Ql, Qh, MLA_QK) if part < 2 else (Kl, Kh, HD)
            nc.vector.tensor_tensor(dst[0:n, h % 2, sl], ps[0:n, 7, :], hi[0:n, h % 2, sl].bitcast(F32),
                                    ALU.subtract).then_inc(sem("qk_lo"), 1)

        def m_out(b):
            h, qb = divmod(b, 4)
            rows = slice(HD * (h % 2), HD * (h % 2) + HD)
            dve.wait_ge(*after("m_valued", b + 1))
            dve.wait_ge(*after(f"zm_in{b % 2}", 16 * (b // 2 + 1)))
            if b >= 2:
                dve.wait_ge(*after(f"am_out{b % 2}", 16 * (b // 2)))
            nc.vector.tensor_tensor(am[rows, b % 2, :], ps[rows, 6, 0:256], zm[rows, b % 2, :], ALU.mult).then_inc(sem("m_out"), 1)

        for x_ in range(4):
            head_lo(x_)
        for i in range(n_t + 3):
            if i < n_t:
                dve.wait_ge(*after("m_scored", i + 1))
                if i >= 8:
                    dve.wait_ge(*after("m_exp", i - 7))
                nc.vector.tensor_reduce(rstd[:, i % 8:i % 8 + 1], ps[:, 2 * (i % 2):2 * (i % 2) + 2, :].rearrange("p b c -> p (b c)"),
                                        AX_X, ALU.max, negate=True).then_inc(sem("m_max"), 1)
                h, qt = divmod(i, TT)
                if h + 1 < H1 and qt in (2, 3, 4, 5):
                    head_lo(4 * (h + 1) + qt - 2)
                dve.wait_ge(*after("m_exp", i + 1))
                nc.vector.reciprocal(ssq[:, i % 8:i % 8 + 1], ssq[:, i % 8:i % 8 + 1]).then_inc(sem("m_recip"), 1)
            if 1 <= i <= n_t:
                k = i - 1
                dve.wait_ge(*after("m_hi", k + 1))
                dst = (slice(None), (k // 2) % 2, slice(None), slice(P * (k % 2), P * (k % 2) + P))
                nc.vector.tensor_tensor(PTl[dst], ps[:, 4:6, :].rearrange("p b (j c) -> p (b j) c", c=P),
                                        PTh[dst].bitcast(F32), ALU.subtract).then_inc(sem("m_lo"), 1)
            if i >= 3 and i % 2 == 1 and (i - 3) // 2 < 4 * H1:
                m_out((i - 3) // 2)
        phase_end(dve, "dve")

        phase_start(dve, "dve", 12)
        for n in range(HALF):
            for k in range(8):
                dve.wait_ge(*after("mixers_hi", 8 * n + k + 1))
                nc.vector.tensor_tensor(ol[:, k, :], raw[:, k, :], oh[:, k, :].bitcast(F32), ALU.subtract).then_inc(sem("mixers_lo"), 1)
            for m_ in range(KT):
                u = KT * n + m_
                sl = slice(COLS * n, COLS * n + COLS)
                dve.wait_ge(*after("y2_done", u + 1))
                dve.wait_ge(*after(f"gates_in{u % 2}", 32 * (u // 2 + 1)))
                if u >= 1:
                    dve.wait_ge(*after("merged_lo", u))
                nc.vector.tensor_tensor(yg[:, 0, :], ps[:, 2 * (u % 2), :], gg[:, u % 2, 0, :], ALU.mult).then_inc(sem("y2_first"), 1)
                nc.vector.tensor_tensor(yg[:, 1, :], ps[:, 2 * (u % 2) + 1, :], gg[:, u % 2, 1, :], ALU.mult).then_inc(sem("y2_read"), 1)
                dve.wait_ge(*after("y2_first", u + 1))
                dve.wait_ge(*after("y2_read", u + 1))
                nc.vector.tensor_tensor(yg[:, 0, :], yg[:, 0, :], yg[:, 1, :], ALU.add).then_inc(sem("merged"), 1)
                dve.wait_ge(*after("merged_hi", u + 1))
                nc.vector.tensor_tensor(Ml[:, m_, sl], yg[:, 0, :], Mh[:, m_, sl].bitcast(F32), ALU.subtract).then_inc(sem("merged_lo"), 1)
        phase_end(dve, "dve")

        phase_start(dve, "dve", 13)
        dve.wait_ge(*after("gfin", 16))
        for t in range(TT):
            b = 2 * (t % 2)
            dve.wait_ge(*after("o_done", t + 1))
            dve.wait_ge(*after(f"x1_back{t % 2}", 16 * (t // 2 + 1)))
            if t >= 1:
                dve.wait_ge(*after("final", t))
                dve.wait_ge(*after("o_sq", t))
            nc.vector.tensor_tensor(oo[:].rearrange("p (b c) -> p b c", b=2), ps[:, b:b + 2, :],
                                    xr2[:, t % 2, :].rearrange("p (b c) -> p b c", b=2), ALU.add).then_inc(sem("o_read"), 1)
            dve.wait_ge(*after("o_root", t + 1))
            nc.vector.reciprocal(rstd[:, t:t + 1], rstd[:, t:t + 1]).then_inc(sem("o_rstd"), 1)
            dve.wait_ge(*after("o_rstd", t + 1))
            if t >= 2:
                dve.wait_ge(*after(f"out_stored{t % 2}", 16 * (t // 2)))
            nc.vector.scalar_tensor_tensor(fin[:, t % 2, :], oo[:], rstd[:, t:t + 1], gfin[:], ALU.mult, ALU.mult).then_inc(sem("final"), 1)

    ctx.close()


_INS = ["x", "w_in", "pool_w", "pool_scale", "attn_sinks", "w_out", "norm_pre", "norm_post", "positions_2",
        "attn_norm_g_2", "w_in_2", "b_gate_2", "mla_q_norm_g_2", "mla_kv_norm_g_2", "w_uq_2", "w_ukv_2",
        "w_o_mla_2", "w_o_dil_2", "w_out_2", "final_norm_g_2"]


def kernel(**inputs):
    import concourse.bacc as bacc
    from concourse.bass_utils import run_bass_kernel_spmd

    nc = bacc.Bacc("TRN2", target_bir_lowering=False, num_devices=1)
    arrays, args = {}, []
    for name in _INS:
        arrays[f"in_{name}"] = np.ascontiguousarray(inputs[name])
    arrays.update(constants())
    for name, a in arrays.items():
        args.append(nc.dram_tensor(name, a.shape, mybir.dt.from_np(a.dtype), kind="ExternalInput").ap())
    out = nc.dram_tensor("out_0", (1, S, D), F32, kind="ExternalOutput").ap()
    hybrid_blocks_kernel(nc, *args, out)
    r = run_bass_kernel_spmd(nc, [arrays], core_ids=[0])
    return r.results[0]["out_0"]
```

```python
from contextlib import ExitStack

import concourse.bass as bass
import numpy as np
from concourse import mybir

F32 = mybir.dt.float32
F32R = mybir.dt.float32r
I32 = mybir.dt.int32
ALU = mybir.AluOpType
ACT = mybir.ActivationFunctionType
AX_X = mybir.AxisListType.X

P = 128
S = 1024
D = 1024
KT = D // P
TT = S // P
COLS = 512
HALF = S // COLS
EPS = 1e-6
NEG = -1e30
H1 = 8
HD = 64
POOL_W = (2, 4, 8, 16)
PAD = 16
G = 4
HH = H1 // G
MASK_W = 3 * P
FREQS = 32
MLA_R = 32
MLA_QK = 96
C_Q, C_KV = 256, 128
C_W = C_Q + C_KV + MLA_R
DIL_QKV = 1536
DILATIONS = (1, 4, 16)
STAT = 2 * H1
CHUNK_K = 2
STAGE = 2
TWO_PI = 6.283185307179586
TWO_PI_PARTS = (6.28125, 0.0019350051879882812, 3.019915981956752e-07)
PI_IN = 3.1415925
ROUND = 12582912.0


def constants():
    q = np.arange(P)[:, None]
    c = np.arange(2 * P)[None, :]
    dist = (q + P - c).astype(np.float32)
    slopes = np.exp2(-8.0 * np.arange(1, H1 + 1, dtype=np.float32) / H1).astype(np.float32)
    valid = (dist >= 0) & (dist < P)
    swa = np.where(valid[:, None, :], -slopes[None, :, None] * dist[:, None, :], np.float32(NEG))
    j = np.arange(MASK_W)[None, :]
    band = np.where(np.abs(j - P - q) <= HD, 0.0, NEG)
    k = np.arange(P)[None, :]
    pairs = np.where(q % 2 == k % 2, 0.0, NEG)
    n = np.arange(PAD)
    inv = np.stack([1.0 / np.minimum(n + 1, w) for w in POOL_W])
    f32 = 10000.0 ** (-np.arange(0, HD, 2, dtype=np.float32) / np.float32(HD))
    f16 = 10000.0 ** (-np.arange(0, MLA_R, 2, dtype=np.float32) / np.float32(MLA_R))
    return {
        "c_swa": np.ascontiguousarray(swa.reshape(P, -1), np.float32),
        "c_mask": np.ascontiguousarray(np.concatenate([band, pairs], 1), np.float32),
        "c_inv": np.ascontiguousarray(inv, np.float32),
        "c_freq": np.ascontiguousarray(np.concatenate([f32, f16])[None, :], np.float32),
        "c_ident": np.eye(P, dtype=np.float32),
    }


def hybrid_blocks_kernel(nc, x, w_in, pool_w, pool_scale, attn_sinks, w_out, norm_pre, norm_post,
                         positions, attn_norm_g, w_in_2, b_gate, q_norm_g, kv_norm_g, w_uq, w_ukv,
                         w_o_mla, w_o_dil, w_out_2, final_norm_g,
                         c_swa, c_mask, c_inv, c_freq, c_ident, out, upto=99):
    ctx = ExitStack()
    sems = {}
    shared = {
        "product_done": (("u_done", 8), ("pg_done", 8), ("qkv_done", 12), ("ag_done", 16), ("y_done", TT),
                         ("c_done", TT), ("g_done", 48), ("qm_done", 2 * TT), ("y2_done", 4 * KT), ("o_done", 2 * TT)),
        "product_copied": (("u_evac", 8), ("pg_evac", 8), ("qkv_evac", 12), ("ag_evac", 16), ("c_evac", TT), ("g_evac", 48)),
        "product_used": (("pg_mul", 8), ("ag_mul", 16), ("y_read", TT), ("qm_read", 2 * TT), ("y2_read", 4 * KT), ("o_read", 2 * TT)),
        "input_transposed": (("x_T", 16), ("x1_T", 16), ("cT", 8)),
        "input_high": (("x_hi", 16), ("x1_hi", 16), ("cT_hi", 8)),
        "input_split": (("x_evac", 16), ("x1_evac", 16), ("cT_lo", 8)),
        "rows_scaled": (("x_scaled", TT), ("x1_scaled", TT), ("c_scaled", 2 * TT)),
        "squared": (("x_sq", TT), ("y_sq", TT), ("c_sqd", 2 * TT), ("o_sq", 2 * TT)),
        "rooted": (("x_root", 1), ("y_root", TT), ("c_root", 2), ("o_root", TT)),
        "inverted": (("x_rstd", 1), ("y_rstd", TT), ("o_rstd", TT)),
        "scored": (("swa_scored", 16), ("d_scored", 48)),
        "masked": (("swa_masked", 16), ("d_masked", 48)),
        "row_max": (("swa_max", 16), ("d_max", 48)),
        "exponentials": (("swa_exp", 64), ("d_exp", 192)),
        "probs_transposed": (("swa_T", 16), ("d_T", 48)),
        "probs_copied": (("swa_pT", 16), ("d_pT", 48)),
        "values_summed": (("swa_valued", 16), ("d_valued", 48)),
        "values_copied": (("swa_out", 16), ("d_out", 48)),
        "high_part": (("mixT_hi", KT), ("vm_hi", TT), ("mixers_hi", 8)),
        "low_part": (("mixT_split", KT), ("vm_lo", TT), ("mixers_lo", 8)),
        "pool_in_out": (("pool_c", 80), ("pool_spill", 64), ("pool_back", 64)),
    }
    for t in range(TT):
        shared[f"rows_in{t}"] = ((f"x_in{t}", 16),)
    for b in range(2):
        shared[f"x_tile_in{b}"] = ((f"x_back{b}", 64), (f"x1_back{b}", 64))
        shared[f"tile_out{b}"] = ((f"x1_out{b}", 64), (f"d_store{b}", 192), (f"qm_spill{b}", 64))
    alias = {}
    for own, users in shared.items():
        base = 0
        for name, count in users:
            alias[name] = own, base
            base += count

    def sem(name):
        name = alias.get(name, (name, 0))[0]
        if name not in sems:
            sems[name] = ctx.enter_context(nc.semaphore(name))
        return sems[name]

    def after(name, count):
        return sem(name), alias.get(name, (name, 0))[1] + count

    w1 = w_in[0].rearrange("(k p) n -> p k n", p=P)
    w2 = w_in_2[0].rearrange("(k p) n -> p k n", p=P)
    wo1 = w_out[0].rearrange("(k p) n -> p k n", p=P)
    wo2 = w_out_2[0].rearrange("(k p) n -> p k n", p=P)

    def panel(w, c0, n=COLS):
        return [(k, n, w[:, k:k + CHUNK_K, c0:c0 + n]) for k in range(0, KT, CHUNK_K)]

    off2 = np.cumsum([0, C_Q, C_KV, MLA_R, 512, DIL_QKV, DIL_QKV, DIL_QKV, 512, D, D]).tolist()
    o_c, _, _, o_zm, o_q, o_k, o_v, o_zd, o_gm, o_gd, _ = off2
    panels = []
    index = {}

    def add(name, chunks):
        index[name] = len(panels)
        panels.append(chunks)

    add("u", panel(w1, 0))
    add("pgate", panel(w1, 512))
    add("q", panel(w1, 1024))
    add("kv", panel(w1, 1536, 256))
    add("agate", panel(w1, 1792))
    add("o0", panel(wo1, 0))
    add("o1", panel(wo1, 512))
    add("c", panel(w2, o_c, C_W))
    add("zm", panel(w2, o_zm))
    add("zd", panel(w2, o_zd))
    for g in range(3):
        add(f"k{g}", panel(w2, o_k + COLS * g))
        add(f"v{g}", panel(w2, o_v + COLS * g))
        add(f"q{g}", panel(w2, o_q + COLS * g))
    for i in range(2):
        add(f"gm{i}", panel(w2, o_gm + COLS * i))
    for i in range(2):
        add(f"gd{i}", panel(w2, o_gd + COLS * i))
    uq = w_uq[0].rearrange("(k p) n -> p k n", p=P)
    ukv = w_ukv[0].rearrange("p (k n) -> p k n", k=2)
    add("mla", [(0, 384, uq[:, :, 0:384]), (2, 384, uq[:, :, 384:768]), (4, 512, ukv)])
    for name, w in (("om", w_o_mla), ("od", w_o_dil)):
        wk = w[0].rearrange("(k p) n -> p k n", p=P)
        add(name, [(4 * n + k, COLS, wk[:, k:k + 2, COLS * n:COLS * n + COLS])
                   for n in range(2) for k in (0, 2)])
    add("p0", panel(wo2, 0))
    add("p1", panel(wo2, 512))
    if upto <= 1:
        panels = panels[:7]
    elif upto <= 2:
        panels = panels[:index["mla"]]
    chunk_end = np.cumsum([len(p) for p in panels]).tolist()

    x1_d = nc.dram_tensor("x1_scr", [S, D], F32, kind="Internal").ap()
    pool_d = nc.dram_tensor("pool_scr", [512, S], F32, kind="Internal").ap()
    zm_d = nc.dram_tensor("zm_scr", [512, S], F32, kind="Internal").ap()
    zd_d = nc.dram_tensor("zd_scr", [512, S], F32, kind="Internal").ap()
    g_d = nc.dram_tensor("gate_scr", [2 * D, S], F32, kind="Internal").ap()
    rope_d = nc.dram_tensor("rope_scr", [P, 2 * TT * MLA_R // 2], F32, kind="Internal").ap()
    c_d = nc.dram_tensor("c_scr", [S, C_W], F32, kind="Internal").ap()
    qm_d = nc.dram_tensor("qmla_scr", [S, H1 * MLA_QK], F32, kind="Internal").ap()
    am_d = nc.dram_tensor("amla_scr", [512, S], F32, kind="Internal").ap()
    dd_d = nc.dram_tensor("dilout_scr", [512, S], F32, kind="Internal").ap()
    dil_d = [nc.dram_tensor(f"dil{g}_scr", [S, 512 + STAT], F32, kind="Internal").ap()
             for g in range(3)]

    def sb(name, shape, dt=F32, scope=ctx):
        return scope.enter_context(nc.sbuf_tensor(name, shape, dt))

    ps = ctx.enter_context(nc.psum_tensor("ps", [P, 8, COLS], F32))
    ident = sb("ident", [P, P])
    stage = sb("w_stage", [P, STAGE, CHUNK_K, COLS])
    wh = sb("w_hi", [P, 2, KT, COLS], F32R)
    wl = sb("w_lo", [P, 2, KT, COLS], F32R)
    small = sb("small", [P, 88])
    EPS_C = small[:, 87:88]
    ssq, rstd = small[:, 0:8], small[:, 8:16]
    gain_pre, pscale = small[:, 16:24], small[:, 24:28]
    gain_2 = small[:, 28:36]
    gain_q, gain_kv = small[:, 36:38], small[:, 38:39]
    bgate = small[:, 40:56]
    sinks_n = small[:, 56:64]
    sinks_p = small[:, 64:72]
    ssq2 = small[:, 72:80]

    keep = ExitStack()
    aT = sb("attn_outT", [P, 4, S], F32, keep)
    a1 = ExitStack()
    hTh = sb("h1T_hi", [P, KT, S], F32R, a1)
    hTl = sb("h1T_lo", [P, KT, S], F32R, a1)
    s0 = ExitStack()
    xt = sb("x_tiles", [P, TT, D], F32, s0)
    junk = sb("x_sq", [P, D], F32, s0)
    s0.close()
    s1 = ExitStack()
    uT = sb("uT", [P, 2, PAD + S], F32, s1)
    sA = sb("wsumA", [P, PAD + S], F32, s1)
    sB = sb("wsumB", [P, PAD + S], F32, s1)
    pooled = sb("pooled", [P, 2, S], F32, s1)
    edge = sb("pool_edge", [P, 4, PAD], F32, s1)
    edge_t = sb("pool_edge_t", [P, PAD], F32, s1)
    pool_wt = sb("pool_wt", [P, 4, P], F32, s1)
    pmT = sb("pool_outT", [P, 4, S], F32, s1)
    sg1 = sb("silu_pool", [P, 2, COLS], F32, s1)
    s1.close()
    s2 = ExitStack()
    qT = sb("q1T", [P, 4, S], F32, s2)
    kT = sb("k1T", [P, S], F32, s2)
    vT = sb("v1T", [P, S], F32, s2)
    v1 = sb("v1", [P, TT, P], F32, s2)
    swa_b = sb("swa_bias", [P, H1, 2 * P], F32, s2)
    pr = sb("probs", [P, 2, G, 2 * P], F32, s2)
    pT = sb("probsT", [P, 2 * G, P], F32, s2)
    ao = sb("attn_tok", [P, H1, HD], F32, s2)
    st = sb("attn_stats", [P, 4, H1], F32, s2)
    sgA = sb("exp_attn_gate", [P, 2, 2 * P], F32, s2)
    s2.close()
    a1.close()
    a2 = ExitStack()
    pmR = sb("pool_outT_back", [P, 4, S], F32, a2)
    mTh = sb("mixT_hi", [P, KT, S], F32R, a2)
    mTl = sb("mixT_lo", [P, KT, S], F32R, a2)
    xr = sb("x_back", [P, 2, D], F32, a2)
    yn = sb("y_normed", [P, D], F32, a2)
    ysq = sb("y_sq", [P, D], F32, a2)
    x1 = sb("x1_tile", [P, 2, D], F32, a2)
    gpost = sb("gain_post", [P, D], F32, a2)
    a2.close()
    keep.close()

    b1 = ExitStack()
    xt2 = sb("x1_normed", [P, TT, D], F32, b1)
    h2h = sb("h2T_hi", [P, KT, S], F32R, b1)
    h2l = sb("h2T_lo", [P, KT, S], F32R, b1)
    tab = ExitStack()
    cos_d = sb("cos_dil", [P, 3, TT, FREQS], F32, tab)
    sin_d = sb("sin_dil", [P, 3, TT, FREQS], F32, tab)
    cos_m = sb("cos_mla", [P, TT, MLA_R // 2], F32, tab)
    sin_m = sb("sin_mla", [P, TT, MLA_R // 2], F32, tab)
    s5 = ExitStack()
    posi = sb("positions", [P, 3, TT], I32, s5)
    posf = sb("positions_f", [P, 3, TT], F32, s5)
    freq = sb("freqs", [P, FREQS + MLA_R // 2], F32, s5)
    ang = sb("angles", [P, 28, FREQS], F32, s5)
    turn = sb("turns", [P, 28, FREQS], F32, s5)
    red = sb("reduced", [P, 28, FREQS], F32, s5)
    c_sb = sb("c_tok", [P, TT, C_W], F32, s5)
    c_sq = sb("c_sq", [P, C_Q], F32, s5)
    c_ss = sb("c_ss", [P, 2, TT], F32, s5)
    c_t = sb("c_rope_t", [P, 4, TT, MLA_R // 2], F32, s5)
    s5.close()
    s8 = ExitStack()
    vd = sb("v_dil", [P, TT + 1, COLS], F32, s8)
    rc = sb("rope_cos_part", [P, COLS], F32, s8)
    rs = sb("rope_sin_part", [P, COLS], F32, s8)
    rr = sb("rope_out", [P, COLS], F32, s8)
    osb = sb("dil_out", [P, 2, COLS + STAT], F32, s8)
    masks = sb("masks", [P, MASK_W + P], F32, s8)
    s8.close()
    tab.close()
    s9 = ExitStack()
    gt2 = sb("gate_tiles_2", [P, 4, S], F32, s9)
    dgT = sb("dil_gatedT", [P, 4, S], F32, s9)
    wsum = sb("dil_weighted", [P, 3, COLS], F32, s9)
    s9.close()
    b1.close()
    s7 = ExitStack()
    gt = sb("gate_tiles", [P, 4, S], F32, s7)
    s7.close()
    s8 = ExitStack()
    kTd = sb("kT_dil", [P, 4, S], F32, s8)
    qTd = sb("qT_dil", [P, 2, 4, P], F32, s8)
    prd = sb("probs_dil", [P, 2, G, 2 * P], F32, s8)
    pTd = sb("probsT_dil", [P, 2 * G, P], F32, s8)
    s8.close()
    s9 = ExitStack()
    zdT = sb("z_dilT", [P, 4, S], F32, s9)
    nums = sb("dil_nums", [P, 2, 3, COLS], F32, s9)
    stats = sb("dil_stats", [P, 3, TT, STAT], F32, s9)
    coef = sb("dil_coef", [P, 3, TT, H1], F32, s9)
    joint = sb("dil_joint", [P, TT, H1], F32, s9)
    dsum = sb("dil_sum", [P, TT, H1], F32, s9)
    s9.close()
    b2 = ExitStack()
    cqh, cql = (sb(f"cqT_{x}", [P, 2, S], F32R, b2) for x in ("hi", "lo"))
    ckh, ckl = (sb(f"ckvT_{x}", [P, S], F32R, b2) for x in ("hi", "lo"))
    Kh, Kl = (sb(f"kT_mla_{x}", [MLA_QK, 2, S], F32R, b2) for x in ("hi", "lo"))
    Vh, Vl = (sb(f"v_mla_{x}", [P, TT, COLS], F32R, b2) for x in ("hi", "lo"))
    s10 = ExitStack()
    c_bk = sb("c_back", [P, TT, C_W], F32, s10)
    q_sb = sb("q_tok", [P, 2, H1, MLA_QK], F32, s10)
    q_t = sb("q_rope_t", [P, 4, H1, MLA_R // 2], F32, s10)
    cos_q = sb("cos_mla_q", [P, TT, MLA_R // 2], F32, s10)
    sin_q = sb("sin_mla_q", [P, TT, MLA_R // 2], F32, s10)
    s10.close()
    Qh, Ql = (sb(f"qT_mla_{x}", [MLA_QK, 2, S], F32R, b2) for x in ("hi", "lo"))
    PTh, PTl = (sb(f"pT_mla_{x}", [P, 2, TT, 2 * P], F32R, b2) for x in ("hi", "lo"))
    pm = sb("p_mla", [P, 2, S], F32, b2)
    am = sb("a_mla", [P, 2, 2 * P], F32, b2)
    zm = sb("z_mlaT", [P, 2, 2 * P], F32, b2)
    qm = sb("q_tok_back", [P, TT, MLA_QK], F32, b2)
    b2.close()
    b3 = ExitStack()
    Mh, Ml = (sb(f"mergedT_{x}", [P, KT, S], F32R, b3) for x in ("hi", "lo"))
    s11 = ExitStack()
    dh, dl = (sb(f"dilT_{x}", [P, 4, S], F32R, s11) for x in ("hi", "lo"))
    raw = sb("mixersT", [P, 2, S], F32, s11)
    gg = sb("gates", [P, 4, COLS], F32, s11)
    yg = sb("y_gated", [P, COLS], F32, s11)
    s11.close()
    s12 = ExitStack()
    xo = sb("block_out", [P, TT, D], F32, s12)
    osq = sb("block_out_sq", [P, COLS], F32, s12)
    fin = sb("final", [P, 2, D], F32, s12)
    gfin = sb("gain_final", [P, D], F32, s12)
    s12.close()
    b3.close()
    s13 = ExitStack()
    mh, ml = (sb(f"mlaT_{x}", [P, 4, S], F32R, s13) for x in ("hi", "lo"))
    ym = sb("y_mla_gated", [P, KT, S], F32, s13)
    s13.close()

    JOINT_LAG, JOINT_STEP = 6, 3
    MIX_ORDER = (4, 5, 6, 7, 0, 1, 2, 3)
    GATES = (("zm", "zd"), ("gm0", "gm1", "gd0", "gd1"))
    C_KINDS = ((0, P), (P, P), (C_Q, P), (C_W - MLA_QK, MLA_QK))
    C_UNITS = [(n, kind) for n in range(HALF) for kind in range(4)]

    def tile_start(g, t):
        return ((P * t, 1), (t // 2 + 4 * P * (t % 2), 4), (t, 8))[g]

    def spread(start, step):
        return lambda h, k: h[:, k, start:start + step * (P - 1) + 1:step]

    def group_toks(g, t):
        return spread(*tile_start(g, t))

    def value_tiles(g):
        if g:
            return [(t, group_toks(g, t)) for t in range(TT)]
        starts = [0] + [P * t - HD for t in range(1, TT)] + [S - P]
        return [(t, spread(s_, 1)) for t, s_ in enumerate(starts)]

    def window(g, t):
        if g == 2:
            return P * t, P, MASK_W, [(0, P, t, 0, P)]
        if g == 1:
            first = t - t % 2
            return P * first, 2 * P, P * (1 - t % 2), [(0, P, first, 0, P), (P, P, first + 1, 0, P)]
        if t == 0:
            return 0, 3 * HD, P, [(0, HD, 0, 0, HD), (HD, P, 1, 0, P)]
        if t == TT - 1:
            return S - 3 * HD, 3 * HD, HD, [(0, P, t, 0, P), (HD, P, t + 1, HD, HD)]
        return P * t - HD, 2 * P, HD, [(0, P, t, 0, P), (P, P, t + 1, 0, P)]

    n_t = H1 * TT
    m_sum = ssq

    def d_step(g, i):
        return HH * TT * g + i

    D_UNITS = [(g, kind, t) for g in range(3) for kind in "kvq"
               for t in range(len(value_tiles(g)) if kind == "v" else TT)]
    D_SLOTS = 2 * len(D_UNITS) + 6
    step_at = {2 * u + 3 + hh: (g, HH * t + hh)
               for u, (g, kind, t) in enumerate(D_UNITS) if kind == "q" for hh in range(HH)}

    def unit_before(slot):
        u = slot // 2 - 1
        if slot % 2 or not 0 <= u < len(D_UNITS):
            return None
        g, kind, t = D_UNITS[u]
        return u, sum(k != "v" for _, k, _ in D_UNITS[:u]), g, kind, t

    block = ctx.enter_context(nc.Block())
    ENG = ("pe", "act", "dve")
    phases = {who: 0 for who in ENG}

    def phase_end(e, who):
        e.drain().then_inc(sem(f"through_{who}"), 1)
        phases[who] += 1

    def phase_start(e, who):
        for other in ENG:
            if other != who:
                e.wait_ge(*after(f"through_{other}", phases[who]))

    @block.sync
    def _(sp):
        n = 0
        for chunks in panels:
            for k, cols, src in chunks:
                if n >= STAGE:
                    sp.wait_ge(*after("w_split", n - STAGE + 1))
                sp.dma_start(stage[:, n % STAGE, :, 0:cols], src).then_inc(sem(f"w_landed{n % STAGE}"), 16)
                n += 1

    @block.gpsimd
    def _(pool):
        n = 0
        for p, chunks in enumerate(panels):
            if p >= 2:
                pool.wait_ge(*after("panel_used", p - 1))
            for k, cols, src in chunks:
                raw = stage[:, n % STAGE, :, 0:cols]
                hi = wh[:, p % 2, k:k + CHUNK_K, 0:cols]
                lo = wl[:, p % 2, k:k + CHUNK_K, 0:cols]
                parts = [(raw, hi, lo)]
                if p == index["q"]:
                    parts = [(raw[:, i].rearrange("p (a m c) -> p m a c", a=2, c=HD),
                              *(w[:, i].rearrange("p (m a c) -> p m a c", a=2, c=HD) for w in (hi, lo)))
                             for i in range(CHUNK_K)]
                pool.wait_ge(*after(f"w_landed{n % STAGE}", 16 * (n // STAGE + 1)))
                for raw_, hi_, _ in parts:
                    last = nc.gpsimd.tensor_copy(hi_, raw_)
                last.then_inc(sem("w_high"), 1)
                pool.wait_ge(*after("w_high", n + 1))
                for raw_, hi_, lo_ in parts:
                    last = nc.gpsimd.tensor_tensor(lo_, raw_, hi_.bitcast(F32), ALU.subtract)
                last.then_inc(sem("w_split"), 1)
                n += 1

    @block.tensor
    def _(pe):
        units = {"n": 0}

        def panel_ready(name):
            pe.wait_ge(*after("w_split", chunk_end[index[name]]))

        def unit_bank(phase, ring, u, free):
            if u >= ring:
                pe.wait_ge(*after(free, u - ring + 1))
            return u % ring

        def three_passes(acc, pairs, last_inc=None, n_k=KT):
            m = None
            for i, (ah, al, bh, bl) in enumerate(pairs):
                for j, (a, b) in enumerate(((ah, bh), (ah, bl), (al, bh))):
                    m = pe.matmul(acc, a, b, start=(i == 0 and j == 0),
                                  stop=(i == len(pairs) - 1 and j == 2))
            return m

        def wide_unit(name, acc, hh, hl, n, wcols):
            s = index[name] % 2
            sl = slice(COLS * n, COLS * n + COLS)
            return three_passes(acc, [(wcols(wh, s, k), wcols(wl, s, k), hh[:, k, sl], hl[:, k, sl])
                                      for k in range(KT)])

        def tok_unit(name, acc, hh, hl, toks, cols=COLS, k0=0, n_k=KT):
            s = index[name] % 2
            return three_passes(acc, [(toks(hh, k), toks(hl, k), wh[:, s, k0 + k, 0:cols], wl[:, s, k0 + k, 0:cols])
                                      for k in range(n_k)])

        def plain_cols(m):
            return lambda w, s, k: w[:, s, k, P * m:P * m + P]

        def plain_toks(t):
            return lambda h, k: h[:, k, P * t:P * t + P]

        pe.wait_ge(*after("const", 16 * 8))
        def transposes_in(tiles, tag):
            for n in range(HALF):
                for k in range(KT):
                    u = n * KT + k
                    b = unit_bank(tag, 4, u, f"{tag}_evac")
                    for j in range(4):
                        t = 4 * n + j
                        if k == 0:
                            pe.wait_ge(*after(f"{tag}_scaled", t + 1))
                        m = pe.transpose(ps[:, b, P * j:P * j + P], tiles[:, t, P * k:P * k + P], ident[:])
                    m.then_inc(sem(f"{tag}_T"), 1)
        transposes_in(xt, "x")
        phase_end(pe, "pe")

        phase_start(pe, "pe")
        panel_ready("u")
        for g in range(4):
            for n in range(HALF):
                u = 2 * g + n
                b = unit_bank("u", 4, u, "u_evac")
                wide_unit("u", ps[:, b, :], hTh, hTl, n, plain_cols(g)).then_inc(sem("u_done"), 1)
        pe.drain().then_inc(sem("panel_used"), 1)
        panel_ready("pgate")

        def pool_mix(g):
            pe.wait_ge(*after("pooled", g + 1))
            for n in range(HALF):
                u = 2 * g + n
                if u >= 2:
                    pe.wait_ge(*after("mix_evac", u - 1))
                pe.matmul(ps[:, 4 + u % 2, :], pool_wt[:, g, :], pooled[:, g % 2, COLS * n:COLS * n + COLS],
                          start=True, stop=True).then_inc(sem("mix_done"), 1)

        for m in range(4):
            pool_mix(m)
            for n in range(HALF):
                u = 2 * m + n
                if u == 0:
                    pe.wait_ge(*after("u_evac", 8))
                b = unit_bank("pg", 2, u, "pg_evac")
                wide_unit("pgate", ps[:, b, :], hTh, hTl, n, plain_cols(m)).then_inc(sem("pg_done"), 1)
        pe.drain().then_inc(sem("panel_used"), 1)
        phase_end(pe, "pe")

        phase_start(pe, "pe")
        u = 0
        for name, ms in (("q", range(4)), ("kv", range(2))):
            panel_ready(name)
            for m in ms:
                for n in range(HALF):
                    b = unit_bank("qkv", 4, u, "qkv_evac")
                    wide_unit(name, ps[:, b, :], hTh, hTl, n, plain_cols(m)).then_inc(sem("qkv_done"), 1)
                    u += 1
            pe.drain().then_inc(sem("panel_used"), 1)
        pe.wait_ge(*after("qkv_evac", u))
        for half in range(2):
            for j in range(4):
                t = 4 * half + j
                m = pe.transpose(ps[:, 4 + half, P * j:P * j + P], vT[:, P * t:P * t + P], ident[:])
            m.then_inc(sem("v1_T"), 1)
        pe.wait_ge(*after("v1_evac", 2))

        def keys_of(t):
            return (0, P) if t == 0 else (P * (t - 1), 2 * P)

        def swa_scores(i):
            t, hh = divmod(i, HH)
            k0, nk = keys_of(t)
            if i >= 1:
                pe.wait_ge(*after("swa_masked", i))
            for j in range(G):
                h = G * hh + j
                rows = slice(HD * (h // 4), HD * (h // 4) + HD)
                m = pe.matmul(ps[:, j // 2, (j % 2) * 256:(j % 2) * 256 + nk], qT[rows, h % 4, P * t:P * t + P],
                              kT[rows, k0:k0 + nk], start=True, stop=True)
            m.then_inc(sem("swa_scored"), 1)

        def swa_transposes(i):
            t, hh = divmod(i, HH)
            nb = keys_of(t)[1] // P
            pe.wait_ge(*after("swa_exp", G * (i + 1)))
            if i >= 1:
                pe.wait_ge(*after("swa_pT", i))
            for j in range(G):
                for kb in range(nb):
                    c = 2 * j + kb
                    m = pe.transpose(ps[:, 2 + c // 4, (c % 4) * P:(c % 4) * P + P],
                                     pr[:, i % 2, j, P * kb:P * kb + P], ident[:])
            m.then_inc(sem("swa_T"), 1)

        def swa_values(i):
            t, hh = divmod(i, HH)
            nb = keys_of(t)[1] // P
            pe.wait_ge(*after("swa_pT", i + 1))
            if i >= 2:
                pe.wait_ge(*after("swa_out", i - 1))
            for j in range(G):
                h = G * hh + j
                for kb in range(nb):
                    kt = t - nb + 1 + kb
                    m = pe.matmul(ps[:, 4 + i % 2, HD * j:HD * j + HD], pT[:, 2 * j + kb, :],
                                  v1[:, kt, HD * (h // 4):HD * (h // 4) + HD], start=(kb == 0), stop=(kb == nb - 1))
            m.then_inc(sem("swa_valued"), 1)

        def swa_back(t):
            pe.wait_ge(*after("swa_out", 2 * t + 2))
            if t >= 1:
                pe.wait_ge(*after("swa_aT", t))
            flat = ao[:].rearrange("p h d -> p (h d)")
            for j in range(4):
                m = pe.transpose(ps[:, 6, P * j:P * j + P], flat[:, P * j:P * j + P], ident[:])
            m.then_inc(sem("swa_backT"), 1)

        def attn_gate(i):
            quarter, m_ = divmod(i, 4)
            if i >= 1:
                pe.wait_ge(*after("ag_mul", i))
            s = index["agate"] % 2
            sl = slice(2 * P * quarter, 2 * P * quarter + 2 * P)
            three_passes(ps[:, 7, 0:2 * P], [(wh[:, s, k, P * m_:P * m_ + P], wl[:, s, k, P * m_:P * m_ + P], hTh[:, k, sl], hTl[:, k, sl])
                                             for k in range(KT)]).then_inc(sem("ag_done"), 1)

        steps = TT * HH
        panel_ready("agate")
        for i in range(steps + 3):
            if i < steps:
                swa_scores(i)
            if 2 <= i < steps + 2:
                swa_values(i - 2)
            if i < steps:
                attn_gate(i)
            if i >= 4 and i % 2 == 0:
                swa_back((i - 4) // 2)
            if 1 <= i <= steps:
                swa_transposes(i - 1)
        pe.drain().then_inc(sem("panel_used"), 1)
        phase_end(pe, "pe")

        phase_start(pe, "pe")
        panel_ready("o1")
        s_o = [index[name] % 2 for name in ("o0", "o1")]

        def y_part(t, ks, first, last):
            for k in ks:
                if t == 0:
                    pe.wait_ge(*after("mixT_split", MIX_ORDER.index(k) + 1))
                for half in range(2):
                    acc = ps[:, 2 * (t % 2) + half, :]
                    tk = slice(P * t, P * t + P)
                    for j, (a, b) in enumerate(((mTh, wh), (mTh, wl), (mTl, wh))):
                        m = pe.matmul(acc, a[:, k, tk], b[:, s_o[half], k, :], start=(k == first and j == 0),
                                      stop=(k == last and j == 2))
            return m

        for t in range(2):
            y_part(t, MIX_ORDER[:4], MIX_ORDER[0], None)
        for t in range(TT):
            if t >= 2:
                pe.wait_ge(*after("y_read", t - 1))
            y_part(t, MIX_ORDER[4:] if t < 2 else MIX_ORDER, MIX_ORDER[0], MIX_ORDER[-1]).then_inc(sem("y_done"), 1)
        pe.drain().then_inc(sem("panel_used"), 2)
        phase_end(pe, "pe")

        phase_start(pe, "pe")
        transposes_in(xt2, "x1")
        phase_end(pe, "pe")

        phase_start(pe, "pe")
        panel_ready("c")
        for t in range(TT):
            b = unit_bank("c", 4, t, "c_evac")
            tok_unit("c", ps[:, b, 0:C_W], h2h, h2l, plain_toks(t), C_W).then_inc(sem("c_done"), 1)
        pe.drain().then_inc(sem("panel_used"), 1)

        def gate_panels(names, u, after_unit=lambda u: None):
            for name in names:
                panel_ready(name)
                for m in range(4):
                    for n in range(HALF):
                        if u == 0:
                            pe.wait_ge(*after("c_evac", TT))
                        b = unit_bank("g", 4, u, "g_evac")
                        wide_unit(name, ps[:, b, :], h2h, h2l, n, plain_cols(m)).then_inc(sem("g_done"), 1)
                        after_unit(u)
                        u += 1
                pe.drain().then_inc(sem("panel_used"), 1)
        gate_panels(GATES[0], 0)
        phase_end(pe, "pe")

        phase_start(pe, "pe")
        pe.wait_ge(*after("masks_in", 16))

        def d_proj(slot):
            u, part = divmod(slot, 2)
            g, kind, t = D_UNITS[u]
            name = f"{kind}{g}"
            toks = value_tiles(g)[t][1] if kind == "v" else group_toks(g, t)
            s = index[name] % 2
            if part == 0:
                if t == 0:
                    panel_ready(name)
                if u >= 2:
                    pe.wait_ge(*after("d_read", u - 1))
            for k in range(KT // 2 * part, KT // 2 * (part + 1)):
                for a, b in ((h2h, wh), (h2h, wl), (h2l, wh)):
                    m = pe.matmul(ps[:, u % 2, :], toks(a, k), b[:, s, k, :], start=(k == 0 and b is wh and a is h2h),
                                  stop=(k == KT - 1 and a is h2l))
            if part == 1:
                m.then_inc(sem("d_done"), 1)
                if u + 1 == len(D_UNITS) or D_UNITS[u + 1][:2] != (g, kind):
                    pe.drain().then_inc(sem("panel_used"), 1)

        def rotated_transposes(r):
            pe.wait_ge(*after("rotated", r + 1))
            if r >= 1:
                pe.wait_ge(*after("rotT_read", r))
            for j in range(4):
                m = pe.transpose(ps[:, 2, P * j:P * j + P], rr[:, P * j:P * j + P], ident[:])
            m.then_inc(sem("rotT"), 1)

        def d_scores(g, i):
            n = d_step(g, i)
            t, hh = divmod(i, HH)
            k0, nk, _, _ = window(g, t)
            pe.wait_ge(*after("rotT_read", 2 * TT * g + TT + t + 1))
            if n >= 1:
                pe.wait_ge(*after("d_masked", n))
            for j in range(G):
                h = G * hh + j
                rows = slice(HD * (h % 2), HD * (h % 2) + HD)
                m = pe.matmul(ps[:, 3 + j % 2, (j // 2) * 256:(j // 2) * 256 + nk], qTd[rows, t % 2, h // 2, :],
                              kTd[rows, h // 2, k0:k0 + nk], start=True, stop=True)
            m.then_inc(sem("d_scored"), 1)

        def d_transposes(g, i):
            n = d_step(g, i)
            blocks = window(g, i // HH)[3]
            pe.wait_ge(*after("d_exp", G * (n + 1)))
            if n >= 1:
                pe.wait_ge(*after("d_pT", n))
            for j in range(G):
                for kb, (c0, width, _, _, _) in enumerate(blocks):
                    c = 2 * j + kb
                    m = pe.transpose(ps[0:width, 5 + c // 4, (c % 4) * P:(c % 4) * P + P],
                                     prd[:, i % 2, j, c0:c0 + width], ident[:])
            m.then_inc(sem("d_T"), 1)

        def d_values(g, i):
            n = d_step(g, i)
            t, hh = divmod(i, HH)
            blocks = window(g, t)[3]
            if i == 0:
                pe.wait_ge(*after("d_read", D_UNITS.index((g, "q", 0))))
            pe.wait_ge(*after("d_pT", n + 1))
            if n >= 1:
                pe.wait_ge(*after("d_out", n))
            for j in range(G):
                h = G * hh + j
                for kb, (_, _, vt, r0, nr) in enumerate(blocks):
                    m = pe.matmul(ps[:, 7, HD * j:HD * j + HD], pTd[r0:r0 + nr, 2 * j + kb, :],
                                  vd[r0:r0 + nr, vt, HD * h:HD * h + HD], start=(kb == 0), stop=(kb == len(blocks) - 1))
            m.then_inc(sem("d_valued"), 1)

        for slot in range(D_SLOTS):
            if slot in step_at:
                d_scores(*step_at[slot])
            if slot - 2 in step_at:
                d_values(*step_at[slot - 2])
            if slot < 2 * len(D_UNITS):
                d_proj(slot)
            done = unit_before(slot)
            if done and done[3] != "v":
                rotated_transposes(done[1])
            if slot - 1 in step_at:
                d_transposes(*step_at[slot - 1])
        phase_end(pe, "pe")

        phase_start(pe, "pe")

        def joint_transposes(u):
            t, r = divmod(u - 16 - JOINT_LAG, JOINT_STEP)
            if r or not 0 <= t < TT:
                return
            pe.wait_ge(*after("joint", t + 1))
            if t >= 2:
                pe.wait_ge(*after("dg_done", t - 1))
            for j in range(4):
                m = pe.transpose(ps[:, 4 + t % 2, P * j:P * j + P], wsum[:, 0, P * j:P * j + P], ident[:])
            m.then_inc(sem("jointT"), 1)

        gate_panels(GATES[1], 16, joint_transposes)
        phase_end(pe, "pe")

        phase_start(pe, "pe")
        pe.wait_ge(*after("c_back", 16))
        for u, (n, kind) in enumerate(C_UNITS):
            b = unit_bank("cT", 4, u, "cT_lo")
            c0, width = C_KINDS[kind]
            for j in range(4):
                m = pe.transpose(ps[0:width, b, P * j:P * j + P], c_bk[:, 4 * n + j, c0:c0 + width], ident[:])
            m.then_inc(sem("cT"), 1)
        pe.wait_ge(*after("cT_lo", len(C_UNITS)))
        panel_ready("mla")
        s = index["mla"] % 2
        for t in range(TT):
            for half in range(2):
                u = 2 * t + half
                if u >= 4:
                    pe.wait_ge(*after("qm_read", u - 3))
                three_passes(ps[:, u % 4, 0:384], [
                    (cqh[:, k, P * t:P * t + P], cql[:, k, P * t:P * t + P],
                     wh[:, s, 2 * half + k, 0:384], wl[:, s, 2 * half + k, 0:384]) for k in range(2)]).then_inc(sem("qm_done"), 1)
            if t >= 2:
                pe.wait_ge(*after("vm_lo", t - 1))
            for n in range(2):
                v_cols = [w[:, s, 4 + n, :].rearrange("p (h c) -> p h c", c=P)[:, :, HD:] for w in (wh, wl)]
                m = three_passes(ps[:, 4 + t % 2, 256 * n:256 * n + 256].rearrange("p (h c) -> p h c", c=HD), [
                    (ckh[:, P * t:P * t + P], ckl[:, P * t:P * t + P], *v_cols)])
            m.then_inc(sem("vm_done"), 1)
        phase_end(pe, "pe")

        phase_start(pe, "pe")

        def head_inputs(h, part):
            x = 4 * h + part
            if x >= 1:
                pe.wait_ge(*after("qk_lo", x))
            if part < 2:
                pe.wait_ge(*after("qm_back", 16 * (h + 1)))
                for j in range(4):
                    m = pe.transpose(ps[0:MLA_QK, 7, P * j:P * j + P], qm[:, 4 * part + j, :], ident[:])
            else:
                n = part - 2
                w = [y[:, s, 4 + h // 4, P * (h % 4):P * (h % 4) + P] for y in (wh, wl)]
                m = three_passes(ps[:, 7, :], [(*w, ckh[:, COLS * n:COLS * n + COLS], ckl[:, COLS * n:COLS * n + COLS])])
            m.then_inc(sem("qk_done"), 1)

        def m_scores(i):
            h, qt = divmod(i, TT)
            pe.wait_ge(*after("qk_lo", 4 * h + 4))
            if i >= 2:
                pe.wait_ge(*after("m_exp", i - 1))
            for n in range(HALF):
                m = three_passes(ps[:, 2 * (i % 2) + n, :], [
                    (Qh[:, h % 2, P * qt:P * qt + P], Ql[:, h % 2, P * qt:P * qt + P],
                     Kh[:, h % 2, COLS * n:COLS * n + COLS], Kl[:, h % 2, COLS * n:COLS * n + COLS])])
            m.then_inc(sem("m_scored"), 1)

        def m_transposes(i):
            pe.wait_ge(*after("m_normed", i + 1))
            if i >= 1:
                pe.wait_ge(*after("m_lo", i))
            for kt in range(TT):
                m = pe.transpose(ps[:, 4 + kt // 4, (kt % 4) * P:(kt % 4) * P + P], pm[:, i % 2, P * kt:P * kt + P], ident[:])
            m.then_inc(sem("m_T"), 1)

        def m_values(b, part):
            h = b // 4
            pe.wait_ge(*after("m_lo", 2 * b + 2))
            if b >= 1:
                pe.wait_ge(*after("m_out", b))
            c = P * (h // 2)
            ops = [(a[:, kt, c:c + P], p[:, b % 2, kt, :]) for kt in range(4 * part, 4 * part + 4)
                   for a, p in ((Vh, PTh), (Vh, PTl), (Vl, PTh))]
            for i, (a, p) in enumerate(ops):
                m = pe.matmul(ps[:, 6, 0:256], a, p, start=(part == 0 and i == 0), stop=(part == 1 and i == 11))
            if part == 1:
                m.then_inc(sem("m_valued"), 1)

        for part in range(4):
            head_inputs(0, part)
        for j in range(n_t + 5):
            if j < n_t:
                m_scores(j)
            if 5 <= j:
                m_values((j - 5) // 2, (j - 5) % 2)
            if j < n_t:
                h, qt = divmod(j, TT)
                if h + 1 < H1 and qt in (2, 3, 4, 5):
                    head_inputs(h + 1, qt - 2)
            if 2 <= j < n_t + 2:
                m_transposes(j - 2)
        pe.drain().then_inc(sem("panel_used"), 1)
        phase_end(pe, "pe")

        phase_start(pe, "pe")
        for o, (name, h_, l_) in enumerate((("om", mh, ml), ("od", dh, dl))):
            panel_ready(name)
            s = index[name] % 2
            for n in range(HALF):
                sl = slice(COLS * n, COLS * n + COLS)
                for m_ in range(KT):
                    u = 2 * KT * o + KT * n + m_
                    if u >= 8:
                        pe.wait_ge(*after("y2_read", u - 7))
                    c = P * (m_ % 4)
                    for k in range(4):
                        if n == 0 and m_ == 0:
                            pe.wait_ge(*after("mixers_lo", 4 * o + k + 1))
                        w_hi, w_lo = (w[:, s, 4 * (m_ // 4) + k, c:c + P] for w in (wh, wl))
                        for j, (a, b) in enumerate(((w_hi, h_), (w_hi, l_), (w_lo, h_))):
                            m = pe.matmul(ps[:, u % 8, :], a, b[:, k, sl], start=(k == 0 and j == 0), stop=(k == 3 and j == 2))
                    m.then_inc(sem("y2_done"), 1)
            pe.drain().then_inc(sem("panel_used"), 1)

        for half, name in enumerate(("p0", "p1")):
            panel_ready(name)
            for t in range(TT):
                u = TT * half + t
                if t in (0, 4) and half == 0:
                    pe.wait_ge(*after("merged_lo", 2 * t + 8))
                pe.wait_ge(*(after("o_read", u - 7) if u >= 8 else after("y2_read", 4 * KT - 7 + u)))
                tok_unit(name, ps[:, u % 8, :], Mh, Ml, plain_toks(t)).then_inc(sem("o_done"), 1)
            pe.drain().then_inc(sem("panel_used"), 1)

    @block.scalar
    def _(act):
        x_tok = x[0].rearrange("(t p) d -> t p d", p=P)
        for t in range(TT):
            act.dma_start(xt[:, t, :], x_tok[t]).then_inc(sem(f"x_in{t}"), 16)
        consts = [
            (ident[:], c_ident),
            (gain_pre, norm_pre[0].rearrange("(k p) -> p k", p=P)),
            (pscale, pool_scale[0].rearrange("(k p) -> p k", p=P)),
            (gain_2, attn_norm_g[0].rearrange("(k p) -> p k", p=P)),
            (gain_q, q_norm_g[0].rearrange("(k p) -> p k", p=P)),
            (gain_kv, kv_norm_g[0].rearrange("(k p) -> p k", p=P)),
            (bgate, b_gate[0].rearrange("(k p) -> p k", p=P)),
            (sinks_p, attn_sinks[0:1, :].to_broadcast([P, H1])),
        ]
        with nc.allow_non_contiguous_dma(reason="vectors of one value a partition"):
            for dst, src in consts:
                act.dma_start(dst, src).then_inc(sem("const"), 16)
        act.wait_ge(*after("zeroed", 1))

        def norm_stats(tiles, width, squares, tag):
            for t in range(TT):
                act.wait_ge(*after(f"{tag}_in{t}", 16))
                act.activation(squares, tiles[:, t, :], ACT.Square, accum_out=ssq[:, t:t + 1]).then_inc(sem(f"{tag}_sq"), 1)
                act.wait_ge(*after(f"{tag}_sq", t + 1))
            act.activation(rstd, ssq, ACT.Sqrt, scale=1.0 / width, bias=EPS_C).then_inc(sem(f"{tag}_root"), 1)

        norm_stats(xt, D, junk[:], "x")
        for n in range(HALF):
            for k in range(KT):
                u = n * KT + k
                act.wait_ge(*after("x_T", u + 1))
                act.activation(hTh[:, k, COLS * n:COLS * n + COLS], ps[:, u % 4, :], ACT.Copy,
                               scale=gain_pre[:, k:k + 1]).then_inc(sem("x_hi"), 1)
        phase_end(act, "act")

        phase_start(act, "act")
        act.dma_start(pool_wt[:], pool_w[0].rearrange("g c d -> c g d")).then_inc(sem("pool_c"), 16)
        for g in range(4):
            act.dma_start(edge[:, g, :], c_inv[g:g + 1, :].to_broadcast([P, PAD])).then_inc(sem("pool_c"), 16)
        act.wait_ge(*after("u_pad", 1))
        for u in range(8):
            g, n = divmod(u, 2)
            act.wait_ge(*after("u_done", u + 1))
            if g >= 2:
                act.wait_ge(*after("pooled", g - 1))
            act.activation(uT[:, g % 2, PAD + COLS * n:PAD + COLS * n + COLS], ps[:, u % 4, :],
                           ACT.Copy).then_inc(sem("u_evac"), 1)
        for u in range(8):
            act.wait_ge(*after("pg_done", u + 1))
            if u >= 2:
                act.wait_ge(*after("pg_mul", u - 1))
            act.activation(sg1[:, u % 2, :], ps[:, u % 2, :], ACT.Silu).then_inc(sem("pg_evac"), 1)
        for g in range(4):
            act.wait_ge(*after("pg_mul", 2 * g + 2))
            act.dma_start(pool_d[P * g:P * g + P, :], pmT[:, g, :]).then_inc(sem("pool_spill"), 16)
        act.wait_ge(*after("pool_spill", 64))
        phase_end(act, "act")

        phase_start(act, "act")
        act.dma_start(swa_b[:].rearrange("p h k -> p (h k)"), c_swa).then_inc(sem("swa_c"), 16)
        for u in range(12):
            act.wait_ge(*after("qkv_done", u + 1))
            m, n = divmod(u, 2)
            sl = slice(COLS * n, COLS * n + COLS)
            dst = qT[:, m, sl] if m < 4 else (kT[:, sl] if m == 4 else vT[:, sl])
            act.activation(dst, ps[:, u % 4, :], ACT.Copy, scale=HD ** -0.5 if m < 4 else 1.0).then_inc(sem("qkv_evac"), 1)
        act.wait_ge(*after("v1_T", 2))
        for half in range(2):
            act.activation(v1[:, 4 * half:4 * half + 4, :], ps[:, 4 + half, :], ACT.Copy).then_inc(sem("v1_evac"), 1)

        steps = TT * HH

        def swa_pT(i):
            nb = 1 if i < HH else 2
            act.wait_ge(*after("swa_T", i + 1))
            if i >= 1:
                act.wait_ge(*after("swa_valued", i))
            src = ps[:, 2:4, :].rearrange("p b (j c) -> p (b j) c", c=P)
            if nb == 1:
                act.activation(pT[:, 0:8:2, :], src[:, 0:8:2, :], ACT.Copy).then_inc(sem("swa_pT"), 1)
            else:
                act.activation(pT[:], src, ACT.Copy).then_inc(sem("swa_pT"), 1)

        for i in range(steps + 1):
            if i < steps:
                t, hh = divmod(i, HH)
                nk = P if t == 0 else 2 * P
                act.wait_ge(*after("swa_max", i + 1))
                for j in range(G):
                    h = G * hh + j
                    act.activation(pr[:, i % 2, j, 0:nk], pr[:, i % 2, j, 0:nk], ACT.Exp,
                                   bias=st[:, 0, h:h + 1], accum_out=st[:, 1, h:h + 1]).then_inc(sem("swa_exp"), 1)
                act.activation(st[:, 2, G * hh:G * hh + G], st[:, 3, G * hh:G * hh + G], ACT.Exp).then_inc(sem("swa_sink"), 1)
                act.wait_ge(*after("ag_done", i + 1))
                if i >= 2:
                    act.wait_ge(*after("ag_mul", i - 1))
                act.activation(sgA[:, i % 2, :], ps[:, 7, 0:2 * P], ACT.Exp, scale=-1.0).then_inc(sem("ag_evac"), 1)
            if i >= 1:
                swa_pT(i - 1)
        phase_end(act, "act")

        phase_start(act, "act")
        for g in range(4):
            act.dma_start(pmR[:, g, :], pool_d[P * g:P * g + P, :]).then_inc(sem("pool_back"), 16)
        act.dma_start(gpost[:], norm_post[0:1, :].to_broadcast([P, D])).then_inc(sem("gpost"), 16)
        for i, k in enumerate(MIX_ORDER):
            if i == 4:
                act.wait_ge(*after("pool_back", 64))
            src = pmR[:, k, :] if k < 4 else aT[:, k - 4, :]
            act.activation(mTh[:, k, :], src, ACT.Copy).then_inc(sem("mixT_hi"), 1)
        x1_tok = x1_d.rearrange("(t p) d -> t p d", p=P)

        def x_back(t):
            if t >= 2:
                act.wait_ge(*after("x1_made", t - 1))
            act.dma_start(xr[:, t % 2, :], x_tok[t]).then_inc(sem(f"x_back{t % 2}"), 16)

        def x1_store(t):
            act.wait_ge(*after("x1_made", t + 1))
            act.dma_start(x1_tok[t], x1[:, t % 2, :]).then_inc(sem(f"x1_out{t % 2}"), 16)

        def x1_root(t):
            if t >= 1:
                act.wait_ge(*after("x1_sq", t))
            act.wait_ge(*after("y_sq", t + 1))
            act.activation(ysq[:], x1[:, t % 2, :], ACT.Square, accum_out=ssq2[:, t:t + 1]).then_inc(sem("x1_sq"), 1)
            act.wait_ge(*after("x1_sq", t + 1))
            act.activation(ssq2[:, t:t + 1], ssq2[:, t:t + 1], ACT.Sqrt, scale=1.0 / D, bias=EPS_C).then_inc(sem("x1_root"), 1)

        x_back(0)
        x_back(1)
        for t in range(TT):
            act.wait_ge(*after("y_done", t + 1))
            if t >= 1:
                act.wait_ge(*after("y_sq", t))
            if t >= 2:
                act.wait_ge(*after("x1_sq", t - 1))
            b = 2 * (t % 2)
            act.activation(ysq[:].rearrange("p (b c) -> p b c", b=2), ps[:, b:b + 2, :], ACT.Square,
                           accum_out=ssq[:, t:t + 1]).then_inc(sem("y_sq"), 1)
            act.wait_ge(*after("y_sq", t + 1))
            act.activation(rstd[:, t:t + 1], ssq[:, t:t + 1], ACT.Sqrt, scale=1.0 / D, bias=EPS_C).then_inc(sem("y_root"), 1)
            if t >= 1:
                x1_store(t - 1)
                x1_root(t - 1)
                if t + 1 < TT:
                    x_back(t + 1)
        x1_store(TT - 1)
        x1_root(TT - 1)
        for b in range(2):
            act.wait_ge(*after(f"x1_out{b}", 16 * TT // 2))
        phase_end(act, "act")

        phase_start(act, "act")
        with nc.allow_non_contiguous_dma(reason="one position a partition"):
            pos_row = positions[0]
            for g in range(3):
                for t in range(TT):
                    start, step = tile_start(g, t)
                    src = pos_row[start:start + step * (P - 1) + 1:step].rearrange("(p a) -> p a", a=1)
                    act.dma_start(posi[:, g, t:t + 1], src).then_inc(sem("pos_in"), 16)
            act.dma_start(freq[:], c_freq.to_broadcast([P, FREQS + MLA_R // 2])).then_inc(sem("pos_in"), 16)
        for n in range(HALF):
            for k in range(KT):
                u = n * KT + k
                act.wait_ge(*after("x1_T", u + 1))
                act.activation(h2h[:, k, COLS * n:COLS * n + COLS], ps[:, u % 4, :], ACT.Copy,
                               scale=gain_2[:, k:k + 1]).then_inc(sem("x1_hi"), 1)
        phase_end(act, "act")

        phase_start(act, "act")
        for t in range(TT):
            act.wait_ge(*after("c_done", t + 1))
            act.activation(c_sb[:, t, :], ps[:, t % 4, 0:C_W], ACT.Copy).then_inc(sem("c_evac"), 1)
            act.wait_ge(*after("c_evac", t + 1))
            for i, (c0, w) in enumerate(((0, C_Q), (C_Q, C_KV))):
                act.activation(c_sq[:, 0:w], c_sb[:, t, c0:c0 + w], ACT.Square, accum_out=c_ss[:, i, t:t + 1]).then_inc(sem("c_sqd"), 1)
                act.wait_ge(*after("c_sqd", 2 * t + i + 1))
        for i, (dst, q) in enumerate(((sin_d, 0), (cos_d, 1))):
            act.wait_ge(*after("angles", i + 1))
            act.activation(dst[:].rearrange("p g t f -> p (g t) f"), red[:, 0:24, :], ACT.Sin).then_inc(sem("tables"), 1)
            m_dst = (sin_m, cos_m)[i]
            act.activation(m_dst[:], red[:, 24:28, :].rearrange("p a (b f) -> p (a b) f", b=2), ACT.Sin).then_inc(sem("tables"), 1)
        act.wait_ge(*after("tables", 4))
        w_m = TT * MLA_R // 2
        act.dma_start(rope_d[:, 0:w_m], cos_m[:].rearrange("p t f -> p (t f)")).then_inc(sem("rope_spill"), 16)
        act.dma_start(rope_d[:, w_m:], sin_m[:].rearrange("p t f -> p (t f)")).then_inc(sem("rope_spill"), 16)
        for i, w in enumerate((C_Q, C_KV)):
            act.activation(c_ss[:, i, :], c_ss[:, i, :], ACT.Sqrt, scale=1.0 / w, bias=EPS_C).then_inc(sem("c_root"), 1)
        act.wait_ge(*after("c_roped", 1))
        act.wait_ge(*after("c_scaled", 2 * TT))
        act.dma_start(c_d.rearrange("(t p) c -> p t c", p=P), c_sb[:]).then_inc(sem("c_spill"), 16)

        def gate_evac(units, tiles, after_unit=lambda u: None):
            for u in units:
                mt, n = divmod(u, 2)
                gi, m = divmod(mt, 4)
                dst = (zm_d, zd_d, g_d, g_d, g_d, g_d)[gi]
                row0 = 0 if gi < 2 else COLS * (gi - 2)
                if n == 0 and mt >= 4:
                    act.wait_ge(*after(f"g_spill{mt % 4}", 16 * (mt // 4)))
                act.wait_ge(*after("g_done", u + 1))
                d = tiles[:, mt % 4, COLS * n:COLS * n + COLS]
                if gi < 2:
                    act.activation(d, ps[:, u % 4, :], ACT.Silu).then_inc(sem("g_evac"), 1)
                else:
                    c = row0 // P + m
                    act.activation(d, ps[:, u % 4, :], ACT.Sigmoid, bias=bgate[:, c:c + 1]).then_inc(sem("g_evac"), 1)
                if n:
                    act.wait_ge(*after("g_evac", u + 1))
                    act.dma_start(dst[row0 + P * m:row0 + P * m + P, :], tiles[:, mt % 4, :]).then_inc(sem(f"g_spill{mt % 4}"), 16)
                after_unit(u)
        gate_evac(range(16), gt)
        act.wait_ge(*after("rope_spill", 32))
        act.wait_ge(*after("c_spill", 16))
        for b in range(4):
            act.wait_ge(*after(f"g_spill{b}", 16 * 2))
        phase_end(act, "act")

        phase_start(act, "act")
        act.dma_start(masks[:], c_mask).then_inc(sem("masks_in"), 16)

        def rotT_read(r, g, t, keys):
            act.wait_ge(*after("rotT", r + 1))
            src = ps[:, 2, :].rearrange("p (j c) -> p j c", c=P)
            if keys:
                act.activation(kTd[:, :, P * t:P * t + P], src, ACT.Copy).then_inc(sem("rotT_read"), 1)
            else:
                if t >= 2:
                    act.wait_ge(*after("d_scored", d_step(g, 2 * (t - 2) + 2)))
                act.activation(qTd[:, t % 2, :, :], src, ACT.Copy, scale=HD ** -0.5).then_inc(sem("rotT_read"), 1)

        def d_exp(g, i):
            n = d_step(g, i)
            t, hh = divmod(i, HH)
            nk = window(g, t)[1]
            act.wait_ge(*after("d_max", n + 1))
            for j in range(G):
                h = G * hh + j
                o = osb[:, t % 2, :]
                act.activation(prd[:, i % 2, j, 0:nk], prd[:, i % 2, j, 0:nk], ACT.Exp, bias=o[:, COLS + h:COLS + h + 1],
                               accum_out=o[:, COLS + H1 + h:COLS + H1 + h + 1]).then_inc(sem("d_exp"), 1)

        def d_pT(g, i):
            n = d_step(g, i)
            blocks = window(g, i // HH)[3]
            act.wait_ge(*after("d_T", n + 1))
            if n >= 1:
                act.wait_ge(*after("d_valued", n))
            src = ps[:, 5:7, :].rearrange("p b (j c) -> p (b j) c", c=P)
            if len(blocks) == 1:
                act.activation(pTd[:, 0:8:2, :], src[:, 0:8:2, :], ACT.Copy).then_inc(sem("d_pT"), 1)
            elif blocks[0][1] < P:
                w = blocks[0][1]
                act.activation(pTd[0:w, 0:8:2, :], src[0:w, 0:8:2, :], ACT.Copy)
                act.activation(pTd[:, 1:8:2, :], src[:, 1:8:2, :], ACT.Copy).then_inc(sem("d_pT"), 1)
            else:
                act.activation(pTd[:], src, ACT.Copy).then_inc(sem("d_pT"), 1)

        def d_store(g, t):
            act.wait_ge(*after("d_out", d_step(g, 2 * t + 2)))
            start, step = tile_start(g, t)
            act.dma_start(dil_d[g][start:start + step * (P - 1) + 1:step, :], osb[:, t % 2, :]).then_inc(sem(f"d_store{t % 2}"), 16)

        for slot in range(D_SLOTS):
            done = unit_before(slot)
            if done and done[3] == "v":
                u, _, g, _, t = done
                if t == 0:
                    act.wait_ge(*after("d_read", u))
                    if g:
                        act.wait_ge(*after("d_valued", d_step(g, 0)))
                act.wait_ge(*after("d_done", u + 1))
                act.activation(vd[:, t, :], ps[:, u % 2, :], ACT.Copy).then_inc(sem("d_read"), 1)
            if slot in step_at:
                d_exp(*step_at[slot])
            if done and done[3] != "v":
                rotT_read(done[1], done[2], done[4], done[3] == "k")
            if slot - 1 in step_at:
                d_pT(*step_at[slot - 1])
            if slot - 2 in step_at:
                g, i = step_at[slot - 2]
                if i % HH == HH - 1:
                    d_store(g, i // HH)
        for b in range(2):
            act.wait_ge(*after(f"d_store{b}", 16 * 3 * TT // 2))
        phase_end(act, "act")

        phase_start(act, "act")
        for g in range(3):
            act.dma_start(stats[:, g, :, :], dil_d[g].rearrange("(t p) c -> p t c", p=P)[:, :, COLS:]).then_inc(sem("stats_in"), 16)
        for j in range(4):
            act.dma_start(zdT[:, j, :], zd_d[P * j:P * j + P, :]).then_inc(sem("zd_in"), 16)

        def nums_in(t):
            if t >= 2:
                act.wait_ge(*after("weighted", 3 * (t - 1)))
            for g in range(3):
                act.dma_start(nums[:, t % 2, g, :], dil_d[g][P * t:P * t + P, 0:COLS]).then_inc(sem(f"nums_in{t % 2}"), 16)

        nums_in(0)
        nums_in(1)
        for g in range(3):
            act.wait_ge(*after("coef_arg", g + 1))
            act.activation(coef[:, g, :, :], coef[:, g, :, :], ACT.Exp).then_inc(sem("coef_exp"), 1)

        def more_nums(u):
            t, r = divmod(u - 16 - JOINT_LAG, JOINT_STEP)
            if not r and 0 <= t < TT - 2:
                nums_in(t + 2)

        gate_evac(range(16, 48), gt2, more_nums)
        for b in range(4):
            act.wait_ge(*after(f"g_spill{b}", 16 * 6))
        act.wait_ge(*after("dg_done", TT))
        for j in range(4):
            act.dma_start(dd_d[P * j:P * j + P, :], dgT[:, j, :]).then_inc(sem("dg_spill"), 16)
        act.wait_ge(*after("dg_spill", 64))
        phase_end(act, "act")

        phase_start(act, "act")
        act.dma_start(c_bk[:], c_d.rearrange("(t p) c -> p t c", p=P)).then_inc(sem("c_back"), 16)
        act.dma_start(cos_q[:].rearrange("p t f -> p (t f)"), rope_d[:, 0:w_m]).then_inc(sem("rope_back"), 16)
        act.dma_start(sin_q[:].rearrange("p t f -> p (t f)"), rope_d[:, w_m:]).then_inc(sem("rope_back"), 16)
        for u, (n, kind) in enumerate(C_UNITS):
            sl = slice(COLS * n, COLS * n + COLS)
            act.wait_ge(*after("cT", u + 1))
            if kind < 2:
                act.activation(cqh[:, kind, sl], ps[:, u % 4, :], ACT.Copy, scale=gain_q[:, kind:kind + 1]).then_inc(sem("cT_hi"), 1)
            elif kind == 2:
                act.activation(ckh[:, sl], ps[:, u % 4, :], ACT.Copy, scale=gain_kv).then_inc(sem("cT_hi"), 1)
            else:
                for b in range(2):
                    last = act.activation(Kh[HD:MLA_QK, b, sl], ps[HD:MLA_QK, u % 4, :], ACT.Copy)
                last.then_inc(sem("cT_hi"), 1)
        for t in range(TT):
            for half in range(2):
                u = 2 * t + half
                act.wait_ge(*after("qm_done", u + 1))
                if half == 0 and t >= 2:
                    act.wait_ge(*after(f"qm_spill{t % 2}", 16 * (t // 2)))
                act.activation(q_sb[:, t % 2, 4 * half:4 * half + 4, :], ps[:, u % 4, 0:384].rearrange("p (h c) -> p h c", c=MLA_QK),
                               ACT.Copy, scale=float(MLA_QK) ** -0.5).then_inc(sem("qm_read"), 1)
            act.wait_ge(*after("vm_done", t + 1))
            act.activation(Vh[:, t, :], ps[:, 4 + t % 2, :], ACT.Copy).then_inc(sem("vm_hi"), 1)
            if t >= 1:
                act.wait_ge(*after("qm_roped", t))
                act.dma_start(qm_d[P * (t - 1):P * t, :], q_sb[:, (t - 1) % 2].rearrange("p h c -> p (h c)")).then_inc(sem(f"qm_spill{(t - 1) % 2}"), 16)
        act.wait_ge(*after("qm_roped", TT))
        act.dma_start(qm_d[P * (TT - 1):, :], q_sb[:, (TT - 1) % 2].rearrange("p h c -> p (h c)")).then_inc(sem(f"qm_spill{(TT - 1) % 2}"), 16)
        for b in range(2):
            act.wait_ge(*after(f"qm_spill{b}", 16 * TT // 2))
        phase_end(act, "act")

        phase_start(act, "act")
        qm_rows = qm_d.rearrange("(t p) c -> p t c", p=P)

        def head_load(h):
            if h >= 1:
                act.wait_ge(*after("qk_done", 4 * (h - 1) + 2))
            act.dma_start(qm[:], qm_rows[:, :, MLA_QK * h:MLA_QK * h + MLA_QK]).then_inc(sem("qm_back"), 16)

        def head_hi(x):
            h, part = divmod(x, 4)
            sl = slice(COLS * (part % 2), COLS * (part % 2) + COLS)
            act.wait_ge(*after("qk_done", x + 1))
            if h >= 2:
                act.wait_ge(*after("m_scored", TT * (h - 1)))
            dst, n = (Qh, MLA_QK) if part < 2 else (Kh, HD)
            act.activation(dst[0:n, h % 2, sl], ps[0:n, 7, :], ACT.Copy).then_inc(sem("qk_hi"), 1)

        def zm_load(b):
            h, qb = divmod(b, 4)
            if b >= 2:
                act.wait_ge(*after("m_out", b - 1))
            rows = slice(HD * (h % 2), HD * (h % 2) + HD)
            act.dma_start(zm[rows, b % 2, :], zm_d[HD * h:HD * h + HD, 256 * qb:256 * qb + 256]).then_inc(sem(f"zm_in{b % 2}"), 16)

        def am_store(b):
            h, qb = divmod(b, 4)
            act.wait_ge(*after("m_out", b + 1))
            rows = slice(HD * (h % 2), HD * (h % 2) + HD)
            act.dma_start(am_d[HD * h:HD * h + HD, 256 * qb:256 * qb + 256], am[rows, b % 2, :]).then_inc(sem(f"am_out{b % 2}"), 16)

        head_load(0)
        zm_load(0)
        zm_load(1)
        for part in range(4):
            head_hi(part)
        head_load(1)
        for j in range(n_t + 5):
            if j < n_t:
                h, qt = divmod(j, TT)
                if h + 1 < H1 and qt in (2, 3, 4, 5):
                    head_hi(4 * (h + 1) + qt - 2)
                    if qt == 5 and h + 2 < H1:
                        head_load(h + 2)
            if 2 <= j < n_t + 2:
                k = j - 2
                act.wait_ge(*after("m_T", k + 1))
                if k >= 4:
                    act.wait_ge(*after("m_valued", (k - 4) // 2 + 1))
                act.activation(PTh[:, (k // 2) % 2, :, P * (k % 2):P * (k % 2) + P],
                               ps[:, 4:6, :].rearrange("p b (j c) -> p (b j) c", c=P), ACT.Copy).then_inc(sem("m_hi"), 1)
            if j < n_t:
                act.wait_ge(*after("m_max", j + 1))
                act.activation(pm[:, j % 2, :].rearrange("p (b c) -> p b c", b=2), ps[:, 2 * (j % 2):2 * (j % 2) + 2, :], ACT.Exp,
                               bias=rstd[:, j % 8:j % 8 + 1], accum_out=m_sum[:, j % 8:j % 8 + 1]).then_inc(sem("m_exp"), 1)
            if j >= 6 and j % 2 == 0:
                b = (j - 6) // 2
                am_store(b)
                if b + 2 < 4 * H1:
                    zm_load(b + 2)
        for b in range(2):
            act.wait_ge(*after(f"am_out{b}", 16 * 2 * H1))
        phase_end(act, "act")

        phase_start(act, "act")

        def mixer_in(x_):
            if x_ >= 2:
                act.wait_ge(*after("mixers_lo", x_ - 1))
            src = (am_d, dd_d)[x_ // 4]
            act.dma_start(raw[:, x_ % 2, :], src[P * (x_ % 4):P * (x_ % 4) + P, :]).then_inc(sem(f"mixer_in{x_ % 2}"), 16)

        def gates_in(u):
            o, r = divmod(u, 2 * KT)
            n, m_ = divmod(r, KT)
            if u >= 4:
                act.wait_ge(*after("y2_read", u - 3))
            r0 = D * o + P * m_
            act.dma_start(gg[:, u % 4, :], g_d[r0:r0 + P, COLS * n:COLS * n + COLS]).then_inc(sem(f"gates_in{u % 4}"), 16)

        mixer_in(0)
        mixer_in(1)
        for u in range(4):
            gates_in(u)
        for x_ in range(8):
            act.wait_ge(*after(f"mixer_in{x_ % 2}", 16 * (x_ // 2 + 1)))
            act.activation((mh, dh)[x_ // 4][:, x_ % 4, :], raw[:, x_ % 2, :], ACT.Copy).then_inc(sem("mixers_hi"), 1)
            if 1 <= x_ < 7:
                mixer_in(x_ + 1)
        for u in range(4, 2 * KT + 4):
            gates_in(u)
        for u in range(2 * KT):
            n, m_ = divmod(u, KT)
            act.wait_ge(*after("merged", u + 1))
            act.activation(Mh[:, m_, COLS * n:COLS * n + COLS], yg[:], ACT.Copy).then_inc(sem("merged_hi"), 1)
            if u + 4 < 2 * KT:
                gates_in(2 * KT + u + 4)

        out_tok = out[0].rearrange("(t p) d -> t p d", p=P)
        act.wait_ge(*after("y2_done", 4 * KT))
        act.wait_ge(*after("merged_lo", 2 * KT))
        for t in range(TT):
            act.dma_start(xo[:, t, :], x1_tok[t]).then_inc(sem(f"x1_back{t}"), 16)
        act.dma_start(gfin[:], final_norm_g.rearrange("(a d) -> a d", a=1).to_broadcast([P, D])).then_inc(sem("gfin"), 16)

        def out_store(t):
            act.wait_ge(*after("final", t + 1))
            act.dma_start(out_tok[t], fin[:, t % 2, :]).then_inc(sem(f"out_stored{t % 2}"), 16)

        for u in range(2 * TT):
            half, t = divmod(u, TT)
            act.wait_ge(*after("o_read", u + 1))
            if u >= 1:
                act.wait_ge(*after("o_sq", u))
            act.activation(osq[:], xo[:, t, COLS * half:COLS * half + COLS], ACT.Square,
                           accum_out=(ssq, ssq2)[half][:, t:t + 1]).then_inc(sem("o_sq"), 1)
            if half:
                act.wait_ge(*after("o_total", t + 1))
                act.activation(rstd[:, t:t + 1], rstd[:, t:t + 1], ACT.Sqrt, scale=1.0 / D, bias=EPS_C).then_inc(sem("o_root"), 1)
                if t >= 1:
                    out_store(t - 1)
        out_store(TT - 1)
        for b in range(2):
            act.wait_ge(*after(f"out_stored{b}", 16 * TT // 2))

    @block.vector
    def _(dve):
        turns_taken = [0]

        def in_turn(ins):
            ins.then_inc(sem("vector_step"), 1)
            turns_taken[0] += 1
            dve.wait_ge(sem("vector_step"), turns_taken[0])

        nc.vector.memset(EPS_C, EPS).then_inc(sem("zeroed"), 1)
        dve.wait_ge(*after("const", 16 * 8))
        nc.vector.tensor_scalar(sinks_n, sinks_p, -1.0, None, ALU.mult).then_inc(sem("sink_c"), 1)

        def inverse_root(tag, n=1):
            dve.wait_ge(*after(f"{tag}_root", n))

        inverse_root("x")
        nc.vector.reciprocal(rstd, rstd).then_inc(sem("x_rstd"), 1)
        dve.wait_ge(*after("x_rstd", 1))
        for t in range(TT):
            nc.vector.tensor_scalar(xt[:, t, :], xt[:, t, :], rstd[:, t:t + 1], None, ALU.mult).then_inc(sem("x_scaled"), 1)
        for n in range(HALF):
            for k in range(KT):
                u = n * KT + k
                sl = slice(COLS * n, COLS * n + COLS)
                dve.wait_ge(*after("x_hi", u + 1))
                nc.vector.scalar_tensor_tensor(hTl[:, k, sl], ps[:, u % 4, :], gain_pre[:, k:k + 1],
                                               hTh[:, k, sl].bitcast(F32), ALU.mult, ALU.subtract).then_inc(sem("x_evac"), 1)
        phase_end(dve, "dve")

        phase_start(dve, "dve")
        for buf in (uT[:, 0, 0:PAD], uT[:, 1, 0:PAD], sA[:, 0:PAD]):
            nc.vector.memset(buf, 0.0)
        nc.vector.memset(sB[:, 0:PAD], 0.0).then_inc(sem("u_pad"), 1)
        dve.wait_ge(*after("u_pad", 1))
        dve.wait_ge(*after("pool_c", 80))
        def pool_mul(u):
            g, n = divmod(u, 2)
            sl = slice(COLS * n, COLS * n + COLS)
            dve.wait_ge(*after("mix_done", u + 1))
            nc.vector.tensor_scalar(pmT[:, g, sl], ps[:, 4 + u % 2, :], pscale[:, g:g + 1], None,
                                    ALU.mult).then_inc(sem("mix_evac"), 1)

        def pool_finish(g):
            pool_mul(2 * g)
            pool_mul(2 * g + 1)
            for n in range(HALF):
                u = 2 * g + n
                sl = slice(COLS * n, COLS * n + COLS)
                dve.wait_ge(*after("pg_evac", u + 1))
                dve.wait_ge(*after("mix_evac", u + 1))
                nc.vector.tensor_tensor(pmT[:, g, sl], pmT[:, g, sl], sg1[:, u % 2, :], ALU.mult).then_inc(sem("pg_mul"), 1)

        for g, w in enumerate(POOL_W):
            dve.wait_ge(*after("u_evac", 2 * g + 2))
            src, d, bufs = uT[:, g % 2, :], 1, [sA, sB]
            while d < w:
                dst = bufs[0][:]
                in_turn(nc.vector.tensor_tensor(dst[:, PAD:], src[:, PAD:], src[:, PAD - d:PAD + S - d], ALU.add))
                src, d = dst, 2 * d
                bufs.reverse()
            if g >= 2:
                dve.wait_ge(*after("mix_done", 2 * (g - 1)))
            in_turn(nc.vector.scalar_tensor_tensor(pooled[:, g % 2, :], src[:, PAD:], 1.0 / w, uT[:, g % 2, PAD:],
                                                ALU.mult, ALU.subtract))
            in_turn(nc.vector.tensor_tensor(edge_t[:], src[:, PAD:2 * PAD], edge[:, g, :], ALU.mult))
            in_turn(nc.vector.tensor_tensor(pooled[:, g % 2, 0:PAD], edge_t[:], uT[:, g % 2, PAD:2 * PAD], ALU.subtract))
            nc.vector.memset(edge_t[:, 0:1], 0.0).then_inc(sem("pooled"), 1)
            if g >= 1:
                pool_finish(g - 1)
        pool_finish(3)
        phase_end(dve, "dve")

        phase_start(dve, "dve")
        dve.wait_ge(*after("swa_c", 16))
        steps = TT * HH
        def softmax_in(i):
            t, hh = divmod(i, HH)
            hs = slice(G * hh, G * hh + G)
            nk = P if t == 0 else 2 * P
            sc = ps[:, 0:2, :].rearrange("p b (j k) -> p (b j) k", j=2)[:, :, 0:nk]
            dst = pr[:, i % 2, :, 0:nk]
            dve.wait_ge(*after("swa_scored", i + 1))
            if i >= 2:
                dve.wait_ge(*after("swa_T", i - 1))
            nc.vector.tensor_tensor(dst, sc, swa_b[:, hs, 2 * P - nk:2 * P], ALU.add).then_inc(sem("swa_masked"), 1)
            dve.wait_ge(*after("swa_masked", i + 1))
            if t >= 1:
                dve.wait_ge(*after("swa_out", 2 * (t - 1) + hh + 1))
            in_turn(nc.vector.tensor_reduce(st[:, 0, hs], dst, AX_X, ALU.max, negate=True))
            in_turn(nc.vector.tensor_tensor(st[:, 0, hs], st[:, 0, hs], sinks_n[:, hs], ALU.min))
            nc.vector.tensor_tensor(st[:, 3, hs], st[:, 0, hs], sinks_p[:, hs], ALU.add).then_inc(sem("swa_max"), 1)

        def normalise(i):
            t, hh = divmod(i, HH)
            hs = slice(G * hh, G * hh + G)
            dve.wait_ge(*after("swa_valued", i + 1))
            dve.wait_ge(*after("swa_sink", i + 1))
            in_turn(nc.vector.tensor_tensor(st[:, 1, hs], st[:, 1, hs], st[:, 2, hs], ALU.add))
            in_turn(nc.vector.reciprocal(st[:, 1, hs], st[:, 1, hs]))
            if t >= 1:
                dve.wait_ge(*after("swa_backT", t))
            nc.vector.tensor_tensor(ao[:, hs, :], ps[:, 4 + i % 2, 0:256].rearrange("p (h d) -> p h d", d=HD),
                                    st[:, 1, hs].unsqueeze(2).to_broadcast([P, G, HD]), ALU.mult).then_inc(sem("swa_out"), 1)

        def back(t):
            dve.wait_ge(*after("swa_backT", t + 1))
            dve.wait_ge(*after("ag_mul", 2 * t + 4 if t % 2 == 0 else 2 * t + 2))
            dst = aT[:, :, P * t:P * t + P]
            nc.vector.tensor_tensor(dst, ps[:, 6, :].rearrange("p (j c) -> p j c", c=P), dst, ALU.mult).then_inc(sem("swa_aT"), 1)

        def gate_attn(i):
            quarter, m_ = divmod(i, 4)
            dve.wait_ge(*after("ag_evac", i + 1))
            e = sgA[:, i % 2, :]
            in_turn(nc.vector.tensor_scalar(e, e, 1.0, None, ALU.add))
            in_turn(nc.vector.reciprocal(e, e))
            nc.vector.tensor_tensor(aT[:, m_, 2 * P * quarter:2 * P * quarter + 2 * P], ps[:, 7, 0:2 * P], e, ALU.mult).then_inc(sem("ag_mul"), 1)

        for i in range(steps + 3):
            if 2 <= i < steps + 2:
                normalise(i - 2)
            if i < steps:
                softmax_in(i)
            if i >= 4 and i % 2 == 0:
                back((i - 4) // 2)
            if i < steps:
                gate_attn(i)
        phase_end(dve, "dve")

        phase_start(dve, "dve")
        for i, k in enumerate(MIX_ORDER):
            if i == 4:
                dve.wait_ge(*after("pool_back", 64))
            src = pmR[:, k, :] if k < 4 else aT[:, k - 4, :]
            dve.wait_ge(*after("mixT_hi", i + 1))
            nc.vector.tensor_tensor(mTl[:, k, :], src, mTh[:, k, :].bitcast(F32), ALU.subtract).then_inc(sem("mixT_split"), 1)
        dve.wait_ge(*after("mixT_split", KT))
        dve.wait_ge(*after("gpost", 16))

        def x1_scale(t):
            dve.wait_ge(*after("x1_root", t + 1))
            nc.vector.reciprocal(ssq2[:, t:t + 1], ssq2[:, t:t + 1]).then_inc(sem("x1_rstd"), 1)
            dve.wait_ge(*after("x1_rstd", t + 1))
            nc.vector.tensor_scalar(xt2[:, t, :], x1[:, t % 2, :], ssq2[:, t:t + 1], None, ALU.mult).then_inc(sem("x1_scaled"), 1)

        for t in range(TT):
            b = 2 * (t % 2)
            dve.wait_ge(*after("y_root", t + 1))
            nc.vector.reciprocal(rstd[:, t:t + 1], rstd[:, t:t + 1]).then_inc(sem("y_rstd"), 1)
            dve.wait_ge(*after("y_rstd", t + 1))
            nc.vector.scalar_tensor_tensor(yn[:].rearrange("p (b c) -> p b c", b=2), ps[:, b:b + 2, :], rstd[:, t:t + 1],
                                           gpost[:].rearrange("p (b c) -> p b c", b=2), ALU.mult, ALU.mult).then_inc(sem("y_read"), 1)
            dve.wait_ge(*after("y_read", t + 1))
            dve.wait_ge(*after(f"x_back{t % 2}", 16 * (t // 2 + 1)))
            if t >= 2:
                dve.wait_ge(*after(f"x1_out{t % 2}", 16 * (t // 2)))
                dve.wait_ge(*after("x1_scaled", t - 1))
            nc.vector.tensor_tensor(x1[:, t % 2, :], yn[:], xr[:, t % 2, :], ALU.add).then_inc(sem("x1_made"), 1)
            if t >= 1:
                x1_scale(t - 1)
        x1_scale(TT - 1)
        phase_end(dve, "dve")

        phase_start(dve, "dve")
        for n in range(HALF):
            for k in range(KT):
                u = n * KT + k
                sl = slice(COLS * n, COLS * n + COLS)
                dve.wait_ge(*after("x1_hi", u + 1))
                nc.vector.scalar_tensor_tensor(h2l[:, k, sl], ps[:, u % 4, :], gain_2[:, k:k + 1],
                                               h2h[:, k, sl].bitcast(F32), ALU.mult, ALU.subtract).then_inc(sem("x1_evac"), 1)
        phase_end(dve, "dve")

        phase_start(dve, "dve")
        dve.wait_ge(*after("pos_in", 16 * 25))
        in_turn(nc.vector.tensor_copy(posf[:], posi[:]))
        for i in range(3 * TT):
            in_turn(nc.vector.tensor_scalar(ang[:, i, :], freq[:, 0:FREQS], posf[:, i // TT, i % TT:i % TT + 1], None, ALU.mult))
        for t in range(TT):
            in_turn(nc.vector.tensor_scalar(ang[:, 24 + t // 2, 16 * (t % 2):16 * (t % 2) + 16], freq[:, FREQS:],
                                         posf[:, 0, t:t + 1], None, ALU.mult))
        for i, quarter in enumerate((0.0, 0.25)):
            in_turn(nc.vector.tensor_scalar(turn[:], ang[:], 1.0 / TWO_PI, quarter, ALU.mult, ALU.add))
            in_turn(nc.vector.tensor_scalar(turn[:], turn[:], ROUND, None, ALU.add))
            in_turn(nc.vector.tensor_scalar(turn[:], turn[:], ROUND, None, ALU.subtract))
            if i:
                dve.wait_ge(*after("tables", 2))
            src = ang
            for part in TWO_PI_PARTS:
                in_turn(nc.vector.scalar_tensor_tensor(red[:], turn[:], -part, src[:], ALU.mult, ALU.add))
                src = red
            if i:
                in_turn(nc.vector.tensor_scalar(red[:], red[:], TWO_PI / 4, None, ALU.add))
            nc.vector.tensor_scalar(red[:], red[:], PI_IN, -PI_IN, ALU.min, ALU.max).then_inc(sem("angles"), 1)
        dve.wait_ge(*after("tables", 4))
        dve.wait_ge(*after("c_evac", TT))
        r0, hw = C_Q + C_KV, MLA_R // 2
        lo_, hi_ = c_sb[:, :, r0:r0 + hw], c_sb[:, :, r0 + hw:r0 + 2 * hw]
        for i, (a, b) in enumerate(((lo_, cos_m), (hi_, sin_m), (hi_, cos_m), (lo_, sin_m))):
            in_turn(nc.vector.tensor_tensor(c_t[:, i], a, b[:], ALU.mult))
        in_turn(nc.vector.tensor_tensor(lo_, c_t[:, 0], c_t[:, 1], ALU.subtract))
        nc.vector.tensor_tensor(hi_, c_t[:, 2], c_t[:, 3], ALU.add).then_inc(sem("c_roped"), 1)
        dve.wait_ge(*after("c_root", 2))
        in_turn(nc.vector.reciprocal(c_ss[:], c_ss[:]))
        for t in range(TT):
            for i, (c0, w) in enumerate(((0, C_Q), (C_Q, C_KV))):
                nc.vector.tensor_scalar(c_sb[:, t, c0:c0 + w], c_sb[:, t, c0:c0 + w], c_ss[:, i, t:t + 1], None,
                                        ALU.mult).then_inc(sem("c_scaled"), 1)
        phase_end(dve, "dve")

        phase_start(dve, "dve")
        dve.wait_ge(*after("masks_in", 16))

        def rotate(u, r, g, t):
            dve.wait_ge(*after("d_done", u + 1))
            src = ps[:, u % 2, :].rearrange("p (h f) -> p h f", f=FREQS)
            cos, sin = (x_[:, g, t:t + 1, :].to_broadcast([P, 2 * H1, FREQS]) for x_ in (cos_d, sin_d))
            nc.vector.tensor_tensor(rc[:].rearrange("p (h f) -> p h f", f=FREQS), src, cos, ALU.mult).then_inc(sem("rope_cos"), 1)
            nc.vector.tensor_tensor(rs[:].rearrange("p (h f) -> p h f", f=FREQS), src, sin, ALU.mult).then_inc(sem("d_read"), 1)
            dve.wait_ge(*after("rope_cos", r + 1))
            dve.wait_ge(*after("d_read", u + 1))
            if r >= 1:
                dve.wait_ge(*after("rotT", r))
            c4, s4_, o4 = (x_[:].rearrange("p (h a f) -> p h a f", a=2, f=FREQS) for x_ in (rc, rs, rr))
            nc.vector.tensor_tensor(o4[:, :, 0, :], c4[:, :, 0, :], s4_[:, :, 1, :], ALU.subtract).then_inc(sem("rope_half"), 1)
            nc.vector.tensor_tensor(o4[:, :, 1, :], c4[:, :, 1, :], s4_[:, :, 0, :], ALU.add).then_inc(sem("rotated"), 1)
            dve.wait_ge(*after("rotated", r + 1))

        def d_soft(g, i):
            n = d_step(g, i)
            t, hh = divmod(i, HH)
            _, nk, mc, _ = window(g, t)
            dve.wait_ge(*after("d_scored", n + 1))
            if n >= 2:
                dve.wait_ge(*after("d_T", n - 1))
            dst = prd[:, i % 2, :, 0:nk]
            for b in range(2):
                sc = ps[:, 3 + b, :].rearrange("p (j k) -> p j k", j=2)[:, :, 0:nk]
                mask = masks[:, mc:mc + nk].unsqueeze(1).to_broadcast([P, 2, nk])
                last = nc.vector.tensor_tensor(dst[:, b::2, :], sc, mask, ALU.add)
            last.then_inc(sem("d_masked"), 1)
            dve.wait_ge(*after("d_masked", n + 1))
            if i % HH == 0 and (g or t >= 2):
                dve.wait_ge(*after(f"d_store{t % 2}", 16 * ((TT * g + t) // 2)))
            c0 = COLS + G * hh
            nc.vector.tensor_reduce(osb[:, t % 2, c0:c0 + G], dst, AX_X, ALU.max, negate=True).then_inc(sem("d_max"), 1)

        def d_out(g, i):
            n = d_step(g, i)
            t, hh = divmod(i, HH)
            dve.wait_ge(*after("d_valued", n + 1))
            nc.vector.tensor_copy(osb[:, t % 2, 256 * hh:256 * hh + 256], ps[:, 7, 0:256]).then_inc(sem("d_out"), 1)

        for slot in range(D_SLOTS):
            done = unit_before(slot)
            if done and done[3] != "v":
                u, r, g, kind, t = done
                if kind == "q" and t == 0:
                    dve.wait_ge(*after("d_read", u))
                rotate(u, r, g, t)
            if slot in step_at:
                d_soft(*step_at[slot])
            if slot - 2 in step_at:
                d_out(*step_at[slot - 2])
        phase_end(dve, "dve")

        phase_start(dve, "dve")
        dve.wait_ge(*after("stats_in", 48))
        nm = [stats[:, g, :, 0:H1] for g in range(3)]
        den = [stats[:, g, :, H1:] for g in range(3)]
        in_turn(nc.vector.tensor_tensor(joint[:], nm[0], nm[1], ALU.min))
        in_turn(nc.vector.tensor_tensor(joint[:], joint[:], nm[2], ALU.min))
        for g in range(3):
            nc.vector.tensor_tensor(coef[:, g], joint[:], nm[g], ALU.subtract).then_inc(sem("coef_arg"), 1)
        dve.wait_ge(*after("coef_exp", 3))
        for g in range(3):
            in_turn(nc.vector.tensor_tensor(den[g], den[g], coef[:, g], ALU.mult))
        in_turn(nc.vector.tensor_tensor(dsum[:], den[0], den[1], ALU.add))
        in_turn(nc.vector.tensor_tensor(dsum[:], dsum[:], den[2], ALU.add))
        in_turn(nc.vector.reciprocal(dsum[:], dsum[:]))
        for g in range(3):
            in_turn(nc.vector.tensor_tensor(coef[:, g], coef[:, g], dsum[:], ALU.mult))
        dve.wait_ge(*after("zd_in", 64))

        def gate(t):
            dve.wait_ge(*after("jointT", t + 1))
            nc.vector.tensor_tensor(dgT[:, :, P * t:P * t + P], ps[:, 4 + t % 2, :].rearrange("p (j c) -> p j c", c=P),
                                    zdT[:, :, P * t:P * t + P], ALU.mult).then_inc(sem("dg_done"), 1)

        for t in range(TT):
            dve.wait_ge(*after(f"nums_in{t % 2}", 48 * (t // 2 + 1)))
            if t >= 1:
                dve.wait_ge(*after("jointT", t))
            for g in range(3):
                nc.vector.tensor_tensor(wsum[:, g, :].rearrange("p (h d) -> p h d", d=HD),
                                        nums[:, t % 2, g, :].rearrange("p (h d) -> p h d", d=HD),
                                        coef[:, g, t, :].unsqueeze(2).to_broadcast([P, H1, HD]), ALU.mult).then_inc(sem("weighted"), 1)
            dve.wait_ge(*after("weighted", 3 * t + 3))
            in_turn(nc.vector.tensor_tensor(wsum[:, 0, :], wsum[:, 0, :], wsum[:, 1, :], ALU.add))
            nc.vector.tensor_tensor(wsum[:, 0, :], wsum[:, 0, :], wsum[:, 2, :], ALU.add).then_inc(sem("joint"), 1)
            dve.wait_ge(*after("joint", t + 1))
            gate(t)
        phase_end(dve, "dve")

        phase_start(dve, "dve")
        for u, (n, kind) in enumerate(C_UNITS):
            sl = slice(COLS * n, COLS * n + COLS)
            dve.wait_ge(*after("cT_hi", u + 1))
            if kind < 2:
                last = nc.vector.scalar_tensor_tensor(cql[:, kind, sl], ps[:, u % 4, :], gain_q[:, kind:kind + 1],
                                                      cqh[:, kind, sl].bitcast(F32), ALU.mult, ALU.subtract)
            elif kind == 2:
                last = nc.vector.scalar_tensor_tensor(ckl[:, sl], ps[:, u % 4, :], gain_kv, ckh[:, sl].bitcast(F32),
                                                      ALU.mult, ALU.subtract)
            else:
                for b in range(2):
                    last = nc.vector.tensor_tensor(Kl[HD:MLA_QK, b, sl], ps[HD:MLA_QK, u % 4, :],
                                                   Kh[HD:MLA_QK, b, sl].bitcast(F32), ALU.subtract)
            last.then_inc(sem("cT_lo"), 1)
        dve.wait_ge(*after("rope_back", 32))
        for t in range(TT):
            dve.wait_ge(*after("qm_read", 2 * t + 2))
            q_lo, q_hi = q_sb[:, t % 2, :, HD:HD + hw], q_sb[:, t % 2, :, HD + hw:]
            cos, sin = (x_[:, t:t + 1, :].to_broadcast([P, H1, hw]) for x_ in (cos_q, sin_q))
            for i, (a, b) in enumerate(((q_lo, cos), (q_hi, sin), (q_hi, cos), (q_lo, sin))):
                in_turn(nc.vector.tensor_tensor(q_t[:, i], a, b, ALU.mult))
            in_turn(nc.vector.tensor_tensor(q_lo, q_t[:, 0], q_t[:, 1], ALU.subtract))
            nc.vector.tensor_tensor(q_hi, q_t[:, 2], q_t[:, 3], ALU.add).then_inc(sem("qm_roped"), 1)
            dve.wait_ge(*after("vm_hi", t + 1))
            nc.vector.tensor_tensor(Vl[:, t, :], ps[:, 4 + t % 2, :], Vh[:, t, :].bitcast(F32), ALU.subtract).then_inc(sem("vm_lo"), 1)
        phase_end(dve, "dve")

        phase_start(dve, "dve")

        def head_lo(x_):
            h, part = divmod(x_, 4)
            sl = slice(COLS * (part % 2), COLS * (part % 2) + COLS)
            dve.wait_ge(*after("qk_hi", x_ + 1))
            dst, hi, n = (Ql, Qh, MLA_QK) if part < 2 else (Kl, Kh, HD)
            nc.vector.tensor_tensor(dst[0:n, h % 2, sl], ps[0:n, 7, :], hi[0:n, h % 2, sl].bitcast(F32),
                                    ALU.subtract).then_inc(sem("qk_lo"), 1)

        def m_out(b):
            h, qb = divmod(b, 4)
            rows = slice(HD * (h % 2), HD * (h % 2) + HD)
            dve.wait_ge(*after("m_valued", b + 1))
            dve.wait_ge(*after(f"zm_in{b % 2}", 16 * (b // 2 + 1)))
            if b >= 2:
                dve.wait_ge(*after(f"am_out{b % 2}", 16 * (b // 2)))
            nc.vector.tensor_tensor(am[rows, b % 2, :], ps[rows, 6, 0:256], zm[rows, b % 2, :], ALU.mult).then_inc(sem("m_out"), 1)

        for x_ in range(4):
            head_lo(x_)
        for j in range(n_t + 5):
            if 3 <= j < n_t + 3:
                k = j - 3
                dve.wait_ge(*after("m_hi", k + 1))
                dst = (slice(None), (k // 2) % 2, slice(None), slice(P * (k % 2), P * (k % 2) + P))
                nc.vector.tensor_tensor(PTl[dst], ps[:, 4:6, :].rearrange("p b (j c) -> p (b j) c", c=P),
                                        PTh[dst].bitcast(F32), ALU.subtract).then_inc(sem("m_lo"), 1)
            if j < n_t:
                dve.wait_ge(*after("m_scored", j + 1))
                if j >= 8:
                    dve.wait_ge(*after("m_exp", j - 7))
                nc.vector.tensor_reduce(rstd[:, j % 8:j % 8 + 1], ps[:, 2 * (j % 2):2 * (j % 2) + 2, :].rearrange("p b c -> p (b c)"),
                                        AX_X, ALU.max, negate=True).then_inc(sem("m_max"), 1)
            if 1 <= j <= n_t:
                k = j - 1
                dve.wait_ge(*after("m_exp", k + 1))
                total = m_sum[:, k % 8:k % 8 + 1]
                nc.vector.reciprocal(total, total).then_inc(sem("m_recip"), 1)
                dve.wait_ge(*after("m_recip", k + 1))
                nc.vector.tensor_scalar(pm[:, k % 2, :], pm[:, k % 2, :], total, None, ALU.mult).then_inc(sem("m_normed"), 1)
            if j < n_t:
                h, qt = divmod(j, TT)
                if h + 1 < H1 and qt in (2, 3, 4, 5):
                    head_lo(4 * (h + 1) + qt - 2)
            if j >= 6 and j % 2 == 0:
                m_out((j - 6) // 2)
        phase_end(dve, "dve")

        phase_start(dve, "dve")
        for x_ in range(8):
            dve.wait_ge(*after("mixers_hi", x_ + 1))
            hi, lo = ((mh, ml), (dh, dl))[x_ // 4]
            nc.vector.tensor_tensor(lo[:, x_ % 4, :], raw[:, x_ % 2, :], hi[:, x_ % 4, :].bitcast(F32), ALU.subtract).then_inc(sem("mixers_lo"), 1)
        for u in range(4 * KT):
            o, r = divmod(u, 2 * KT)
            n, m_ = divmod(r, KT)
            sl = slice(COLS * n, COLS * n + COLS)
            dve.wait_ge(*after("y2_done", u + 1))
            dve.wait_ge(*after(f"gates_in{u % 4}", 16 * (u // 4 + 1)))
            if o == 0:
                nc.vector.tensor_tensor(ym[:, m_, sl], ps[:, u % 8, :], gg[:, u % 4, :], ALU.mult).then_inc(sem("y2_read"), 1)
                continue
            if r == 0:
                dve.wait_ge(*after("y2_read", 2 * KT))
            if r >= 1:
                dve.wait_ge(*after("merged_lo", r))
            nc.vector.tensor_tensor(yg[:], ps[:, u % 8, :], gg[:, u % 4, :], ALU.mult).then_inc(sem("y2_read"), 1)
            dve.wait_ge(*after("y2_read", u + 1))
            nc.vector.tensor_tensor(yg[:], yg[:], ym[:, m_, sl], ALU.add).then_inc(sem("merged"), 1)
            dve.wait_ge(*after("merged_hi", r + 1))
            nc.vector.tensor_tensor(Ml[:, m_, sl], yg[:], Mh[:, m_, sl].bitcast(F32), ALU.subtract).then_inc(sem("merged_lo"), 1)

        for u in range(2 * TT):
            half, t = divmod(u, TT)
            sl = slice(COLS * half, COLS * half + COLS)
            dve.wait_ge(*after("o_done", u + 1))
            dve.wait_ge(*after(f"x1_back{t}", 16))
            nc.vector.tensor_tensor(xo[:, t, sl], ps[:, u % 8, :], xo[:, t, sl], ALU.add).then_inc(sem("o_read"), 1)
            if half:
                dve.wait_ge(*after("o_sq", u + 1))
                nc.vector.tensor_tensor(rstd[:, t:t + 1], ssq[:, t:t + 1], ssq2[:, t:t + 1], ALU.add).then_inc(sem("o_total"), 1)
                dve.wait_ge(*after("o_root", t + 1))
                nc.vector.reciprocal(rstd[:, t:t + 1], rstd[:, t:t + 1]).then_inc(sem("o_rstd"), 1)
                dve.wait_ge(*after("o_rstd", t + 1))
                if t == 0:
                    dve.wait_ge(*after("gfin", 16))
                if t >= 2:
                    dve.wait_ge(*after(f"out_stored{t % 2}", 16 * (t // 2)))
                nc.vector.scalar_tensor_tensor(fin[:, t % 2, :], xo[:, t, :], rstd[:, t:t + 1], gfin[:], ALU.mult, ALU.mult).then_inc(sem("final"), 1)

    ctx.close()


_INS = ["x", "w_in", "pool_w", "pool_scale", "attn_sinks", "w_out", "norm_pre", "norm_post", "positions_2",
        "attn_norm_g_2", "w_in_2", "b_gate_2", "mla_q_norm_g_2", "mla_kv_norm_g_2", "w_uq_2", "w_ukv_2",
        "w_o_mla_2", "w_o_dil_2", "w_out_2", "final_norm_g_2"]


def kernel(**inputs):
    import concourse.bacc as bacc
    from concourse.bass_utils import run_bass_kernel_spmd

    nc = bacc.Bacc("TRN2", target_bir_lowering=False, num_devices=1)
    arrays, args = {}, []
    for name in _INS:
        arrays[f"in_{name}"] = np.ascontiguousarray(inputs[name])
    arrays.update(constants())
    for name, a in arrays.items():
        args.append(nc.dram_tensor(name, a.shape, mybir.dt.from_np(a.dtype), kind="ExternalInput").ap())
    out = nc.dram_tensor("out_0", (1, S, D), F32, kind="ExternalOutput").ap()
    hybrid_blocks_kernel(nc, *args, out)
    r = run_bass_kernel_spmd(nc, [arrays], core_ids=[0])
    return r.results[0]["out_0"]
```

```python
from contextlib import ExitStack

import concourse.bass as bass
import numpy as np
from concourse import mybir

F32 = mybir.dt.float32
F32R = mybir.dt.float32r
I32 = mybir.dt.int32
ALU = mybir.AluOpType
ACT = mybir.ActivationFunctionType
AX_X = mybir.AxisListType.X

P = 128
S = 1024
D = 1024
KT = D // P
TT = S // P
COLS = 512
HALF = S // COLS
EPS = 1e-6
NEG = -1e30
H1 = 8
HD = 64
POOL_W = (2, 4, 8, 16)
PAD = 16
G = 4
HH = H1 // G
MASK_W = 3 * P
FREQS = 32
MLA_R = 32
MLA_QK = 96
C_Q, C_KV = 256, 128
C_W = C_Q + C_KV + MLA_R
DIL_QKV = 1536
DILATIONS = (1, 4, 16)
STAT = 2 * H1
CHUNK_K = 2
STAGE = 2
TWO_PI = 6.283185307179586
TWO_PI_PARTS = (6.28125, 0.0019350051879882812, 3.019915981956752e-07)
PI_IN = 3.1415925
ROUND = 12582912.0


def constants():
    q = np.arange(P)[:, None]
    c = np.arange(2 * P)[None, :]
    dist = (q + P - c).astype(np.float32)
    slopes = np.exp2(-8.0 * np.arange(1, H1 + 1, dtype=np.float32) / H1).astype(np.float32)
    valid = (dist >= 0) & (dist < P)
    swa = np.where(valid[:, None, :], -slopes[None, :, None] * dist[:, None, :], np.float32(NEG))
    j = np.arange(MASK_W)[None, :]
    band = np.where(np.abs(j - P - q) <= HD, 0.0, NEG)
    k = np.arange(P)[None, :]
    pairs = np.where(q % 2 == k % 2, 0.0, NEG)
    n = np.arange(PAD)
    inv = np.stack([1.0 / np.minimum(n + 1, w) for w in POOL_W])
    f32 = 10000.0 ** (-np.arange(0, HD, 2, dtype=np.float32) / np.float32(HD))
    f16 = 10000.0 ** (-np.arange(0, MLA_R, 2, dtype=np.float32) / np.float32(MLA_R))
    return {
        "c_swa": np.ascontiguousarray(swa.reshape(P, -1), np.float32),
        "c_mask": np.ascontiguousarray(np.concatenate([band, pairs], 1), np.float32),
        "c_inv": np.ascontiguousarray(inv, np.float32),
        "c_freq": np.ascontiguousarray(np.concatenate([f32, f16])[None, :], np.float32),
        "c_ident": np.eye(P, dtype=np.float32),
    }


def hybrid_blocks_kernel(nc, x, w_in, pool_w, pool_scale, attn_sinks, w_out, norm_pre, norm_post,
                         positions, attn_norm_g, w_in_2, b_gate, q_norm_g, kv_norm_g, w_uq, w_ukv,
                         w_o_mla, w_o_dil, w_out_2, final_norm_g,
                         c_swa, c_mask, c_inv, c_freq, c_ident, out):
    ctx = ExitStack()
    sems = {}
    shared = {
        "product_done": (("u_done", 8), ("pg_done", 8), ("qkv_done", 12), ("ag_done", 16), ("y_done", TT),
                         ("c_done", TT), ("g_done", 48), ("qm_done", 2 * TT), ("y2_done", 4 * KT), ("o_done", 2 * TT)),
        "product_copied": (("u_evac", 8), ("pg_evac", 8), ("qkv_evac", 12), ("ag_evac", 16), ("c_evac", TT), ("g_evac", 48)),
        "product_used": (("pg_mul", 8), ("ag_mul", 16), ("y_read", TT), ("qm_read", 2 * TT), ("y2_read", 4 * KT), ("o_read", 2 * TT)),
        "input_transposed": (("x_T", 16), ("x1_T", 16), ("cT", 8)),
        "input_high": (("x_hi", 16), ("x1_hi", 16), ("cT_hi", 8)),
        "input_split": (("x_evac", 16), ("x1_evac", 16), ("cT_lo", 8)),
        "rows_scaled": (("x_scaled", TT), ("x1_scaled", TT), ("c_scaled", 2 * TT)),
        "squared": (("x_sq", TT), ("y_sq", TT), ("c_sqd", 2 * TT), ("o_sq", 2 * TT)),
        "rooted": (("x_root", TT), ("y_root", TT), ("c_root", 2), ("o_root", TT)),
        "inverted": (("x_rstd", TT), ("y_rstd", TT), ("o_rstd", TT)),
        "scored": (("swa_scored", 16), ("d_scored", 48)),
        "masked": (("swa_masked", 16), ("d_masked", 48)),
        "row_max": (("swa_max", 16), ("d_max", 48)),
        "exponentials": (("swa_exp", 64), ("d_exp", 192)),
        "probs_transposed": (("swa_T", 16), ("d_T", 48)),
        "probs_copied": (("swa_pT", 16), ("d_pT", 48)),
        "values_summed": (("swa_valued", 16), ("d_valued", 48)),
        "values_copied": (("swa_out", 16), ("d_out", 48)),
        "high_part": (("mixT_hi", KT), ("vm_hi", TT), ("mixers_hi", 8)),
        "low_part": (("mixT_split", KT), ("vm_lo", TT), ("mixers_lo", 8)),
        "pool_in_out": (("pool_c", 80), ("pool_spill", 64), ("pool_back", 64)),
    }
    for t in range(TT):
        shared[f"rows_in{t}"] = ((f"x_in{t}", 16),)
    for b in range(2):
        shared[f"x_tile_in{b}"] = ((f"x_back{b}", 64), (f"x1_back{b}", 64))
        shared[f"tile_out{b}"] = ((f"x1_out{b}", 64), (f"d_store{b}", 192), (f"qm_spill{b}", 64))
    alias = {}
    for own, users in shared.items():
        base = 0
        for name, count in users:
            alias[name] = own, base
            base += count

    def sem(name):
        name = alias.get(name, (name, 0))[0]
        if name not in sems:
            sems[name] = ctx.enter_context(nc.semaphore(name))
        return sems[name]

    def after(name, count):
        return sem(name), alias.get(name, (name, 0))[1] + count

    w1 = w_in[0].rearrange("(k p) n -> p k n", p=P)
    w2 = w_in_2[0].rearrange("(k p) n -> p k n", p=P)
    wo1 = w_out[0].rearrange("(k p) n -> p k n", p=P)
    wo2 = w_out_2[0].rearrange("(k p) n -> p k n", p=P)

    def panel(w, c0, n=COLS):
        return [(k, n, w[:, k:k + CHUNK_K, c0:c0 + n]) for k in range(0, KT, CHUNK_K)]

    off2 = np.cumsum([0, C_Q, C_KV, MLA_R, 512, DIL_QKV, DIL_QKV, DIL_QKV, 512, D, D]).tolist()
    o_c, _, _, o_zm, o_q, o_k, o_v, o_zd, o_gm, o_gd, _ = off2
    panels = []
    index = {}

    def add(name, chunks):
        index[name] = len(panels)
        panels.append(chunks)

    add("u", panel(w1, 0))
    add("pgate", panel(w1, 512))
    add("q", panel(w1, 1024))
    add("kv", panel(w1, 1536, 256))
    add("agate", panel(w1, 1792))
    add("o0", panel(wo1, 0))
    add("o1", panel(wo1, 512))
    add("c", panel(w2, o_c, C_W))
    add("zm", panel(w2, o_zm))
    add("zd", panel(w2, o_zd))
    for g in range(3):
        add(f"k{g}", panel(w2, o_k + COLS * g))
        add(f"v{g}", panel(w2, o_v + COLS * g))
        add(f"q{g}", panel(w2, o_q + COLS * g))
    for i in range(2):
        add(f"gm{i}", panel(w2, o_gm + COLS * i))
    for i in range(2):
        add(f"gd{i}", panel(w2, o_gd + COLS * i))
    uq = w_uq[0].rearrange("(k p) n -> p k n", p=P)
    ukv = w_ukv[0].rearrange("p (k n) -> p k n", k=2)
    add("mla", [(0, 384, uq[:, :, 0:384]), (2, 384, uq[:, :, 384:768]), (4, 512, ukv)])
    for name, w in (("od", w_o_dil), ("om", w_o_mla)):
        wk = w[0].rearrange("(k p) n -> p k n", p=P)
        add(name, [(4 * n + k, COLS, wk[:, k:k + 2, COLS * n:COLS * n + COLS])
                   for n in range(2) for k in (0, 2)])
    add("p0", panel(wo2, 0))
    add("p1", panel(wo2, 512))
    chunk_end = np.cumsum([len(p) for p in panels]).tolist()

    x1_d = nc.dram_tensor("x1_scr", [S, D], F32, kind="Internal").ap()
    pool_d = nc.dram_tensor("pool_scr", [512, S], F32, kind="Internal").ap()
    zm_d = nc.dram_tensor("zm_scr", [512, S], F32, kind="Internal").ap()
    zd_d = nc.dram_tensor("zd_scr", [512, S], F32, kind="Internal").ap()
    g_d = nc.dram_tensor("gate_scr", [2 * D, S], F32, kind="Internal").ap()
    rope_d = nc.dram_tensor("rope_scr", [P, 2 * TT * MLA_R // 2], F32, kind="Internal").ap()
    c_d = nc.dram_tensor("c_scr", [S, C_W], F32, kind="Internal").ap()
    qm_d = nc.dram_tensor("qmla_scr", [S, H1 * MLA_QK], F32, kind="Internal").ap()
    am_d = nc.dram_tensor("amla_scr", [512, S], F32, kind="Internal").ap()
    dd_d = nc.dram_tensor("dilout_scr", [512, S], F32, kind="Internal").ap()
    dil_d = [nc.dram_tensor(f"dil{g}_scr", [S, 512 + STAT], F32, kind="Internal").ap()
             for g in range(3)]

    def sb(name, shape, dt=F32, scope=ctx):
        return scope.enter_context(nc.sbuf_tensor(name, shape, dt))

    ps = ctx.enter_context(nc.psum_tensor("ps", [P, 8, COLS], F32))
    ident = sb("ident", [P, P])
    stage = sb("w_stage", [P, STAGE, CHUNK_K, COLS])
    wh = sb("w_hi", [P, 2, KT, COLS], F32R)
    wl = sb("w_lo", [P, 2, KT, COLS], F32R)
    small = sb("small", [P, 88])
    EPS_C = small[:, 87:88]
    ssq, rstd = small[:, 0:8], small[:, 8:16]
    gain_pre, pscale = small[:, 16:24], small[:, 24:28]
    gain_2 = small[:, 28:36]
    gain_q, gain_kv = small[:, 36:38], small[:, 38:39]
    bgate = small[:, 40:56]
    sinks_n = small[:, 56:64]
    sinks_p = small[:, 64:72]
    ssq2 = small[:, 72:80]

    with ExitStack() as s_pool:
        pmT = sb("pool_outT", [P, 4, S], F32, s_pool)
    keep = ExitStack()
    aT = sb("attn_outT", [P, 4, S], F32, keep)
    a1 = ExitStack()
    hTh = sb("h1T_hi", [P, KT, S], F32R, a1)
    hTl = sb("h1T_lo", [P, KT, S], F32R, a1)
    s0 = ExitStack()
    xt = sb("x_tiles", [P, TT, D], F32, s0)
    junk = sb("x_sq", [P, D], F32, s0)
    s0.close()
    s1 = ExitStack()
    uT = sb("uT", [P, 4, PAD + S], F32, s1)
    sA = sb("wsumA", [P, PAD + S], F32, s1)
    sB = sb("wsumB", [P, PAD + S], F32, s1)
    pooled = sb("pooled", [P, 2, S], F32, s1)
    edge = sb("pool_edge", [P, 4, PAD], F32, s1)
    edge_t = sb("pool_edge_t", [P, PAD], F32, s1)
    pool_wt = sb("pool_wt", [P, 4, P], F32, s1)
    sg1 = sb("silu_pool", [P, 2, COLS], F32, s1)
    s1.close()
    s2 = ExitStack()
    qT = sb("q1T", [P, 4, S], F32, s2)
    kT = sb("k1T", [P, S], F32, s2)
    vT = sb("v1T", [P, S], F32, s2)
    v1 = sb("v1", [P, TT, P], F32, s2)
    swa_b = sb("swa_bias", [P, H1, 2 * P], F32, s2)
    pr = sb("probs", [P, 2, G, 2 * P], F32, s2)
    pT = sb("probsT", [P, 2 * G, P], F32, s2)
    ao = sb("attn_tok", [P, H1, HD], F32, s2)
    st = sb("attn_stats", [P, 2, 4, H1], F32, s2)
    sgA = sb("exp_attn_gate", [P, 2, 2 * P], F32, s2)
    s2.close()
    a1.close()
    a2 = ExitStack()
    pmR = sb("pool_outT_back", [P, 4, S], F32, a2)
    mTh = sb("mixT_hi", [P, KT, S], F32R, a2)
    mTl = sb("mixT_lo", [P, KT, S], F32R, a2)
    xr = sb("x_back", [P, 2, D], F32, a2)
    yn = sb("y_normed", [P, D], F32, a2)
    ysq = sb("y_sq", [P, D], F32, a2)
    x1 = sb("x1_tile", [P, 2, D], F32, a2)
    gpost = sb("gain_post", [P, D], F32, a2)
    a2.close()
    keep.close()

    b1 = ExitStack()
    xt2 = sb("x1_normed", [P, TT, D], F32, b1)
    h2h = sb("h2T_hi", [P, KT, S], F32R, b1)
    h2l = sb("h2T_lo", [P, KT, S], F32R, b1)
    tab = ExitStack()
    cos_d = sb("cos_dil", [P, 3, TT, FREQS], F32, tab)
    sin_d = sb("sin_dil", [P, 3, TT, FREQS], F32, tab)
    cos_m = sb("cos_mla", [P, TT, MLA_R // 2], F32, tab)
    sin_m = sb("sin_mla", [P, TT, MLA_R // 2], F32, tab)
    s5 = ExitStack()
    posi = sb("positions", [P, 3, TT], I32, s5)
    posf = sb("positions_f", [P, 3, TT], F32, s5)
    freq = sb("freqs", [P, FREQS + MLA_R // 2], F32, s5)
    ang = sb("angles", [P, 28, FREQS], F32, s5)
    turn = sb("turns", [P, 28, FREQS], F32, s5)
    red = sb("reduced", [P, 28, FREQS], F32, s5)
    c_sb = sb("c_tok", [P, TT, C_W], F32, s5)
    c_sq = sb("c_sq", [P, C_Q], F32, s5)
    c_ss = sb("c_ss", [P, 2, TT], F32, s5)
    c_t = sb("c_rope_t", [P, 4, TT, MLA_R // 2], F32, s5)
    s5.close()
    s8 = ExitStack()
    vd = sb("v_dil", [P, TT + 1, COLS], F32, s8)
    rc = sb("rope_cos_part", [P, COLS], F32, s8)
    rs = sb("rope_sin_part", [P, COLS], F32, s8)
    rr = sb("rope_out", [P, COLS], F32, s8)
    osb = sb("dil_out", [P, 2, COLS + STAT], F32, s8)
    masks = sb("masks", [P, MASK_W + P], F32, s8)
    s8.close()
    tab.close()
    s9 = ExitStack()
    gt2 = sb("gate_tiles_2", [P, 4, S], F32, s9)
    s9b = ExitStack()
    c_bk = sb("c_back", [P, TT, C_W], F32, s9b)
    cos_q = sb("cos_mla_q", [P, TT, MLA_R // 2], F32, s9b)
    sin_q = sb("sin_mla_q", [P, TT, MLA_R // 2], F32, s9b)
    s9b.close()
    dgT = sb("dil_gatedT", [P, 4, S], F32, s9)
    wsum = sb("dil_weighted", [P, 3, COLS], F32, s9)
    s9.close()
    b1.close()
    s7 = ExitStack()
    gt = sb("gate_tiles", [P, 4, S], F32, s7)
    s7.close()
    s8 = ExitStack()
    kTd = sb("kT_dil", [P, 4, S], F32, s8)
    qTd = sb("qT_dil", [P, 2, 4, P], F32, s8)
    prd = sb("probs_dil", [P, 2, G, 2 * P], F32, s8)
    pTd = sb("probsT_dil", [P, 2 * G, P], F32, s8)
    s8.close()
    s9 = ExitStack()
    zdT = sb("z_dilT", [P, 4, S], F32, s9)
    nums = sb("dil_nums", [P, 2, 3, COLS], F32, s9)
    stats = sb("dil_stats", [P, 3, TT, STAT], F32, s9)
    coef = sb("dil_coef", [P, 3, TT, H1], F32, s9)
    joint = sb("dil_joint", [P, TT, H1], F32, s9)
    dsum = sb("dil_sum", [P, TT, H1], F32, s9)
    s9.close()
    b2 = ExitStack()
    cqh, cql = (sb(f"cqT_{x}", [P, 2, S], F32R, b2) for x in ("hi", "lo"))
    ckh, ckl = (sb(f"ckvT_{x}", [P, S], F32R, b2) for x in ("hi", "lo"))
    Kh, Kl = (sb(f"kT_mla_{x}", [MLA_QK, 2, S], F32R, b2) for x in ("hi", "lo"))
    V2 = sb("v_mla", [P, TT, H1, 2, HD], F32R, b2)
    s10 = ExitStack()
    q_sb = sb("q_tok", [P, 2, H1, MLA_QK], F32, s10)
    q_t = sb("q_rope_t", [P, 4, H1, MLA_R // 2], F32, s10)
    s10.close()
    Qh, Ql = (sb(f"qT_mla_{x}", [MLA_QK, 2, S], F32R, b2) for x in ("hi", "lo"))
    PTh, PTl = (sb(f"pT_mla_{x}", [P, 2, TT, 2 * P], F32R, b2) for x in ("hi", "lo"))
    pm = sb("p_mla", [P, 2, S], F32, b2)
    am = sb("a_mla", [P, 2, 2 * P], F32, b2)
    zm = sb("z_mlaT", [P, 2, 2 * P], F32, b2)
    qm = sb("q_tok_back", [P, TT, MLA_QK], F32, b2)
    b2.close()
    b3 = ExitStack()
    Mh, Ml = (sb(f"mergedT_{x}", [P, KT, S], F32R, b3) for x in ("hi", "lo"))
    s11 = ExitStack()
    ah, al = (sb(f"mlaT_{x}", [P, 4, S], F32R, s11) for x in ("hi", "lo"))
    raw = sb("mixersT", [P, 2, S], F32, s11)
    gg = sb("gates", [P, 4, COLS], F32, s11)
    yg = sb("y_gated", [P, COLS], F32, s11)
    s11.close()
    s12 = ExitStack()
    xo = sb("block_out", [P, TT, D], F32, s12)
    osq = sb("block_out_sq", [P, COLS], F32, s12)
    fin = sb("final", [P, 2, D], F32, s12)
    gfin = sb("gain_final", [P, D], F32, s12)
    s12.close()
    b3.close()
    s13 = ExitStack()
    dh, dl = (sb(f"dilT_{x}", [P, 4, S], F32R, s13) for x in ("hi", "lo"))
    yd = sb("y_dil_gated", [P, KT, S], F32, s13)
    s13.close()

    JOINT_LAG, JOINT_STEP = 6, 3
    LAST_JOINT = 16 + JOINT_LAG + JOINT_STEP * (TT - 1) + 2
    MIX_ORDER = (4, 5, 6, 7, 0, 1, 2, 3)
    GATES = (("zm", "zd"), ("gm0", "gm1", "gd0", "gd1"))
    C_KINDS = ((0, P), (P, P), (C_Q, P), (C_W - MLA_QK, MLA_QK))
    C_UNITS = [(n, kind) for n in range(HALF) for kind in range(4)]

    def tile_start(g, t):
        return ((P * t, 1), (t // 2 + 4 * P * (t % 2), 4), (t, 8))[g]

    def spread(start, step):
        return lambda h, k: h[:, k, start:start + step * (P - 1) + 1:step]

    def group_toks(g, t):
        return spread(*tile_start(g, t))

    def value_tiles(g):
        if g:
            return [(t, group_toks(g, t)) for t in range(TT)]
        starts = [0] + [P * t - HD for t in range(1, TT)] + [S - P]
        return [(t, spread(s_, 1)) for t, s_ in enumerate(starts)]

    def window(g, t):
        if g == 2:
            return P * t, P, MASK_W, [(0, P, t, 0, P)]
        if g == 1:
            first = t - t % 2
            return P * first, 2 * P, P * (1 - t % 2), [(0, P, first, 0, P), (P, P, first + 1, 0, P)]
        if t == 0:
            return 0, 3 * HD, P, [(0, HD, 0, 0, HD), (HD, P, 1, 0, P)]
        if t == TT - 1:
            return S - 3 * HD, 3 * HD, HD, [(0, P, t, 0, P), (HD, P, t + 1, HD, HD)]
        return P * t - HD, 2 * P, HD, [(0, P, t, 0, P), (P, P, t + 1, 0, P)]

    n_t = H1 * TT
    m_sum = ssq

    def d_step(g, i):
        return HH * TT * g + i

    D_UNITS = [(g, kind, t) for g in range(3) for kind in "kvq"
               for t in range(len(value_tiles(g)) if kind == "v" else TT)]
    D_SLOTS = 2 * len(D_UNITS) + 6
    step_at = {2 * u + 3 + hh: (g, HH * t + hh)
               for u, (g, kind, t) in enumerate(D_UNITS) if kind == "q" for hh in range(HH)}

    def unit_before(slot):
        u = slot // 2 - 1
        if slot % 2 or not 0 <= u < len(D_UNITS):
            return None
        g, kind, t = D_UNITS[u]
        return u, sum(k != "v" for _, k, _ in D_UNITS[:u]), g, kind, t

    block = ctx.enter_context(nc.Block())
    ENG = ("pe", "act", "dve")
    phases = {who: 0 for who in ENG}

    def phase_end(e, who):
        e.drain().then_inc(sem(f"through_{who}"), 1)
        phases[who] += 1

    def phase_start(e, who):
        for other in ENG:
            if other != who:
                e.wait_ge(*after(f"through_{other}", phases[who]))

    @block.sync
    def _(sp):
        n = 0
        for chunks in panels:
            for k, cols, src in chunks:
                if n >= STAGE:
                    sp.wait_ge(*after("w_split", n - STAGE + 1))
                sp.dma_start(stage[:, n % STAGE, :, 0:cols], src).then_inc(sem(f"w_landed{n % STAGE}"), 16)
                n += 1

    @block.gpsimd
    def _(pool):
        n = 0
        for p, chunks in enumerate(panels):
            if p == index["om"]:
                for k in range(n_t):
                    pool.wait_ge(*after("m_recip", k + 1))
                    nc.gpsimd.tensor_scalar(pm[:, k % 2, :], pm[:, k % 2, :], m_sum[:, k % 8:k % 8 + 1], 0.0,
                                            ALU.mult, ALU.add).then_inc(sem("m_normed"), 1)
            if p >= 2:
                pool.wait_ge(*after("panel_used", p - 1))
            for k, cols, src in chunks:
                raw = stage[:, n % STAGE, :, 0:cols]
                hi = wh[:, p % 2, k:k + CHUNK_K, 0:cols]
                lo = wl[:, p % 2, k:k + CHUNK_K, 0:cols]
                parts = [(raw, hi, lo)]
                if p == index["q"]:
                    parts = [(raw[:, i].rearrange("p (a m c) -> p a m c", a=2, c=HD)[:, a],
                              *(w[:, i].rearrange("p (m a c) -> p a m c", a=2, c=HD)[:, a] for w in (hi, lo)))
                             for i in range(CHUNK_K) for a in range(2)]
                pool.wait_ge(*after(f"w_landed{n % STAGE}", 16 * (n // STAGE + 1)))
                for raw_, hi_, _ in parts:
                    last = nc.gpsimd.tensor_scalar(hi_, raw_, 1.0, 0.0, ALU.mult, ALU.add)
                last.then_inc(sem("w_high"), 1)
                pool.wait_ge(*after("w_high", n + 1))
                for raw_, hi_, lo_ in parts:
                    last = nc.gpsimd.tensor_tensor(lo_, raw_, hi_.bitcast(F32), ALU.subtract)
                last.then_inc(sem("w_split"), 1)
                n += 1

    @block.tensor
    def _(pe):
        def panel_ready(name):
            pe.wait_ge(*after("w_split", chunk_end[index[name]]))

        def unit_bank(ring, u, free):
            if u >= ring:
                pe.wait_ge(*after(free, u - ring + 1))
            return u % ring

        def three_passes(acc, pairs):
            m = None
            for i, (ah, al, bh, bl) in enumerate(pairs):
                for j, (a, b) in enumerate(((ah, bh), (ah, bl), (al, bh))):
                    m = pe.matmul(acc, a, b, start=(i == 0 and j == 0),
                                  stop=(i == len(pairs) - 1 and j == 2))
            return m

        def wide_unit(name, acc, hh, hl, n, wcols):
            s = index[name] % 2
            sl = slice(COLS * n, COLS * n + COLS)
            return three_passes(acc, [(wcols(wh, s, k), wcols(wl, s, k), hh[:, k, sl], hl[:, k, sl])
                                      for k in range(KT)])

        def tok_unit(name, acc, hh, hl, toks, cols=COLS):
            s = index[name] % 2
            return three_passes(acc, [(toks(hh, k), toks(hl, k), wh[:, s, k, 0:cols], wl[:, s, k, 0:cols])
                                      for k in range(KT)])

        def plain_cols(m):
            return lambda w, s, k: w[:, s, k, P * m:P * m + P]

        def plain_toks(t):
            return lambda h, k: h[:, k, P * t:P * t + P]

        pe.wait_ge(*after("ident_in", 16))
        def transposes_in(tiles, tag, bank0):
            for n in range(HALF):
                for k in range(KT):
                    u = n * KT + k
                    b = bank0 + unit_bank(4, u, f"{tag}_evac")
                    for j in range(4):
                        t = 4 * n + j
                        if k == 0:
                            pe.wait_ge(*after(f"{tag}_scaled", t + 1))
                        m = pe.transpose(ps[:, b, P * j:P * j + P], tiles[:, t, P * k:P * k + P], ident[:])
                    m.then_inc(sem(f"{tag}_T"), 1)
        transposes_in(xt, "x", 4)

        panel_ready("u")
        for n in range(HALF):
            pe.wait_ge(*after("x_evac", KT * (n + 1)))
            for g in range(4):
                u = 4 * n + g
                b = unit_bank(4, u, "u_evac")
                wide_unit("u", ps[:, b, :], hTh, hTl, n, plain_cols(g)).then_inc(sem("u_done"), 1)
        pe.drain().then_inc(sem("panel_used"), 1)
        panel_ready("pgate")

        pe.wait_ge(*after("x_evac", 2 * KT))

        def pool_mix(g):
            pe.wait_ge(*after("pooled", g + 1))
            for n in range(HALF):
                u = 2 * g + n
                if u >= 2:
                    pe.wait_ge(*after("mix_evac", u - 1))
                pe.matmul(ps[:, 4 + u % 2, :], pool_wt[:, g, :], pooled[:, g % 2, COLS * n:COLS * n + COLS],
                          start=True, stop=True).then_inc(sem("mix_done"), 1)

        for m in range(4):
            pool_mix(m)
            for n in range(HALF):
                u = 2 * m + n
                if u == 0:
                    pe.wait_ge(*after("u_evac", 8))
                b = unit_bank(2, u, "pg_evac")
                wide_unit("pgate", ps[:, b, :], hTh, hTl, n, plain_cols(m)).then_inc(sem("pg_done"), 1)
        pe.drain().then_inc(sem("panel_used"), 1)
        phase_end(pe, "pe")

        pe.wait_ge(*after("pg_evac", 8))
        u = 0
        for name, ms in (("q", range(4)), ("kv", range(2))):
            panel_ready(name)
            for m in ms:
                for n in range(HALF):
                    b = unit_bank(4, u, "qkv_evac")
                    wide_unit(name, ps[:, b, :], hTh, hTl, n, plain_cols(m)).then_inc(sem("qkv_done"), 1)
                    u += 1
            pe.drain().then_inc(sem("panel_used"), 1)
        pe.wait_ge(*after("qkv_evac", u))
        pe.wait_ge(*after("mix_evac", 8))
        for half in range(2):
            for j in range(4):
                t = 4 * half + j
                m = pe.transpose(ps[:, 4 + half, P * j:P * j + P], vT[:, P * t:P * t + P], ident[:])
            m.then_inc(sem("v1_T"), 1)
        pe.wait_ge(*after("v1_evac", 2))

        def keys_of(t):
            return (0, P) if t == 0 else (P * (t - 1), 2 * P)

        def swa_scores(i):
            t, hh = divmod(i, HH)
            k0, nk = keys_of(t)
            if i >= 1:
                pe.wait_ge(*after("swa_masked", i))
            for j in range(G):
                h = G * hh + j
                rows = slice(HD * (h // 4), HD * (h // 4) + HD)
                m = pe.matmul(ps[:, j // 2, (j % 2) * 256:(j % 2) * 256 + nk], qT[rows, h % 4, P * t:P * t + P],
                              kT[rows, k0:k0 + nk], start=True, stop=True)
            m.then_inc(sem("swa_scored"), 1)

        def swa_transposes(i):
            t, hh = divmod(i, HH)
            nb = keys_of(t)[1] // P
            pe.wait_ge(*after("swa_exp", G * (i + 1)))
            if i >= 1:
                pe.wait_ge(*after("swa_pT", i))
            for j in range(G):
                for kb in range(nb):
                    c = 2 * j + kb
                    m = pe.transpose(ps[:, 2 + c // 4, (c % 4) * P:(c % 4) * P + P],
                                     pr[:, i % 2, j, P * kb:P * kb + P], ident[:])
            m.then_inc(sem("swa_T"), 1)

        def swa_values(i):
            t, hh = divmod(i, HH)
            nb = keys_of(t)[1] // P
            pe.wait_ge(*after("swa_pT", i + 1))
            if i >= 2:
                pe.wait_ge(*after("swa_out", i - 1))
            for j in range(G):
                h = G * hh + j
                for kb in range(nb):
                    kt = t - nb + 1 + kb
                    m = pe.matmul(ps[:, 4 + i % 2, HD * j:HD * j + HD], pT[:, 2 * j + kb, :],
                                  v1[:, kt, HD * (h // 4):HD * (h // 4) + HD], start=(kb == 0), stop=(kb == nb - 1))
            m.then_inc(sem("swa_valued"), 1)

        def swa_back(t):
            pe.wait_ge(*after("swa_out", 2 * t + 2))
            if t >= 1:
                pe.wait_ge(*after("swa_aT", t))
            flat = ao[:].rearrange("p h d -> p (h d)")
            for j in range(4):
                m = pe.transpose(ps[:, 6, P * j:P * j + P], flat[:, P * j:P * j + P], ident[:])
            m.then_inc(sem("swa_backT"), 1)

        def attn_gate(i):
            quarter, m_ = divmod(i, 4)
            if i >= 1:
                pe.wait_ge(*after("ag_mul", i))
            s = index["agate"] % 2
            sl = slice(2 * P * quarter, 2 * P * quarter + 2 * P)
            three_passes(ps[:, 7, 0:2 * P], [(wh[:, s, k, P * m_:P * m_ + P], wl[:, s, k, P * m_:P * m_ + P], hTh[:, k, sl], hTl[:, k, sl])
                                             for k in range(KT)]).then_inc(sem("ag_done"), 1)

        steps = TT * HH
        panel_ready("agate")
        for i in range(steps + 3):
            if i < steps:
                swa_scores(i)
            if 2 <= i < steps + 2:
                swa_values(i - 2)
            if i < steps:
                attn_gate(i)
            if i >= 4 and i % 2 == 0:
                swa_back((i - 4) // 2)
            if 1 <= i <= steps:
                swa_transposes(i - 1)
        pe.drain().then_inc(sem("panel_used"), 1)
        phase_end(pe, "pe")

        phase_start(pe, "pe")
        for t0 in range(0, TT, 4):
            for half, name in enumerate(("o0", "o1")):
                if t0 == 0:
                    panel_ready(name)
                s = index[name] % 2
                for ks in (MIX_ORDER[:4], MIX_ORDER[4:]):
                    for t in range(t0, t0 + 4):
                        if t0 and half == 0 and ks[0] == MIX_ORDER[0]:
                            pe.wait_ge(*after("y_read", t - 3))
                        tk = slice(P * t, P * t + P)
                        for k in ks:
                            if t == 0 and half == 0:
                                pe.wait_ge(*after("mixT_split", MIX_ORDER.index(k) + 1))
                            for j, (a, b) in enumerate(((mTh, wh), (mTh, wl), (mTl, wh))):
                                m = pe.matmul(ps[:, 2 * (t % 4) + half, :], a[:, k, tk], b[:, s, k, :],
                                              start=(k == MIX_ORDER[0] and j == 0), stop=(k == MIX_ORDER[-1] and j == 2))
                        if half == 1 and k == MIX_ORDER[-1]:
                            m.then_inc(sem("y_done"), 1)
                if t0:
                    pe.drain().then_inc(sem("panel_used"), 1)
        phase_end(pe, "pe")

        pe.wait_ge(*after("y_read", 6))
        transposes_in(xt2, "x1", 0)

        panel_ready("c")
        for t in range(TT):
            b = 4 + unit_bank(4, t, "c_evac")
            if t == 0:
                pe.wait_ge(*after("y_read", TT))
            pe.wait_ge(*after("x1_evac", KT * (t // 4 + 1)))
            tok_unit("c", ps[:, b, 0:C_W], h2h, h2l, plain_toks(t), C_W).then_inc(sem("c_done"), 1)
        pe.drain().then_inc(sem("panel_used"), 1)

        def gate_unit(u):
            name = (GATES[0] + GATES[1])[u // 8]
            if u % 8 == 0:
                panel_ready(name)
            b = unit_bank(4, u, "g_evac")
            wide_unit(name, ps[:, b, :], h2h, h2l, u % HALF, plain_cols(u // 2 % 4)).then_inc(sem("g_done"), 1)
            if u % 8 == 7:
                pe.drain().then_inc(sem("panel_used"), 1)

        pe.wait_ge(*after("x1_evac", 2 * KT))
        for u in range(16):
            gate_unit(u)
        phase_end(pe, "pe")

        pe.wait_ge(*after("g_evac", 16))

        def d_proj(slot):
            u, part = divmod(slot, 2)
            g, kind, t = D_UNITS[u]
            name = f"{kind}{g}"
            toks = value_tiles(g)[t][1] if kind == "v" else group_toks(g, t)
            s = index[name] % 2
            if part == 0:
                if t == 0:
                    panel_ready(name)
                if u >= 2:
                    pe.wait_ge(*after("d_read", u - 1))
            for k in range(KT // 2 * part, KT // 2 * (part + 1)):
                for a, b in ((h2h, wh), (h2h, wl), (h2l, wh)):
                    m = pe.matmul(ps[:, u % 2, :], toks(a, k), b[:, s, k, :], start=(k == 0 and b is wh and a is h2h),
                                  stop=(k == KT - 1 and a is h2l))
            if part == 1:
                m.then_inc(sem("d_done"), 1)
                if u + 1 == len(D_UNITS) or D_UNITS[u + 1][:2] != (g, kind):
                    pe.drain().then_inc(sem("panel_used"), 1)

        def rotated_transposes(r):
            pe.wait_ge(*after("rotated", r + 1))
            if r >= 1:
                pe.wait_ge(*after("rotT_read", r))
            for j in range(4):
                m = pe.transpose(ps[:, 2, P * j:P * j + P], rr[:, P * j:P * j + P], ident[:])
            m.then_inc(sem("rotT"), 1)

        def d_scores(g, i):
            n = d_step(g, i)
            t, hh = divmod(i, HH)
            k0, nk, _, _ = window(g, t)
            pe.wait_ge(*after("rotT_read", 2 * TT * g + TT + t + 1))
            if n >= 1:
                pe.wait_ge(*after("d_masked", n))
            for j in range(G):
                h = G * hh + j
                rows = slice(HD * (h % 2), HD * (h % 2) + HD)
                m = pe.matmul(ps[:, 3 + j % 2, (j // 2) * 256:(j // 2) * 256 + nk], qTd[rows, t % 2, h // 2, :],
                              kTd[rows, h // 2, k0:k0 + nk], start=True, stop=True)
            m.then_inc(sem("d_scored"), 1)

        def d_transposes(g, i):
            n = d_step(g, i)
            blocks = window(g, i // HH)[3]
            pe.wait_ge(*after("d_exp", G * (n + 1)))
            if n >= 1:
                pe.wait_ge(*after("d_pT", n))
            for j in range(G):
                for kb, (c0, width, _, _, _) in enumerate(blocks):
                    c = 2 * j + kb
                    m = pe.transpose(ps[0:width, 5 + c // 4, (c % 4) * P:(c % 4) * P + P],
                                     prd[:, i % 2, j, c0:c0 + width], ident[:])
            m.then_inc(sem("d_T"), 1)

        def d_values(g, i):
            n = d_step(g, i)
            t, hh = divmod(i, HH)
            blocks = window(g, t)[3]
            if i == 0:
                pe.wait_ge(*after("d_read", D_UNITS.index((g, "q", 0))))
            pe.wait_ge(*after("d_pT", n + 1))
            if n >= 1:
                pe.wait_ge(*after("d_out", n))
            for j in range(G):
                h = G * hh + j
                for kb, (_, _, vt, r0, nr) in enumerate(blocks):
                    m = pe.matmul(ps[:, 7, HD * j:HD * j + HD], pTd[r0:r0 + nr, 2 * j + kb, :],
                                  vd[r0:r0 + nr, vt, HD * h:HD * h + HD], start=(kb == 0), stop=(kb == len(blocks) - 1))
            m.then_inc(sem("d_valued"), 1)

        for slot in range(D_SLOTS):
            if slot in step_at:
                d_scores(*step_at[slot])
            if slot - 2 in step_at:
                d_values(*step_at[slot - 2])
            if slot < 2 * len(D_UNITS):
                d_proj(slot)
            if slot in (2 * len(D_UNITS), 2 * len(D_UNITS) + 2):
                u = 16 + slot // 2 - len(D_UNITS)
                pe.wait_ge(*after("d_read", len(D_UNITS)))
                gate_unit(u)
            done = unit_before(slot)
            if done and done[3] != "v":
                rotated_transposes(done[1])
            if slot - 1 in step_at:
                d_transposes(*step_at[slot - 1])
        phase_end(pe, "pe")

        pe.wait_ge(*after("rotT_read", 6 * TT))
        pe.wait_ge(*after("d_masked", 2 * 3 * TT))
        pe.wait_ge(*after("d_pT", 2 * 3 * TT))

        def joint_transposes(u):
            t, r = divmod(u - 16 - JOINT_LAG, JOINT_STEP)
            if r or not 0 <= t < TT:
                return
            pe.wait_ge(*after("joint", t + 1))
            if t >= 2:
                pe.wait_ge(*after("dg_done", t - 1))
            for j in range(4):
                m = pe.transpose(ps[:, 4 + t % 2, P * j:P * j + P], wsum[:, 0, P * j:P * j + P], ident[:])
            m.then_inc(sem("jointT"), 1)

        for u in range(18, 48):
            gate_unit(u)
            joint_transposes(u)
        phase_end(pe, "pe")

        pe.wait_ge(*after("g_evac", 48))
        pe.wait_ge(*after("c_back", 16))
        for u, (n, kind) in enumerate(C_UNITS):
            b = unit_bank(4, u, "cT_lo")
            c0, width = C_KINDS[kind]
            for j in range(4):
                m = pe.transpose(ps[0:width, b, P * j:P * j + P], c_bk[:, 4 * n + j, c0:c0 + width], ident[:])
            m.then_inc(sem("cT"), 1)
        pe.wait_ge(*after("cT_lo", len(C_UNITS)))
        panel_ready("mla")
        s = index["mla"] % 2
        for t in range(TT):
            for half in range(2):
                u = 2 * t + half
                if u >= 4:
                    pe.wait_ge(*after("qm_read", u - 3))
                three_passes(ps[:, u % 4, 0:384], [
                    (cqh[:, k, P * t:P * t + P], cql[:, k, P * t:P * t + P],
                     wh[:, s, 2 * half + k, 0:384], wl[:, s, 2 * half + k, 0:384]) for k in range(2)]).then_inc(sem("qm_done"), 1)
            if t >= 2:
                pe.wait_ge(*after("vm_lo", t - 1))
            for n in range(2):
                v_cols = [w[:, s, 4 + n, :].rearrange("p (h c) -> p h c", c=P)[:, :, HD:] for w in (wh, wl)]
                m = three_passes(ps[:, 4 + t % 2, 256 * n:256 * n + 256].rearrange("p (h c) -> p h c", c=HD), [
                    (ckh[:, P * t:P * t + P], ckl[:, P * t:P * t + P], *v_cols)])
            m.then_inc(sem("vm_done"), 1)
        phase_end(pe, "pe")


        def head_inputs(h, part):
            x = 4 * h + part
            if x >= 1:
                pe.wait_ge(*after("qk_lo", x))
            if part >= 2:
                pe.wait_ge(*after("qm_back", 16 * (h + 1)))
                for j in range(4):
                    m = pe.transpose(ps[0:MLA_QK, 7, P * j:P * j + P], qm[:, 4 * (part - 2) + j, :], ident[:])
            else:
                n = part
                w = [y[:, s, 4 + h // 4, P * (h % 4):P * (h % 4) + P] for y in (wh, wl)]
                m = three_passes(ps[:, 7, :], [(*w, ckh[:, COLS * n:COLS * n + COLS], ckl[:, COLS * n:COLS * n + COLS])])
            m.then_inc(sem("qk_done"), 1)

        def m_scores(i):
            h, qt = divmod(i, TT)
            pe.wait_ge(*after("qk_lo", 4 * h + 4))
            if i >= 2:
                pe.wait_ge(*after("m_exp", i - 1))
            for n in range(HALF):
                m = three_passes(ps[:, 2 * (i % 2) + n, :], [
                    (Qh[:, h % 2, P * qt:P * qt + P], Ql[:, h % 2, P * qt:P * qt + P],
                     Kh[:, h % 2, COLS * n:COLS * n + COLS], Kl[:, h % 2, COLS * n:COLS * n + COLS])])
            m.then_inc(sem("m_scored"), 1)

        def m_transposes(i):
            pe.wait_ge(*after("m_normed", i + 1))
            for half in range(2):
                if i >= 1:
                    pe.wait_ge(*after("m_lo", 2 * i - 1 + half))
                for j in range(4):
                    kt = 4 * half + j
                    m = pe.transpose(ps[:, 4 + half, P * j:P * j + P], pm[:, i % 2, P * kt:P * kt + P], ident[:])
                m.then_inc(sem("m_T"), 1)

        def m_values(b, part):
            h = b // 4
            pe.wait_ge(*after("m_lo", 4 * b + 4))
            if b >= 1:
                pe.wait_ge(*after("m_out", b))
            ops = [(V2[:, kt, h].rearrange("p a c -> p (a c)"), p[:, b % 2, kt, :])
                   for kt in range(4 * part, 4 * part + 4) for p in (PTh, PTl)]
            for i, (a, p) in enumerate(ops):
                m = pe.matmul(ps[:, 6, 0:256], a, p, start=(part == 0 and i == 0), stop=(part == 1 and i == 7))
            if part == 1:
                m.then_inc(sem("m_valued"), 1)

        for part in range(4):
            head_inputs(0, part)
        pe.wait_ge(*after("qm_read", 2 * TT))
        pe.wait_ge(*after("vm_lo", TT))
        for j in range(n_t + 5):
            if j < n_t:
                m_scores(j)
            if 5 <= j:
                m_values((j - 5) // 2, (j - 5) % 2)
            if j < n_t:
                h, qt = divmod(j, TT)
                if h + 1 < H1 and qt in (2, 3, 4, 5):
                    head_inputs(h + 1, qt - 2)
            if 2 <= j < n_t + 2:
                m_transposes(j - 2)
        pe.drain().then_inc(sem("panel_used"), 1)
        phase_end(pe, "pe")

        phase_start(pe, "pe")
        for o, (name, h_, l_) in enumerate((("od", dh, dl), ("om", ah, al))):
            panel_ready(name)
            s = index[name] % 2
            for n in range(HALF):
                sl = slice(COLS * n, COLS * n + COLS)
                for m_ in range(KT):
                    u = 2 * KT * o + KT * n + m_
                    if u >= 8:
                        pe.wait_ge(*after("y2_read", u - 7))
                    c = P * (m_ % 4)
                    for k in range(4):
                        if n == 0 and m_ == 0:
                            pe.wait_ge(*after("mixers_lo", 4 * o + k + 1))
                        w_hi, w_lo = (w[:, s, 4 * (m_ // 4) + k, c:c + P] for w in (wh, wl))
                        for j, (a, b) in enumerate(((w_hi, h_), (w_hi, l_), (w_lo, h_))):
                            m = pe.matmul(ps[:, u % 8, :], a, b[:, k, sl], start=(k == 0 and j == 0), stop=(k == 3 and j == 2))
                    m.then_inc(sem("y2_done"), 1)
            pe.drain().then_inc(sem("panel_used"), 1)

        for half, name in enumerate(("p0", "p1")):
            panel_ready(name)
            for t in range(TT):
                u = TT * half + t
                if t in (0, 4) and half == 0:
                    pe.wait_ge(*after("merged_lo", 2 * t + 8))
                pe.wait_ge(*(after("o_read", u - 7) if u >= 8 else after("y2_read", 4 * KT - 7 + u)))
                tok_unit(name, ps[:, u % 8, :], Mh, Ml, plain_toks(t)).then_inc(sem("o_done"), 1)
            pe.drain().then_inc(sem("panel_used"), 1)

    @block.scalar
    def _(act):
        x_tok = x[0].rearrange("(t p) d -> t p d", p=P)
        act.dma_start(ident[:], c_ident).then_inc(sem("ident_in"), 16)
        for t in range(TT):
            act.dma_start(xt[:, t, :], x_tok[t]).then_inc(sem(f"x_in{t}"), 16)
            if t == 3:
                with nc.allow_non_contiguous_dma(reason="one gain a partition"):
                    act.dma_start(gain_pre, norm_pre[0].rearrange("(k p) -> p k", p=P)).then_inc(sem("gain_in"), 16)
        consts = [
            (pscale, pool_scale[0].rearrange("(k p) -> p k", p=P)),
            (gain_2, attn_norm_g[0].rearrange("(k p) -> p k", p=P)),
            (gain_q, q_norm_g[0].rearrange("(k p) -> p k", p=P)),
            (gain_kv, kv_norm_g[0].rearrange("(k p) -> p k", p=P)),
            (bgate, b_gate[0].rearrange("(k p) -> p k", p=P)),
            (sinks_p, attn_sinks[0:1, :].to_broadcast([P, H1])),
        ]
        act.wait_ge(*after("zeroed", 1))

        def x_root(t):
            act.wait_ge(*after(f"x_in{t}", 16))
            act.activation(junk[:], xt[:, t, :], ACT.Square, accum_out=ssq[:, t:t + 1]).then_inc(sem("x_sq"), 1)
            act.wait_ge(*after("x_sq", t + 1))
            act.activation(rstd[:, t:t + 1], ssq[:, t:t + 1], ACT.Sqrt, scale=1.0 / D, bias=EPS_C).then_inc(sem("x_root"), 1)

        for n in range(HALF):
            for t in range(4 * n, 4 * n + 4):
                x_root(t)
            if n == 0:
                act.wait_ge(*after("gain_in", 16))
            for k in range(KT):
                u = n * KT + k
                act.wait_ge(*after("x_T", u + 1))
                act.activation(hTh[:, k, COLS * n:COLS * n + COLS], ps[:, 4 + u % 4, :], ACT.Copy,
                               scale=gain_pre[:, k:k + 1]).then_inc(sem("x_hi"), 1)
        with nc.allow_non_contiguous_dma(reason="vectors of one value a partition"):
            for dst, src in consts:
                act.dma_start(dst, src).then_inc(sem("const"), 16)
        act.wait_ge(*after("const", 16 * len(consts)))

        act.dma_start(pool_wt[:], pool_w[0].rearrange("g c d -> c g d")).then_inc(sem("pool_c"), 16)
        for g in range(4):
            act.dma_start(edge[:, g, :], c_inv[g:g + 1, :].to_broadcast([P, PAD])).then_inc(sem("pool_c"), 16)
        act.wait_ge(*after("u_pad", 1))
        for u in range(8):
            n, g = divmod(u, 4)
            act.wait_ge(*after("u_done", u + 1))
            act.activation(uT[:, g, PAD + COLS * n:PAD + COLS * n + COLS], ps[:, u % 4, :],
                           ACT.Copy).then_inc(sem("u_evac"), 1)
        for u in range(8):
            act.wait_ge(*after("pg_done", u + 1))
            if u >= 2:
                act.wait_ge(*after("pg_mul", u - 1))
            act.activation(sg1[:, u % 2, :], ps[:, u % 2, :], ACT.Silu).then_inc(sem("pg_evac"), 1)
        for g in range(4):
            act.wait_ge(*after("pg_mul", 2 * g + 2))
            act.dma_start(pool_d[P * g:P * g + P, :], pmT[:, g, :]).then_inc(sem("pool_spill"), 16)
        act.wait_ge(*after("pool_spill", 64))
        phase_end(act, "act")

        phase_start(act, "act")
        act.dma_start(swa_b[:].rearrange("p h k -> p (h k)"), c_swa).then_inc(sem("swa_c"), 16)
        for u in range(12):
            act.wait_ge(*after("qkv_done", u + 1))
            m, n = divmod(u, 2)
            sl = slice(COLS * n, COLS * n + COLS)
            dst = qT[:, m, sl] if m < 4 else (kT[:, sl] if m == 4 else vT[:, sl])
            act.activation(dst, ps[:, u % 4, :], ACT.Copy, scale=HD ** -0.5 if m < 4 else 1.0).then_inc(sem("qkv_evac"), 1)
        act.wait_ge(*after("v1_T", 2))
        for half in range(2):
            act.activation(v1[:, 4 * half:4 * half + 4, :], ps[:, 4 + half, :], ACT.Copy).then_inc(sem("v1_evac"), 1)

        steps = TT * HH

        def swa_pT(i):
            nb = 1 if i < HH else 2
            act.wait_ge(*after("swa_T", i + 1))
            if i >= 1:
                act.wait_ge(*after("swa_valued", i))
            src = ps[:, 2:4, :].rearrange("p b (j c) -> p (b j) c", c=P)
            if nb == 1:
                act.activation(pT[:, 0:8:2, :], src[:, 0:8:2, :], ACT.Copy).then_inc(sem("swa_pT"), 1)
            else:
                act.activation(pT[:], src, ACT.Copy).then_inc(sem("swa_pT"), 1)

        for i in range(steps + 1):
            if i < steps:
                t, hh = divmod(i, HH)
                nk = P if t == 0 else 2 * P
                act.wait_ge(*after("swa_max", i + 1))
                for j in range(G):
                    h = G * hh + j
                    act.activation(pr[:, i % 2, j, 0:nk], pr[:, i % 2, j, 0:nk], ACT.Exp,
                                   bias=st[:, t % 2, 0, h:h + 1], accum_out=st[:, t % 2, 1, h:h + 1]).then_inc(sem("swa_exp"), 1)
                act.activation(st[:, t % 2, 2, G * hh:G * hh + G], st[:, t % 2, 3, G * hh:G * hh + G], ACT.Exp).then_inc(sem("swa_sink"), 1)
                act.wait_ge(*after("ag_done", i + 1))
                if i >= 2:
                    act.wait_ge(*after("ag_mul", i - 1))
                act.activation(sgA[:, i % 2, :], ps[:, 7, 0:2 * P], ACT.Exp, scale=-1.0).then_inc(sem("ag_evac"), 1)
            if i >= 1:
                swa_pT(i - 1)
        phase_end(act, "act")

        phase_start(act, "act")
        for g in range(4):
            act.dma_start(pmR[:, g, :], pool_d[P * g:P * g + P, :]).then_inc(sem("pool_back"), 16)
        act.dma_start(gpost[:], norm_post[0:1, :].to_broadcast([P, D])).then_inc(sem("gpost"), 16)
        for i, k in enumerate(MIX_ORDER):
            if i == 4:
                act.wait_ge(*after("pool_back", 64))
            src = pmR[:, k, :] if k < 4 else aT[:, k - 4, :]
            act.activation(mTh[:, k, :], src, ACT.Copy).then_inc(sem("mixT_hi"), 1)
        x1_tok = x1_d.rearrange("(t p) d -> t p d", p=P)

        def x_back(t):
            if t >= 2:
                act.wait_ge(*after("x1_made", t - 1))
            act.dma_start(xr[:, t % 2, :], x_tok[t]).then_inc(sem(f"x_back{t % 2}"), 16)

        def x1_store(t):
            act.wait_ge(*after("x1_made", t + 1))
            act.dma_start(x1_tok[t], x1[:, t % 2, :]).then_inc(sem(f"x1_out{t % 2}"), 16)

        def x1_root(t):
            if t >= 1:
                act.wait_ge(*after("x1_sq", t))
            act.wait_ge(*after("y_sq", t + 1))
            act.activation(ysq[:], x1[:, t % 2, :], ACT.Square, accum_out=ssq2[:, t:t + 1]).then_inc(sem("x1_sq"), 1)
            act.wait_ge(*after("x1_sq", t + 1))
            act.activation(ssq2[:, t:t + 1], ssq2[:, t:t + 1], ACT.Sqrt, scale=1.0 / D, bias=EPS_C).then_inc(sem("x1_root"), 1)

        x_back(0)
        x_back(1)
        for t in range(TT):
            act.wait_ge(*after("y_done", t + 1))
            if t >= 1:
                act.wait_ge(*after("y_sq", t))
            if t >= 2:
                act.wait_ge(*after("x1_sq", t - 1))
            act.activation(ysq[:].rearrange("p (b c) -> p b c", b=2), ps[:, 2 * (t % 4):2 * (t % 4) + 2, :], ACT.Square,
                           accum_out=ssq[:, t:t + 1]).then_inc(sem("y_sq"), 1)
            act.wait_ge(*after("y_sq", t + 1))
            act.activation(rstd[:, t:t + 1], ssq[:, t:t + 1], ACT.Sqrt, scale=1.0 / D, bias=EPS_C).then_inc(sem("y_root"), 1)
            if t >= 1:
                x1_store(t - 1)
                x1_root(t - 1)
                if t + 1 < TT:
                    x_back(t + 1)
        x1_store(TT - 1)
        x1_root(TT - 1)
        for b in range(2):
            act.wait_ge(*after(f"x1_out{b}", 16 * TT // 2))
        phase_end(act, "act")

        act.wait_ge(*after("through_pe", phases["act"]))
        for n in range(HALF):
            for k in range(KT):
                u = n * KT + k
                act.wait_ge(*after("x1_T", u + 1))
                act.activation(h2h[:, k, COLS * n:COLS * n + COLS], ps[:, u % 4, :], ACT.Copy,
                               scale=gain_2[:, k:k + 1]).then_inc(sem("x1_hi"), 1)
        act.wait_ge(*after("through_dve", phases["act"]))
        with nc.allow_non_contiguous_dma(reason="one position a partition"):
            pos_row = positions[0]
            for g in range(3):
                for t in range(TT):
                    start, step = tile_start(g, t)
                    src = pos_row[start:start + step * (P - 1) + 1:step].rearrange("(p a) -> p a", a=1)
                    act.dma_start(posi[:, g, t:t + 1], src).then_inc(sem("pos_in"), 16)
            act.dma_start(freq[:], c_freq.to_broadcast([P, FREQS + MLA_R // 2])).then_inc(sem("pos_in"), 16)

        for t in range(TT):
            act.wait_ge(*after("c_done", t + 1))
            act.activation(c_sb[:, t, :], ps[:, 4 + t % 4, 0:C_W], ACT.Copy).then_inc(sem("c_evac"), 1)
            act.wait_ge(*after("c_evac", t + 1))
            for i, (c0, w) in enumerate(((0, C_Q), (C_Q, C_KV))):
                act.activation(c_sq[:, 0:w], c_sb[:, t, c0:c0 + w], ACT.Square, accum_out=c_ss[:, i, t:t + 1]).then_inc(sem("c_sqd"), 1)
                act.wait_ge(*after("c_sqd", 2 * t + i + 1))
        for i, (dst, q) in enumerate(((sin_d, 0), (cos_d, 1))):
            act.wait_ge(*after("angles", i + 1))
            act.activation(dst[:].rearrange("p g t f -> p (g t) f"), red[:, 0:24, :], ACT.Sin).then_inc(sem("tables"), 1)
            m_dst = (sin_m, cos_m)[i]
            act.activation(m_dst[:], red[:, 24:28, :].rearrange("p a (b f) -> p (a b) f", b=2), ACT.Sin).then_inc(sem("tables"), 1)
        act.wait_ge(*after("tables", 4))
        w_m = TT * MLA_R // 2
        act.dma_start(rope_d[:, 0:w_m], cos_m[:].rearrange("p t f -> p (t f)")).then_inc(sem("rope_spill"), 16)
        act.dma_start(rope_d[:, w_m:], sin_m[:].rearrange("p t f -> p (t f)")).then_inc(sem("rope_spill"), 16)
        for i, w in enumerate((C_Q, C_KV)):
            act.activation(c_ss[:, i, :], c_ss[:, i, :], ACT.Sqrt, scale=1.0 / w, bias=EPS_C).then_inc(sem("c_root"), 1)
        act.wait_ge(*after("c_roped", 1))
        act.wait_ge(*after("c_scaled", 2 * TT))
        act.dma_start(c_d.rearrange("(t p) c -> p t c", p=P), c_sb[:]).then_inc(sem("c_spill"), 16)

        def gate_evac(units, tiles, after_unit=lambda u: None):
            for u in units:
                mt, n = divmod(u, 2)
                gi, m = divmod(mt, 4)
                dst = (zm_d, zd_d, g_d, g_d, g_d, g_d)[gi]
                row0 = 0 if gi < 2 else COLS * (gi - 2)
                if n == 0 and mt >= 4:
                    act.wait_ge(*after(f"g_spill{mt % 4}", 16 * (mt // 4)))
                act.wait_ge(*after("g_done", u + 1))
                d = tiles[:, mt % 4, COLS * n:COLS * n + COLS]
                if gi < 2:
                    act.activation(d, ps[:, u % 4, :], ACT.Silu).then_inc(sem("g_evac"), 1)
                else:
                    c = row0 // P + m
                    act.activation(d, ps[:, u % 4, :], ACT.Sigmoid, bias=bgate[:, c:c + 1]).then_inc(sem("g_evac"), 1)
                if n:
                    act.wait_ge(*after("g_evac", u + 1))
                    act.dma_start(dst[row0 + P * m:row0 + P * m + P, :], tiles[:, mt % 4, :]).then_inc(sem(f"g_spill{mt % 4}"), 16)
                after_unit(u)
        gate_evac(range(16), gt)
        act.wait_ge(*after("rope_spill", 32))
        act.wait_ge(*after("c_spill", 16))
        for b in range(4):
            act.wait_ge(*after(f"g_spill{b}", 16 * 2))
        phase_end(act, "act")

        phase_start(act, "act")
        act.dma_start(masks[:], c_mask).then_inc(sem("masks_in"), 16)

        def rotT_read(r, g, t, keys):
            act.wait_ge(*after("rotT", r + 1))
            src = ps[:, 2, :].rearrange("p (j c) -> p j c", c=P)
            if keys:
                act.activation(kTd[:, :, P * t:P * t + P], src, ACT.Copy).then_inc(sem("rotT_read"), 1)
            else:
                if t >= 2:
                    act.wait_ge(*after("d_scored", d_step(g, 2 * (t - 2) + 2)))
                act.activation(qTd[:, t % 2, :, :], src, ACT.Copy, scale=HD ** -0.5).then_inc(sem("rotT_read"), 1)

        def d_exp(g, i):
            n = d_step(g, i)
            t, hh = divmod(i, HH)
            nk = window(g, t)[1]
            act.wait_ge(*after("d_max", n + 1))
            for j in range(G):
                h = G * hh + j
                o = osb[:, t % 2, :]
                act.activation(prd[:, i % 2, j, 0:nk], prd[:, i % 2, j, 0:nk], ACT.Exp, bias=o[:, COLS + h:COLS + h + 1],
                               accum_out=o[:, COLS + H1 + h:COLS + H1 + h + 1]).then_inc(sem("d_exp"), 1)

        def d_pT(g, i):
            n = d_step(g, i)
            blocks = window(g, i // HH)[3]
            act.wait_ge(*after("d_T", n + 1))
            if n >= 1:
                act.wait_ge(*after("d_valued", n))
            src = ps[:, 5:7, :].rearrange("p b (j c) -> p (b j) c", c=P)
            if len(blocks) == 1:
                act.activation(pTd[:, 0:8:2, :], src[:, 0:8:2, :], ACT.Copy).then_inc(sem("d_pT"), 1)
            elif blocks[0][1] < P:
                w = blocks[0][1]
                act.activation(pTd[0:w, 0:8:2, :], src[0:w, 0:8:2, :], ACT.Copy)
                act.activation(pTd[:, 1:8:2, :], src[:, 1:8:2, :], ACT.Copy).then_inc(sem("d_pT"), 1)
            else:
                act.activation(pTd[:], src, ACT.Copy).then_inc(sem("d_pT"), 1)

        def d_store(g, t):
            act.wait_ge(*after("d_out", d_step(g, 2 * t + 2)))
            start, step = tile_start(g, t)
            act.dma_start(dil_d[g][start:start + step * (P - 1) + 1:step, :], osb[:, t % 2, :]).then_inc(sem(f"d_store{t % 2}"), 16)

        for slot in range(D_SLOTS):
            done = unit_before(slot)
            if done and done[3] == "v":
                u, _, g, _, t = done
                if t == 0:
                    act.wait_ge(*after("d_read", u))
                    if g:
                        act.wait_ge(*after("d_valued", d_step(g, 0)))
                act.wait_ge(*after("d_done", u + 1))
                act.activation(vd[:, t, :], ps[:, u % 2, :], ACT.Copy).then_inc(sem("d_read"), 1)
            if slot in step_at:
                d_exp(*step_at[slot])
            if done and done[3] != "v":
                rotT_read(done[1], done[2], done[4], done[3] == "k")
            if slot - 1 in step_at:
                d_pT(*step_at[slot - 1])
            if slot - 2 in step_at:
                g, i = step_at[slot - 2]
                if i % HH == HH - 1:
                    d_store(g, i // HH)
        for b in range(2):
            act.wait_ge(*after(f"d_store{b}", 16 * 3 * TT // 2))
        phase_end(act, "act")

        phase_start(act, "act")
        for g in range(3):
            act.dma_start(stats[:, g, :, :], dil_d[g].rearrange("(t p) c -> p t c", p=P)[:, :, COLS:]).then_inc(sem("stats_in"), 16)
        for j in range(4):
            act.dma_start(zdT[:, j, :], zd_d[P * j:P * j + P, :]).then_inc(sem("zd_in"), 16)

        def nums_in(t):
            if t >= 2:
                act.wait_ge(*after("weighted", 3 * (t - 1)))
            for g in range(3):
                act.dma_start(nums[:, t % 2, g, :], dil_d[g][P * t:P * t + P, 0:COLS]).then_inc(sem(f"nums_in{t % 2}"), 16)

        nums_in(0)
        nums_in(1)
        for g in range(3):
            act.wait_ge(*after("coef_arg", g + 1))
            act.activation(coef[:, g, :, :], coef[:, g, :, :], ACT.Exp).then_inc(sem("coef_exp"), 1)

        def more_nums(u):
            t, r = divmod(u - 16 - JOINT_LAG, JOINT_STEP)
            if not r and 0 <= t < TT - 2:
                nums_in(t + 2)

        gate_evac(range(16, LAST_JOINT), gt2, more_nums)
        act.wait_ge(*after("dg_done", TT))
        for j in range(4):
            act.dma_start(dd_d[P * j:P * j + P, :], dgT[:, j, :]).then_inc(sem("dg_spill"), 16)
        gate_evac(range(LAST_JOINT, LAST_JOINT + 2), gt2)
        act.wait_ge(*after("dg_spill", 64))
        act.dma_start(c_bk[:], c_d.rearrange("(t p) c -> p t c", p=P)).then_inc(sem("c_back"), 16)
        act.dma_start(cos_q[:].rearrange("p t f -> p (t f)"), rope_d[:, 0:w_m]).then_inc(sem("rope_back"), 16)
        act.dma_start(sin_q[:].rearrange("p t f -> p (t f)"), rope_d[:, w_m:]).then_inc(sem("rope_back"), 16)
        gate_evac(range(LAST_JOINT + 2, 48), gt2)
        phase_end(act, "act")

        phase_start(act, "act")
        for u, (n, kind) in enumerate(C_UNITS):
            sl = slice(COLS * n, COLS * n + COLS)
            act.wait_ge(*after("cT", u + 1))
            if kind < 2:
                act.activation(cqh[:, kind, sl], ps[:, u % 4, :], ACT.Copy, scale=gain_q[:, kind:kind + 1]).then_inc(sem("cT_hi"), 1)
            elif kind == 2:
                act.activation(ckh[:, sl], ps[:, u % 4, :], ACT.Copy, scale=gain_kv).then_inc(sem("cT_hi"), 1)
            else:
                for b in range(2):
                    last = act.activation(Kh[HD:MLA_QK, b, sl], ps[HD:MLA_QK, u % 4, :], ACT.Copy)
                last.then_inc(sem("cT_hi"), 1)
        for t in range(TT):
            for half in range(2):
                u = 2 * t + half
                act.wait_ge(*after("qm_done", u + 1))
                if half == 0 and t >= 2:
                    act.wait_ge(*after(f"qm_spill{t % 2}", 16 * (t // 2)))
                act.activation(q_sb[:, t % 2, 4 * half:4 * half + 4, :], ps[:, u % 4, 0:384].rearrange("p (h c) -> p h c", c=MLA_QK),
                               ACT.Copy, scale=float(MLA_QK) ** -0.5).then_inc(sem("qm_read"), 1)
            act.wait_ge(*after("vm_done", t + 1))
            act.activation(V2[:, t, :, 0, :], ps[:, 4 + t % 2, :].rearrange("p (h c) -> p h c", c=HD), ACT.Copy).then_inc(sem("vm_hi"), 1)
            if t >= 1:
                act.wait_ge(*after("qm_roped", t))
                act.dma_start(qm_d[P * (t - 1):P * t, :], q_sb[:, (t - 1) % 2].rearrange("p h c -> p (h c)")).then_inc(sem(f"qm_spill{(t - 1) % 2}"), 16)
        for b in range(4):
            act.wait_ge(*after(f"g_spill{b}", 16 * 6))
        act.wait_ge(*after("qm_roped", TT))
        act.dma_start(qm_d[P * (TT - 1):, :], q_sb[:, (TT - 1) % 2].rearrange("p h c -> p (h c)")).then_inc(sem(f"qm_spill{(TT - 1) % 2}"), 16)
        qm_rows = qm_d.rearrange("(t p) c -> p t c", p=P)

        def head_load(h):
            if h >= 1:
                act.wait_ge(*after("qk_done", 4 * h))
            act.dma_start(qm[:], qm_rows[:, :, MLA_QK * h:MLA_QK * h + MLA_QK]).then_inc(sem("qm_back"), 16)

        def head_hi(x):
            h, part = divmod(x, 4)
            sl = slice(COLS * (part % 2), COLS * (part % 2) + COLS)
            act.wait_ge(*after("qk_done", x + 1))
            if h >= 2:
                act.wait_ge(*after("m_scored", TT * (h - 1)))
            dst, n = (Qh, MLA_QK) if part >= 2 else (Kh, HD)
            act.activation(dst[0:n, h % 2, sl], ps[0:n, 7, :], ACT.Copy).then_inc(sem("qk_hi"), 1)

        def zm_load(b):
            h, qb = divmod(b, 4)
            if b >= 2:
                act.wait_ge(*after("m_out", b - 1))
            act.dma_start(zm[0:HD, b % 2, :], zm_d[HD * h:HD * h + HD, 256 * qb:256 * qb + 256]).then_inc(sem(f"zm_in{b % 2}"), 16)

        def am_store(b):
            h, qb = divmod(b, 4)
            act.wait_ge(*after("m_out", b + 1))
            act.dma_start(am_d[HD * h:HD * h + HD, 256 * qb:256 * qb + 256], am[0:HD, b % 2, :]).then_inc(sem(f"am_out{b % 2}"), 16)

        head_hi(0)
        head_hi(1)
        for b in range(2):
            act.wait_ge(*after(f"qm_spill{b}", 16 * TT // 2))
        head_load(0)
        phase_end(act, "act")

        phase_start(act, "act")
        zm_load(0)
        zm_load(1)
        head_hi(2)
        head_hi(3)
        head_load(1)
        for j in range(n_t + 5):
            if j < n_t:
                h, qt = divmod(j, TT)
                if h + 1 < H1 and qt in (2, 3, 4, 5):
                    head_hi(4 * (h + 1) + qt - 2)
                    if qt == 5 and h + 2 < H1:
                        head_load(h + 2)
            if 2 <= j < n_t + 2:
                k = j - 2
                if k >= 4:
                    act.wait_ge(*after("m_valued", (k - 4) // 2 + 1))
                for half in range(2):
                    act.wait_ge(*after("m_T", 2 * k + half + 1))
                    act.activation(PTh[:, (k // 2) % 2, 4 * half:4 * half + 4, P * (k % 2):P * (k % 2) + P],
                                   ps[:, 4 + half, :].rearrange("p (j c) -> p j c", c=P), ACT.Copy).then_inc(sem("m_hi"), 1)
            if j < n_t:
                act.wait_ge(*after("m_max", j + 1))
                act.activation(pm[:, j % 2, :].rearrange("p (b c) -> p b c", b=2), ps[:, 2 * (j % 2):2 * (j % 2) + 2, :], ACT.Exp,
                               bias=rstd[:, j % 8:j % 8 + 1], accum_out=m_sum[:, j % 8:j % 8 + 1]).then_inc(sem("m_exp"), 1)
            if j >= 6 and j % 2 == 0:
                b = (j - 6) // 2
                am_store(b)
                if b + 2 < 4 * H1:
                    zm_load(b + 2)
        phase_end(act, "act")

        phase_start(act, "act")

        def mixer_in(x_):
            if x_ >= 2:
                act.wait_ge(*after("mixers_lo", x_ - 1))
            if x_ == 4:
                for b in range(2):
                    act.wait_ge(*after(f"am_out{b}", 16 * 2 * H1))
            src = (dd_d, am_d)[x_ // 4]
            act.dma_start(raw[:, x_ % 2, :], src[P * (x_ % 4):P * (x_ % 4) + P, :]).then_inc(sem(f"mixer_in{x_ % 2}"), 16)

        def gates_in(u):
            o, r = divmod(u, 2 * KT)
            n, m_ = divmod(r, KT)
            if u >= 4:
                act.wait_ge(*after("y2_read", u - 3))
            r0 = D * (1 - o) + P * m_
            act.dma_start(gg[:, u % 4, :], g_d[r0:r0 + P, COLS * n:COLS * n + COLS]).then_inc(sem(f"gates_in{u % 4}"), 16)

        mixer_in(0)
        mixer_in(1)
        for u in range(4):
            gates_in(u)
        for x_ in range(8):
            act.wait_ge(*after(f"mixer_in{x_ % 2}", 16 * (x_ // 2 + 1)))
            act.activation((dh, ah)[x_ // 4][:, x_ % 4, :], raw[:, x_ % 2, :], ACT.Copy).then_inc(sem("mixers_hi"), 1)
            if 1 <= x_ < 7:
                mixer_in(x_ + 1)
        for u in range(4, 2 * KT + 4):
            gates_in(u)
        for u in range(2 * KT):
            n, m_ = divmod(u, KT)
            act.wait_ge(*after("merged", u + 1))
            act.activation(Mh[:, m_, COLS * n:COLS * n + COLS], yg[:], ACT.Copy).then_inc(sem("merged_hi"), 1)
            if u + 4 < 2 * KT:
                gates_in(2 * KT + u + 4)

        out_tok = out[0].rearrange("(t p) d -> t p d", p=P)
        act.wait_ge(*after("y2_done", 4 * KT))
        act.wait_ge(*after("merged_lo", 2 * KT))
        for t in range(TT):
            act.dma_start(xo[:, t, :], x1_tok[t]).then_inc(sem(f"x1_back{t}"), 16)
        act.dma_start(gfin[:], final_norm_g.rearrange("(a d) -> a d", a=1).to_broadcast([P, D])).then_inc(sem("gfin"), 16)

        def out_store(t):
            act.wait_ge(*after("final", t + 1))
            act.dma_start(out_tok[t], fin[:, t % 2, :]).then_inc(sem(f"out_stored{t % 2}"), 16)

        for u in range(2 * TT):
            half, t = divmod(u, TT)
            act.wait_ge(*after("o_read", u + 1))
            if u >= 1:
                act.wait_ge(*after("o_sq", u))
            act.activation(osq[:], xo[:, t, COLS * half:COLS * half + COLS], ACT.Square,
                           accum_out=(ssq, ssq2)[half][:, t:t + 1]).then_inc(sem("o_sq"), 1)
            if half:
                act.wait_ge(*after("o_total", t + 1))
                act.activation(rstd[:, t:t + 1], rstd[:, t:t + 1], ACT.Sqrt, scale=1.0 / D, bias=EPS_C).then_inc(sem("o_root"), 1)
                if t >= 1:
                    out_store(t - 1)
        out_store(TT - 1)
        for b in range(2):
            act.wait_ge(*after(f"out_stored{b}", 16 * TT // 2))

    @block.vector
    def _(dve):
        turns_taken = [0]

        def in_turn(ins):
            ins.then_inc(sem("vector_step"), 1)
            turns_taken[0] += 1
            dve.wait_ge(sem("vector_step"), turns_taken[0])

        nc.vector.memset(EPS_C, EPS).then_inc(sem("zeroed"), 1)
        dve.wait_ge(*after("gain_in", 16))

        for t in range(TT):
            dve.wait_ge(*after("x_root", t + 1))
            nc.vector.reciprocal(rstd[:, t:t + 1], rstd[:, t:t + 1]).then_inc(sem("x_rstd"), 1)
            dve.wait_ge(*after("x_rstd", t + 1))
            nc.vector.tensor_scalar(xt[:, t, :], xt[:, t, :], rstd[:, t:t + 1], None, ALU.mult).then_inc(sem("x_scaled"), 1)
            if t in (3, TT - 1):
                for u in range(2 * (t - 3), 2 * (t - 3) + KT):
                    k, n = u % KT, u // KT
                    sl = slice(COLS * n, COLS * n + COLS)
                    dve.wait_ge(*after("x_hi", u + 1))
                    nc.vector.scalar_tensor_tensor(hTl[:, k, sl], ps[:, 4 + u % 4, :], gain_pre[:, k:k + 1],
                                                   hTh[:, k, sl].bitcast(F32), ALU.mult, ALU.subtract).then_inc(sem("x_evac"), 1)

        for g in range(4):
            nc.vector.memset(uT[:, g, 0:PAD], 0.0)
        nc.vector.memset(sA[:, 0:PAD], 0.0)
        nc.vector.memset(sB[:, 0:PAD], 0.0).then_inc(sem("u_pad"), 1)
        dve.wait_ge(*after("u_pad", 1))
        dve.wait_ge(*after("const", 16 * 6))
        in_turn(nc.vector.tensor_scalar(sinks_n, sinks_p, -1.0, None, ALU.mult))
        dve.wait_ge(*after("pool_c", 80))
        def pool_mul(u):
            g, n = divmod(u, 2)
            sl = slice(COLS * n, COLS * n + COLS)
            dve.wait_ge(*after("mix_done", u + 1))
            nc.vector.tensor_scalar(pmT[:, g, sl], ps[:, 4 + u % 2, :], pscale[:, g:g + 1], None,
                                    ALU.mult).then_inc(sem("mix_evac"), 1)

        def pool_finish(g):
            pool_mul(2 * g)
            pool_mul(2 * g + 1)
            for n in range(HALF):
                u = 2 * g + n
                sl = slice(COLS * n, COLS * n + COLS)
                dve.wait_ge(*after("pg_evac", u + 1))
                dve.wait_ge(*after("mix_evac", u + 1))
                nc.vector.tensor_tensor(pmT[:, g, sl], pmT[:, g, sl], sg1[:, u % 2, :], ALU.mult).then_inc(sem("pg_mul"), 1)

        for g, w in enumerate(POOL_W):
            dve.wait_ge(*after("u_evac", 5 + g))
            src, d, bufs = uT[:, g, :], 1, [sA, sB]
            while d < w:
                dst = bufs[0][:]
                in_turn(nc.vector.tensor_tensor(dst[:, PAD:], src[:, PAD:], src[:, PAD - d:PAD + S - d], ALU.add))
                src, d = dst, 2 * d
                bufs.reverse()
            if g >= 2:
                dve.wait_ge(*after("mix_done", 2 * (g - 1)))
            in_turn(nc.vector.scalar_tensor_tensor(pooled[:, g % 2, :], src[:, PAD:], 1.0 / w, uT[:, g, PAD:],
                                                ALU.mult, ALU.subtract))
            in_turn(nc.vector.tensor_tensor(edge_t[:], src[:, PAD:2 * PAD], edge[:, g, :], ALU.mult))
            in_turn(nc.vector.tensor_tensor(pooled[:, g % 2, 0:PAD], edge_t[:], uT[:, g, PAD:2 * PAD], ALU.subtract))
            nc.vector.memset(edge_t[:, 0:1], 0.0).then_inc(sem("pooled"), 1)
            if g >= 1:
                pool_finish(g - 1)
        pool_finish(3)
        phase_end(dve, "dve")

        phase_start(dve, "dve")
        dve.wait_ge(*after("swa_c", 16))
        steps = TT * HH
        def softmax_in(i):
            t, hh = divmod(i, HH)
            hs = slice(G * hh, G * hh + G)
            nk = P if t == 0 else 2 * P
            sc = ps[:, 0:2, :].rearrange("p b (j k) -> p (b j) k", j=2)[:, :, 0:nk]
            dst = pr[:, i % 2, :, 0:nk]
            dve.wait_ge(*after("swa_scored", i + 1))
            if i >= 2:
                dve.wait_ge(*after("swa_T", i - 1))
            nc.vector.tensor_tensor(dst, sc, swa_b[:, hs, 2 * P - nk:2 * P], ALU.add).then_inc(sem("swa_masked"), 1)
            dve.wait_ge(*after("swa_masked", i + 1))
            if t >= 2:
                dve.wait_ge(*after("swa_out", 2 * (t - 2) + hh + 1))
            in_turn(nc.vector.tensor_reduce(st[:, t % 2, 0, hs], dst, AX_X, ALU.max, negate=True))
            in_turn(nc.vector.tensor_tensor(st[:, t % 2, 0, hs], st[:, t % 2, 0, hs], sinks_n[:, hs], ALU.min))
            nc.vector.tensor_tensor(st[:, t % 2, 3, hs], st[:, t % 2, 0, hs], sinks_p[:, hs], ALU.add).then_inc(sem("swa_max"), 1)

        def normalise(i):
            t, hh = divmod(i, HH)
            hs = slice(G * hh, G * hh + G)
            dve.wait_ge(*after("swa_valued", i + 1))
            dve.wait_ge(*after("swa_sink", i + 1))
            in_turn(nc.vector.tensor_tensor(st[:, t % 2, 1, hs], st[:, t % 2, 1, hs], st[:, t % 2, 2, hs], ALU.add))
            in_turn(nc.vector.reciprocal(st[:, t % 2, 1, hs], st[:, t % 2, 1, hs]))
            if t >= 1:
                dve.wait_ge(*after("swa_backT", t))
            nc.vector.tensor_tensor(ao[:, hs, :], ps[:, 4 + i % 2, 0:256].rearrange("p (h d) -> p h d", d=HD),
                                    st[:, t % 2, 1, hs].unsqueeze(2).to_broadcast([P, G, HD]), ALU.mult).then_inc(sem("swa_out"), 1)

        def back(t):
            dve.wait_ge(*after("swa_backT", t + 1))
            dve.wait_ge(*after("ag_mul", 2 * t + 4 if t % 2 == 0 else 2 * t + 2))
            dst = aT[:, :, P * t:P * t + P]
            nc.vector.tensor_tensor(dst, ps[:, 6, :].rearrange("p (j c) -> p j c", c=P), dst, ALU.mult).then_inc(sem("swa_aT"), 1)

        def gate_attn(i):
            quarter, m_ = divmod(i, 4)
            dve.wait_ge(*after("ag_evac", i + 1))
            e = sgA[:, i % 2, :]
            in_turn(nc.vector.tensor_scalar(e, e, 1.0, None, ALU.add))
            in_turn(nc.vector.reciprocal(e, e))
            nc.vector.tensor_tensor(aT[:, m_, 2 * P * quarter:2 * P * quarter + 2 * P], ps[:, 7, 0:2 * P], e, ALU.mult).then_inc(sem("ag_mul"), 1)

        for i in range(steps + 3):
            if i < steps:
                softmax_in(i)
            if 2 <= i < steps + 2:
                normalise(i - 2)
            if i >= 4 and i % 2 == 0:
                back((i - 4) // 2)
            if i < steps:
                gate_attn(i)
        phase_end(dve, "dve")

        phase_start(dve, "dve")
        for i, k in enumerate(MIX_ORDER):
            if i == 4:
                dve.wait_ge(*after("pool_back", 64))
            src = pmR[:, k, :] if k < 4 else aT[:, k - 4, :]
            dve.wait_ge(*after("mixT_hi", i + 1))
            nc.vector.tensor_tensor(mTl[:, k, :], src, mTh[:, k, :].bitcast(F32), ALU.subtract).then_inc(sem("mixT_split"), 1)
        dve.wait_ge(*after("mixT_split", KT))
        dve.wait_ge(*after("gpost", 16))

        def x1_scale(t):
            dve.wait_ge(*after("x1_root", t + 1))
            nc.vector.reciprocal(ssq2[:, t:t + 1], ssq2[:, t:t + 1]).then_inc(sem("x1_rstd"), 1)
            dve.wait_ge(*after("x1_rstd", t + 1))
            nc.vector.tensor_scalar(xt2[:, t, :], x1[:, t % 2, :], ssq2[:, t:t + 1], None, ALU.mult).then_inc(sem("x1_scaled"), 1)

        for t in range(TT):
            dve.wait_ge(*after("y_root", t + 1))
            nc.vector.reciprocal(rstd[:, t:t + 1], rstd[:, t:t + 1]).then_inc(sem("y_rstd"), 1)
            dve.wait_ge(*after("y_rstd", t + 1))
            nc.vector.scalar_tensor_tensor(yn[:].rearrange("p (b c) -> p b c", b=2), ps[:, 2 * (t % 4):2 * (t % 4) + 2, :], rstd[:, t:t + 1],
                                           gpost[:].rearrange("p (b c) -> p b c", b=2), ALU.mult, ALU.mult).then_inc(sem("y_read"), 1)
            dve.wait_ge(*after("y_read", t + 1))
            dve.wait_ge(*after(f"x_back{t % 2}", 16 * (t // 2 + 1)))
            if t >= 2:
                dve.wait_ge(*after(f"x1_out{t % 2}", 16 * (t // 2)))
                dve.wait_ge(*after("x1_scaled", t - 1))
            nc.vector.tensor_tensor(x1[:, t % 2, :], yn[:], xr[:, t % 2, :], ALU.add).then_inc(sem("x1_made"), 1)
            if t >= 1:
                x1_scale(t - 1)
        x1_scale(TT - 1)
        phase_end(dve, "dve")

        dve.wait_ge(*after("through_pe", phases["dve"]))
        for n in range(HALF):
            for k in range(KT):
                u = n * KT + k
                sl = slice(COLS * n, COLS * n + COLS)
                dve.wait_ge(*after("x1_hi", u + 1))
                nc.vector.scalar_tensor_tensor(h2l[:, k, sl], ps[:, u % 4, :], gain_2[:, k:k + 1],
                                               h2h[:, k, sl].bitcast(F32), ALU.mult, ALU.subtract).then_inc(sem("x1_evac"), 1)

        dve.wait_ge(*after("pos_in", 16 * 25))
        in_turn(nc.vector.tensor_copy(posf[:], posi[:]))
        for i in range(3 * TT):
            in_turn(nc.vector.tensor_scalar(ang[:, i, :], freq[:, 0:FREQS], posf[:, i // TT, i % TT:i % TT + 1], None, ALU.mult))
        for t in range(TT):
            in_turn(nc.vector.tensor_scalar(ang[:, 24 + t // 2, 16 * (t % 2):16 * (t % 2) + 16], freq[:, FREQS:],
                                         posf[:, 0, t:t + 1], None, ALU.mult))
        for i, quarter in enumerate((0.0, 0.25)):
            in_turn(nc.vector.tensor_scalar(turn[:], ang[:], 1.0 / TWO_PI, quarter, ALU.mult, ALU.add))
            in_turn(nc.vector.tensor_scalar(turn[:], turn[:], ROUND, None, ALU.add))
            in_turn(nc.vector.tensor_scalar(turn[:], turn[:], ROUND, None, ALU.subtract))
            if i:
                dve.wait_ge(*after("tables", 2))
            src = ang
            for part in TWO_PI_PARTS:
                in_turn(nc.vector.scalar_tensor_tensor(red[:], turn[:], -part, src[:], ALU.mult, ALU.add))
                src = red
            if i:
                in_turn(nc.vector.tensor_scalar(red[:], red[:], TWO_PI / 4, None, ALU.add))
            nc.vector.tensor_scalar(red[:], red[:], PI_IN, -PI_IN, ALU.min, ALU.max).then_inc(sem("angles"), 1)
        dve.wait_ge(*after("tables", 4))
        dve.wait_ge(*after("c_evac", TT))
        r0, hw = C_Q + C_KV, MLA_R // 2
        lo_, hi_ = c_sb[:, :, r0:r0 + hw], c_sb[:, :, r0 + hw:r0 + 2 * hw]
        for i, (a, b) in enumerate(((lo_, cos_m), (hi_, sin_m), (hi_, cos_m), (lo_, sin_m))):
            in_turn(nc.vector.tensor_tensor(c_t[:, i], a, b[:], ALU.mult))
        in_turn(nc.vector.tensor_tensor(lo_, c_t[:, 0], c_t[:, 1], ALU.subtract))
        nc.vector.tensor_tensor(hi_, c_t[:, 2], c_t[:, 3], ALU.add).then_inc(sem("c_roped"), 1)
        dve.wait_ge(*after("c_root", 2))
        in_turn(nc.vector.reciprocal(c_ss[:], c_ss[:]))
        for t in range(TT):
            for i, (c0, w) in enumerate(((0, C_Q), (C_Q, C_KV))):
                nc.vector.tensor_scalar(c_sb[:, t, c0:c0 + w], c_sb[:, t, c0:c0 + w], c_ss[:, i, t:t + 1], None,
                                        ALU.mult).then_inc(sem("c_scaled"), 1)
        phase_end(dve, "dve")

        phase_start(dve, "dve")
        dve.wait_ge(*after("masks_in", 16))

        def rotate(u, r, g, t):
            dve.wait_ge(*after("d_done", u + 1))
            src = ps[:, u % 2, :].rearrange("p (h f) -> p h f", f=FREQS)
            cos, sin = (x_[:, g, t:t + 1, :].to_broadcast([P, 2 * H1, FREQS]) for x_ in (cos_d, sin_d))
            nc.vector.tensor_tensor(rc[:].rearrange("p (h f) -> p h f", f=FREQS), src, cos, ALU.mult).then_inc(sem("rope_cos"), 1)
            nc.vector.tensor_tensor(rs[:].rearrange("p (h f) -> p h f", f=FREQS), src, sin, ALU.mult).then_inc(sem("d_read"), 1)
            dve.wait_ge(*after("rope_cos", r + 1))
            dve.wait_ge(*after("d_read", u + 1))
            if r >= 1:
                dve.wait_ge(*after("rotT", r))
            c4, s4_, o4 = (x_[:].rearrange("p (h a f) -> p h a f", a=2, f=FREQS) for x_ in (rc, rs, rr))
            nc.vector.tensor_tensor(o4[:, :, 0, :], c4[:, :, 0, :], s4_[:, :, 1, :], ALU.subtract).then_inc(sem("rope_half"), 1)
            nc.vector.tensor_tensor(o4[:, :, 1, :], c4[:, :, 1, :], s4_[:, :, 0, :], ALU.add).then_inc(sem("rotated"), 1)
            dve.wait_ge(*after("rotated", r + 1))

        def d_soft(g, i):
            n = d_step(g, i)
            t, hh = divmod(i, HH)
            _, nk, mc, _ = window(g, t)
            dve.wait_ge(*after("d_scored", n + 1))
            if n >= 2:
                dve.wait_ge(*after("d_T", n - 1))
            dst = prd[:, i % 2, :, 0:nk]
            for b in range(2):
                sc = ps[:, 3 + b, :].rearrange("p (j k) -> p j k", j=2)[:, :, 0:nk]
                mask = masks[:, mc:mc + nk].unsqueeze(1).to_broadcast([P, 2, nk])
                last = nc.vector.tensor_tensor(dst[:, b::2, :], sc, mask, ALU.add)
            last.then_inc(sem("d_masked"), 1)
            dve.wait_ge(*after("d_masked", n + 1))
            if i % HH == 0 and (g or t >= 2):
                dve.wait_ge(*after(f"d_store{t % 2}", 16 * ((TT * g + t) // 2)))
            c0 = COLS + G * hh
            nc.vector.tensor_reduce(osb[:, t % 2, c0:c0 + G], dst, AX_X, ALU.max, negate=True).then_inc(sem("d_max"), 1)

        def d_out(g, i):
            n = d_step(g, i)
            t, hh = divmod(i, HH)
            dve.wait_ge(*after("d_valued", n + 1))
            nc.vector.tensor_copy(osb[:, t % 2, 256 * hh:256 * hh + 256], ps[:, 7, 0:256]).then_inc(sem("d_out"), 1)

        for slot in range(D_SLOTS):
            done = unit_before(slot)
            if done and done[3] != "v":
                u, r, g, kind, t = done
                if kind == "q" and t == 0:
                    dve.wait_ge(*after("d_read", u))
                rotate(u, r, g, t)
            if slot in step_at:
                d_soft(*step_at[slot])
            if slot - 2 in step_at:
                d_out(*step_at[slot - 2])
        phase_end(dve, "dve")

        phase_start(dve, "dve")
        dve.wait_ge(*after("stats_in", 48))
        nm = [stats[:, g, :, 0:H1] for g in range(3)]
        den = [stats[:, g, :, H1:] for g in range(3)]
        in_turn(nc.vector.tensor_tensor(joint[:], nm[0], nm[1], ALU.min))
        in_turn(nc.vector.tensor_tensor(joint[:], joint[:], nm[2], ALU.min))
        for g in range(3):
            nc.vector.tensor_tensor(coef[:, g], joint[:], nm[g], ALU.subtract).then_inc(sem("coef_arg"), 1)
        dve.wait_ge(*after("coef_exp", 3))
        for g in range(3):
            in_turn(nc.vector.tensor_tensor(den[g], den[g], coef[:, g], ALU.mult))
        in_turn(nc.vector.tensor_tensor(dsum[:], den[0], den[1], ALU.add))
        in_turn(nc.vector.tensor_tensor(dsum[:], dsum[:], den[2], ALU.add))
        in_turn(nc.vector.reciprocal(dsum[:], dsum[:]))
        for g in range(3):
            in_turn(nc.vector.tensor_tensor(coef[:, g], coef[:, g], dsum[:], ALU.mult))
        dve.wait_ge(*after("zd_in", 64))

        def gate(t):
            dve.wait_ge(*after("jointT", t + 1))
            nc.vector.tensor_tensor(dgT[:, :, P * t:P * t + P], ps[:, 4 + t % 2, :].rearrange("p (j c) -> p j c", c=P),
                                    zdT[:, :, P * t:P * t + P], ALU.mult).then_inc(sem("dg_done"), 1)

        for t in range(TT):
            dve.wait_ge(*after(f"nums_in{t % 2}", 48 * (t // 2 + 1)))
            if t >= 1:
                dve.wait_ge(*after("jointT", t))
            for g in range(3):
                nc.vector.tensor_tensor(wsum[:, g, :].rearrange("p (h d) -> p h d", d=HD),
                                        nums[:, t % 2, g, :].rearrange("p (h d) -> p h d", d=HD),
                                        coef[:, g, t, :].unsqueeze(2).to_broadcast([P, H1, HD]), ALU.mult).then_inc(sem("weighted"), 1)
            dve.wait_ge(*after("weighted", 3 * t + 3))
            in_turn(nc.vector.tensor_tensor(wsum[:, 0, :], wsum[:, 0, :], wsum[:, 1, :], ALU.add))
            nc.vector.tensor_tensor(wsum[:, 0, :], wsum[:, 0, :], wsum[:, 2, :], ALU.add).then_inc(sem("joint"), 1)
            dve.wait_ge(*after("joint", t + 1))
            gate(t)
        phase_end(dve, "dve")

        phase_start(dve, "dve")
        for u, (n, kind) in enumerate(C_UNITS):
            sl = slice(COLS * n, COLS * n + COLS)
            dve.wait_ge(*after("cT_hi", u + 1))
            if kind < 2:
                last = nc.vector.scalar_tensor_tensor(cql[:, kind, sl], ps[:, u % 4, :], gain_q[:, kind:kind + 1],
                                                      cqh[:, kind, sl].bitcast(F32), ALU.mult, ALU.subtract)
            elif kind == 2:
                last = nc.vector.scalar_tensor_tensor(ckl[:, sl], ps[:, u % 4, :], gain_kv, ckh[:, sl].bitcast(F32),
                                                      ALU.mult, ALU.subtract)
            else:
                for b in range(2):
                    last = nc.vector.tensor_tensor(Kl[HD:MLA_QK, b, sl], ps[HD:MLA_QK, u % 4, :],
                                                   Kh[HD:MLA_QK, b, sl].bitcast(F32), ALU.subtract)
            last.then_inc(sem("cT_lo"), 1)
        dve.wait_ge(*after("rope_back", 32))
        for t in range(TT):
            dve.wait_ge(*after("qm_read", 2 * t + 2))
            q_lo, q_hi = q_sb[:, t % 2, :, HD:HD + hw], q_sb[:, t % 2, :, HD + hw:]
            cos, sin = (x_[:, t:t + 1, :].to_broadcast([P, H1, hw]) for x_ in (cos_q, sin_q))
            for i, (a, b) in enumerate(((q_lo, cos), (q_hi, sin), (q_hi, cos), (q_lo, sin))):
                in_turn(nc.vector.tensor_tensor(q_t[:, i], a, b, ALU.mult))
            in_turn(nc.vector.tensor_tensor(q_lo, q_t[:, 0], q_t[:, 1], ALU.subtract))
            nc.vector.tensor_tensor(q_hi, q_t[:, 2], q_t[:, 3], ALU.add).then_inc(sem("qm_roped"), 1)
            dve.wait_ge(*after("vm_hi", t + 1))
            nc.vector.tensor_tensor(V2[:, t, :, 1, :], ps[:, 4 + t % 2, :].rearrange("p (h c) -> p h c", c=HD),
                                    V2[:, t, :, 0, :].bitcast(F32), ALU.subtract).then_inc(sem("vm_lo"), 1)

        def head_lo(x_):
            h, part = divmod(x_, 4)
            sl = slice(COLS * (part % 2), COLS * (part % 2) + COLS)
            dve.wait_ge(*after("qk_hi", x_ + 1))
            dst, hi, n = (Ql, Qh, MLA_QK) if part >= 2 else (Kl, Kh, HD)
            nc.vector.tensor_tensor(dst[0:n, h % 2, sl], ps[0:n, 7, :], hi[0:n, h % 2, sl].bitcast(F32),
                                    ALU.subtract).then_inc(sem("qk_lo"), 1)

        def m_out(b):
            h, qb = divmod(b, 4)
            dve.wait_ge(*after("m_valued", b + 1))
            dve.wait_ge(*after(f"zm_in{b % 2}", 16 * (b // 2 + 1)))
            if b >= 2:
                dve.wait_ge(*after(f"am_out{b % 2}", 16 * (b // 2)))
            dst = am[0:HD, b % 2, :]
            in_turn(nc.vector.tensor_copy(dst, ps[HD:P, 6, 0:256]))
            in_turn(nc.vector.tensor_tensor(dst, ps[0:HD, 6, 0:256], dst, ALU.add))
            nc.vector.tensor_tensor(dst, dst, zm[0:HD, b % 2, :], ALU.mult).then_inc(sem("m_out"), 1)

        head_lo(0)
        head_lo(1)
        phase_end(dve, "dve")

        phase_start(dve, "dve")
        head_lo(2)
        head_lo(3)
        for j in range(n_t + 5):
            if 3 <= j < n_t + 3:
                k = j - 3
                for half in range(2):
                    dve.wait_ge(*after("m_hi", 2 * k + half + 1))
                    dst = (slice(None), (k // 2) % 2, slice(4 * half, 4 * half + 4), slice(P * (k % 2), P * (k % 2) + P))
                    nc.vector.tensor_tensor(PTl[dst], ps[:, 4 + half, :].rearrange("p (j c) -> p j c", c=P),
                                            PTh[dst].bitcast(F32), ALU.subtract).then_inc(sem("m_lo"), 1)
            if 1 <= j <= n_t:
                k = j - 1
                dve.wait_ge(*after("m_exp", k + 1))
                total = m_sum[:, k % 8:k % 8 + 1]
                nc.vector.reciprocal(total, total).then_inc(sem("m_recip"), 1)
            if j >= 6 and j % 2 == 0:
                m_out((j - 6) // 2)
            if j < n_t:
                dve.wait_ge(*after("m_scored", j + 1))
                if j >= 8:
                    dve.wait_ge(*after("m_exp", j - 7))
                nc.vector.tensor_reduce(rstd[:, j % 8:j % 8 + 1], ps[:, 2 * (j % 2):2 * (j % 2) + 2, :].rearrange("p b c -> p (b c)"),
                                        AX_X, ALU.max, negate=True).then_inc(sem("m_max"), 1)
            if j < n_t:
                h, qt = divmod(j, TT)
                if h + 1 < H1 and qt in (2, 3, 4, 5):
                    head_lo(4 * (h + 1) + qt - 2)
        phase_end(dve, "dve")

        phase_start(dve, "dve")
        for x_ in range(8):
            dve.wait_ge(*after("mixers_hi", x_ + 1))
            hi, lo = ((dh, dl), (ah, al))[x_ // 4]
            nc.vector.tensor_tensor(lo[:, x_ % 4, :], raw[:, x_ % 2, :], hi[:, x_ % 4, :].bitcast(F32), ALU.subtract).then_inc(sem("mixers_lo"), 1)
        for u in range(4 * KT):
            o, r = divmod(u, 2 * KT)
            n, m_ = divmod(r, KT)
            sl = slice(COLS * n, COLS * n + COLS)
            dve.wait_ge(*after("y2_done", u + 1))
            dve.wait_ge(*after(f"gates_in{u % 4}", 16 * (u // 4 + 1)))
            if o == 0:
                nc.vector.tensor_tensor(yd[:, m_, sl], ps[:, u % 8, :], gg[:, u % 4, :], ALU.mult).then_inc(sem("y2_read"), 1)
                continue
            if r == 0:
                dve.wait_ge(*after("y2_read", 2 * KT))
            if r >= 1:
                dve.wait_ge(*after("merged_lo", r))
            nc.vector.tensor_tensor(yg[:], ps[:, u % 8, :], gg[:, u % 4, :], ALU.mult).then_inc(sem("y2_read"), 1)
            dve.wait_ge(*after("y2_read", u + 1))
            nc.vector.tensor_tensor(yg[:], yg[:], yd[:, m_, sl], ALU.add).then_inc(sem("merged"), 1)
            dve.wait_ge(*after("merged_hi", r + 1))
            nc.vector.tensor_tensor(Ml[:, m_, sl], yg[:], Mh[:, m_, sl].bitcast(F32), ALU.subtract).then_inc(sem("merged_lo"), 1)

        for u in range(2 * TT):
            half, t = divmod(u, TT)
            sl = slice(COLS * half, COLS * half + COLS)
            dve.wait_ge(*after("o_done", u + 1))
            dve.wait_ge(*after(f"x1_back{t}", 16))
            nc.vector.tensor_tensor(xo[:, t, sl], ps[:, u % 8, :], xo[:, t, sl], ALU.add).then_inc(sem("o_read"), 1)
            if half:
                dve.wait_ge(*after("o_sq", u + 1))
                nc.vector.tensor_tensor(rstd[:, t:t + 1], ssq[:, t:t + 1], ssq2[:, t:t + 1], ALU.add).then_inc(sem("o_total"), 1)
                dve.wait_ge(*after("o_root", t + 1))
                nc.vector.reciprocal(rstd[:, t:t + 1], rstd[:, t:t + 1]).then_inc(sem("o_rstd"), 1)
                dve.wait_ge(*after("o_rstd", t + 1))
                if t == 0:
                    dve.wait_ge(*after("gfin", 16))
                if t >= 2:
                    dve.wait_ge(*after(f"out_stored{t % 2}", 16 * (t // 2)))
                nc.vector.scalar_tensor_tensor(fin[:, t % 2, :], xo[:, t, :], rstd[:, t:t + 1], gfin[:], ALU.mult, ALU.mult).then_inc(sem("final"), 1)

    ctx.close()


_INS = ["x", "w_in", "pool_w", "pool_scale", "attn_sinks", "w_out", "norm_pre", "norm_post", "positions_2",
        "attn_norm_g_2", "w_in_2", "b_gate_2", "mla_q_norm_g_2", "mla_kv_norm_g_2", "w_uq_2", "w_ukv_2",
        "w_o_mla_2", "w_o_dil_2", "w_out_2", "final_norm_g_2"]


def kernel(**inputs):
    import concourse.bacc as bacc
    from concourse.bass_utils import run_bass_kernel_spmd

    nc = bacc.Bacc("TRN2", target_bir_lowering=False, num_devices=1)
    arrays, args = {}, []
    for name in _INS:
        arrays[f"in_{name}"] = np.ascontiguousarray(inputs[name])
    arrays.update(constants())
    for name, a in arrays.items():
        args.append(nc.dram_tensor(name, a.shape, mybir.dt.from_np(a.dtype), kind="ExternalInput").ap())
    out = nc.dram_tensor("out_0", (1, S, D), F32, kind="ExternalOutput").ap()
    hybrid_blocks_kernel(nc, *args, out)
    r = run_bass_kernel_spmd(nc, [arrays], core_ids=[0])
    return r.results[0]["out_0"]
```
